# Optimizing a Trainium2 kernel written in Bass

```python
import math
import jax
import jax.numpy as jnp
from jax import lax
import numpy as np

D_MODEL = 1024
BATCH = 1
SEQ = 128
DEPTH = 2
DEC_BATCH = 1
DEC_SEQ = 512
PAST_LEN = 256

GRID_W = 64
HEAD_DIM = 64
MIX_W = D_MODEL
H_A = 6
A_W = H_A * HEAD_DIM
H_B = 6
KV_B = 2
B_W = H_B * HEAD_DIM
H_C = 4
DIFF_HD = 32
C_W = H_C * 2 * DIFF_HD
CONV_W = 3
CHUNK = 64
Q_BLOCK = 128
ROPE_THETA = 10000.0
D_FF = 2816
N_EXP = 8
TOP_K = 2
D_FF_E = 1408
N_DENSE = (DEPTH + 1) // 2
N_MOE = DEPTH // 2
EPS = 1e-6
SPLIT_SIZES = (3 * A_W, A_W, 2 * H_A, 2 * H_A, B_W, KV_B * HEAD_DIM, KV_B * HEAD_DIM, C_W, C_W, C_W)
IN_COLS = 3 * A_W + A_W + 4 * H_A + B_W + 2 * KV_B * HEAD_DIM + 3 * C_W

kernel_name = 'hymba_deltanet_gqa_diff_dit_step'

def rmsnorm(x, g):
    xf = x.astype(jnp.float32)
    y = xf * lax.rsqrt(jnp.mean(xf * xf, axis=-1, keepdims=True) + EPS)
    return (y * g.astype(jnp.float32)).astype(x.dtype)

def l2norm(x):
    xf = x.astype(jnp.float32)
    return xf * lax.rsqrt(jnp.sum(xf * xf, axis=-1, keepdims=True) + EPS)

def modulate(x, g, shift, scale):
    return rmsnorm(x, g) * (1 + scale) + shift

def axial_rope_tables(rows, rot_dim):
    n_freq = rot_dim // 4
    inv = ROPE_THETA ** (-jnp.arange(n_freq, dtype=jnp.float32) / n_freq)
    row = jnp.repeat(jnp.arange(rows, dtype=jnp.float32), GRID_W)
    col = jnp.tile(jnp.arange(GRID_W, dtype=jnp.float32), rows)
    ang = jnp.stack([row[:, None] * inv, col[:, None] * inv], axis=1)
    return jnp.cos(ang), jnp.sin(ang)

def apply_axial_rope(x, cos, sin):
    shp = x.shape
    nf = shp[-1] // 4
    xr = x.astype(jnp.float32).reshape(*shp[:-1], 2, 2, nf)
    bshape = (shp[1],) + (1,) * (x.ndim - 3) + (2, nf)
    c, s = cos.reshape(bshape), sin.reshape(bshape)
    x1, x2 = xr[..., 0, :], xr[..., 1, :]
    out = jnp.stack([x1 * c - x2 * s, x2 * c + x1 * s], axis=-2)
    return out.reshape(shp).astype(x.dtype)

def short_conv(x, w):
    return lax.conv_general_dilated(
        x, w[:, None, :].astype(x.dtype), window_strides=(1,),
        padding=[(CONV_W // 2, CONV_W // 2)], dimension_numbers=('NWC', 'WIO', 'NWC'),
        feature_group_count=x.shape[-1])

def chunk_gated_delta(q, k, v, g, beta, s0):
    B, T, H, DK = q.shape
    DV = v.shape[-1]
    n_chunk = T // CHUNK

    def chunks(a):
        a = a.astype(jnp.float32).reshape(B, n_chunk, CHUNK, H, *a.shape[3:])
        return jnp.moveaxis(jnp.swapaxes(a, 2, 3), 1, 0)

    qc = chunks(q) * (DK ** -0.5)
    kc, vc, gc, bc = chunks(k), chunks(v), chunks(g), chunks(beta)
    gcum = jnp.cumsum(gc, axis=-1)
    incl = jnp.tril(jnp.ones((CHUNK, CHUNK), dtype=bool))
    strict = jnp.tril(jnp.ones((CHUNK, CHUNK), dtype=bool), -1)
    diff = gcum[..., :, None] - gcum[..., None, :]
    decay = jnp.where(incl, jnp.exp(jnp.where(incl, diff, 0.0)), 0.0)
    kb = kc * bc[..., None]
    lmat = jnp.where(strict, jnp.einsum('nbhcd,nbhed->nbhce', kb, kc) * decay, 0.0)
    eye = jnp.eye(CHUNK, dtype=jnp.float32)
    rhs = jnp.concatenate([vc * bc[..., None], kb * jnp.exp(gcum)[..., None]], axis=-1)
    sol = lax.linalg.triangular_solve(eye + lmat, rhs, left_side=True, lower=True, unit_diagonal=True)
    u, w = sol[..., :DV], sol[..., DV:]
    a_intra = jnp.where(incl, jnp.einsum('nbhcd,nbhed->nbhce', qc, kc) * decay, 0.0)
    q_dec = qc * jnp.exp(gcum)[..., None]
    k_dec = kc * jnp.exp(gcum[..., -1:] - gcum)[..., None]
    g_last = jnp.exp(gcum[..., -1])

    def step(S, xs):
        q_i, k_i, u_i, w_i, a_i, gl = xs
        v_new = u_i - jnp.einsum('bhcd,bhde->bhce', w_i, S)
        o = jnp.einsum('bhcd,bhde->bhce', q_i, S) + jnp.einsum('bhce,bhef->bhcf', a_i, v_new)
        S = S * gl[..., None, None] + jnp.einsum('bhcd,bhce->bhde', k_i, v_new)
        return S, o

    S, out = lax.scan(step, s0.astype(jnp.float32), (q_dec, k_dec, u, w, a_intra, g_last))
    out = jnp.swapaxes(jnp.moveaxis(out, 0, 1), 2, 3).reshape(B, T, H, DV)
    return out, S

def deltanet_mixer(qkv, z, beta_raw, a_raw, a_log, dt_bias, norm_g, s0):
    B, T, _ = qkv.shape
    qkv = qkv.reshape(B, T, 3, H_A, HEAD_DIM)
    q, k, v = l2norm(qkv[:, :, 0]), l2norm(qkv[:, :, 1]), qkv[:, :, 2]
    beta = jax.nn.sigmoid(beta_raw.astype(jnp.float32)).reshape(B, T, 2, H_A)
    g = -jnp.exp(a_log.astype(jnp.float32)) * jax.nn.softplus(
        a_raw.astype(jnp.float32).reshape(B, T, 2, H_A) + dt_bias.astype(jnp.float32))
    o_f, s_f = chunk_gated_delta(q, k, v, g[:, :, 0], beta[:, :, 0], s0[:, 0])
    o_b, s_b = chunk_gated_delta(q[:, ::-1], k[:, ::-1], v[:, ::-1], g[:, ::-1, 1], beta[:, ::-1, 1], s0[:, 1])
    o = o_f + o_b[:, ::-1]
    o = rmsnorm(o, norm_g) * jax.nn.silu(z.astype(jnp.float32).reshape(B, T, H_A, HEAD_DIM))
    return o.reshape(B, T, A_W).astype(z.dtype), jnp.stack([s_f, s_b], axis=1)

def sweep_query_blocks(fn, q):
    B, T = q.shape[:2]
    nb = T // Q_BLOCK
    qb = jnp.moveaxis(q.reshape(B, nb, Q_BLOCK, *q.shape[2:]), 1, 0)
    out = lax.map(fn, qb)
    return jnp.moveaxis(out, 0, 1).reshape(B, T, *out.shape[3:])

def gqa_attend(q, k, v):
    B, T = q.shape[:2]
    qg = q.reshape(B, T, KV_B, H_B // KV_B, HEAD_DIM)

    def blk(qi):
        s = jnp.einsum('bqkgd,bskd->bkgqs', qi, k).astype(jnp.float32) * (HEAD_DIM ** -0.5)
        p = jax.nn.softmax(s, axis=-1).astype(v.dtype)
        return jnp.einsum('bkgqs,bskd->bqkgd', p, v)

    return sweep_query_blocks(blk, qg).reshape(B, T, B_W)

def diff_attend(q, k, v, lam):
    def blk(qi):
        s = jnp.einsum('bqhmd,bshmd->bhmqs', qi, k).astype(jnp.float32) * (DIFF_HD ** -0.5)
        p = jax.nn.softmax(s, axis=-1)
        a = (p[:, :, 0] - lam * p[:, :, 1]).astype(v.dtype)
        return jnp.einsum('bhqs,bshe->bqhe', a, v)

    return sweep_query_blocks(blk, q)

def token_mixer(h, p, l, ctx, rope):
    B, T, _ = h.shape
    idx = np.cumsum(SPLIT_SIZES)[:-1].tolist()
    qkv_a, z_a, beta_raw, a_raw, q_b, k_b, v_b, q_c, k_c, v_c = jnp.split(h @ p['w_in'][l], idx, axis=-1)
    qkv_a = jax.nn.silu(short_conv(qkv_a, p['conv_w'][l]))
    s0 = jnp.zeros((B, 2, H_A, HEAD_DIM, HEAD_DIM), jnp.float32) if ctx is None else ctx[0]
    o_a, s_fin = deltanet_mixer(qkv_a, z_a, beta_raw, a_raw, p['dn_a_log'][l], p['dn_dt_bias'][l],
                                p['dn_norm'][l], s0)
    q_b = rmsnorm(q_b.reshape(B, T, H_B, HEAD_DIM), p['gqa_q_norm'][l])
    k_b = rmsnorm(k_b.reshape(B, T, KV_B, HEAD_DIM), p['gqa_k_norm'][l])
    v_b = v_b.reshape(B, T, KV_B, HEAD_DIM)
    q_c = q_c.reshape(B, T, H_C, 2, DIFF_HD)
    k_c = k_c.reshape(B, T, H_C, 2, DIFF_HD)
    v_c = v_c.reshape(B, T, H_C, 2 * DIFF_HD)
    if ctx is None:
        new_ctx = (s_fin, k_b, v_b, k_c, v_c)
        kb_all, vb_all, kc_all, vc_all = k_b, v_b, k_c, v_c
    else:
        cos_b, sin_b, cos_c, sin_c = rope
        q_b, k_b = apply_axial_rope(q_b, cos_b, sin_b), apply_axial_rope(k_b, cos_b, sin_b)
        q_c, k_c = apply_axial_rope(q_c, cos_c, sin_c), apply_axial_rope(k_c, cos_c, sin_c)
        kb_all = jnp.concatenate([ctx[1].astype(k_b.dtype), k_b], axis=1)
        vb_all = jnp.concatenate([ctx[2].astype(v_b.dtype), v_b], axis=1)
        kc_all = jnp.concatenate([ctx[3].astype(k_c.dtype), k_c], axis=1)
        vc_all = jnp.concatenate([ctx[4].astype(v_c.dtype), v_c], axis=1)
        new_ctx = None
    o_b = gqa_attend(q_b, kb_all, vb_all)
    lam_init = 0.8 - 0.6 * math.exp(-0.3 * l)
    lv = p['diff_lambda'][l].astype(jnp.float32)
    lam = jnp.exp(jnp.sum(lv[0] * lv[1])) - jnp.exp(jnp.sum(lv[2] * lv[3])) + lam_init
    o_c = rmsnorm(diff_attend(q_c, kc_all, vc_all, lam), p['diff_norm'][l]) * (1.0 - lam_init)
    mixed = jnp.concatenate([o_a, o_b, o_c.reshape(B, T, C_W)], axis=-1)
    return mixed @ p['w_out'][l], new_ctx

def swiglu(h, w_gu, w_down):
    g, u = jnp.split(h @ w_gu, 2, axis=-1)
    return (jax.nn.silu(g) * u) @ w_down

def moe_swiglu(h, router, w_gu, w_down):
    B, T, D = h.shape
    hf = h.reshape(B * T, D)
    logits = (hf @ router).astype(jnp.float32)
    top_v, top_i = lax.top_k(logits, TOP_K)
    wts = jax.nn.softmax(top_v, axis=-1)
    gate = jnp.sum(jax.nn.one_hot(top_i, N_EXP, dtype=jnp.float32) * wts[..., None], axis=-2)
    g, u = jnp.split(jnp.einsum('nd,edf->nef', hf, w_gu), 2, axis=-1)
    act = jax.nn.silu(g) * u * gate[..., None].astype(h.dtype)
    return jnp.einsum('nef,efd->nd', act, w_down).reshape(B, T, D)

def trunk_layer(x, cond, l, p, ctx, rope):
    mod = jax.nn.silu(cond) @ p['ada_w'][l] + p['ada_b'][l]
    sh_m, sc_m, g_m, sh_f, sc_f, g_f = jnp.split(mod[:, None, :], 6, axis=-1)
    mix, new_ctx = token_mixer(modulate(x, p['norm_mix'][l], sh_m, sc_m), p, l, ctx, rope)
    x = x + g_m * mix
    h = modulate(x, p['norm_ffn'][l], sh_f, sc_f)
    if l % 2 == 0:
        f = swiglu(h, p['ffn_w_gu'][l // 2], p['ffn_w_down'][l // 2])
    else:
        f = moe_swiglu(h, p['moe_router'][l // 2], p['moe_w_gu'][l // 2], p['moe_w_down'][l // 2])
    return x + g_f * f, new_ctx

def setup_inputs(seed: int = 0) -> dict:
    key = jax.random.key(seed)
    ks = jax.random.split(key, 32)
    f32 = jnp.float32

    def nrm(k, shape, s=1.0):
        return jax.random.normal(k, shape, f32) * s

    def gain(k, shape):
        return 1.0 + 0.05 * jax.random.normal(k, shape, f32)

    dt = jnp.exp(jax.random.uniform(ks[14], (DEPTH, 2, H_A), f32, minval=math.log(1e-3), maxval=math.log(1e-1)))
    return {
        'x_prompt': nrm(ks[0], (BATCH, SEQ, D_MODEL)),
        'x_sample': nrm(ks[1], (DEC_BATCH, DEC_SEQ, D_MODEL)),
        'state_delta': nrm(ks[2], (DEC_BATCH, DEPTH, 2, H_A, HEAD_DIM, HEAD_DIM), HEAD_DIM ** -0.5),
        'cache_gqa_k': nrm(ks[3], (DEC_BATCH, DEPTH, PAST_LEN, KV_B, HEAD_DIM)),
        'cache_gqa_v': nrm(ks[4], (DEC_BATCH, DEPTH, PAST_LEN, KV_B, HEAD_DIM)),
        'cache_diff_k': nrm(ks[5], (DEC_BATCH, DEPTH, PAST_LEN, H_C, 2, DIFF_HD)),
        'cache_diff_v': nrm(ks[6], (DEC_BATCH, DEPTH, PAST_LEN, H_C, 2 * DIFF_HD)),
        'c': nrm(ks[7], (DEC_BATCH, D_MODEL)),
        'c_ctx': nrm(ks[8], (D_MODEL,)),
        'ada_w': nrm(ks[9], (DEPTH, D_MODEL, 6 * D_MODEL), 0.5 * D_MODEL ** -0.5),
        'ada_b': nrm(ks[10], (DEPTH, 6 * D_MODEL), 0.02),
        'norm_mix': gain(ks[11], (DEPTH, D_MODEL)),
        'norm_ffn': gain(ks[12], (DEPTH, D_MODEL)),
        'w_in': nrm(ks[13], (DEPTH, D_MODEL, IN_COLS), D_MODEL ** -0.5),
        'conv_w': nrm(ks[15], (DEPTH, CONV_W, 3 * A_W), CONV_W ** -0.5),
        'dn_a_log': jnp.log(jax.random.uniform(ks[16], (DEPTH, 2, H_A), f32, minval=1.0, maxval=16.0)),
        'dn_dt_bias': jnp.log(jnp.expm1(dt)),
        'dn_norm': gain(ks[17], (DEPTH, HEAD_DIM)),
        'gqa_q_norm': gain(ks[18], (DEPTH, HEAD_DIM)),
        'gqa_k_norm': gain(ks[19], (DEPTH, HEAD_DIM)),
        'diff_lambda': nrm(ks[20], (DEPTH, 4, DIFF_HD), 0.1),
        'diff_norm': gain(ks[21], (DEPTH, 2 * DIFF_HD)),
        'w_out': nrm(ks[22], (DEPTH, MIX_W, D_MODEL), MIX_W ** -0.5),
        'ffn_w_gu': nrm(ks[23], (N_DENSE, D_MODEL, 2 * D_FF), D_MODEL ** -0.5),
        'ffn_w_down': nrm(ks[24], (N_DENSE, D_FF, D_MODEL), D_FF ** -0.5),
        'moe_router': nrm(ks[25], (N_MOE, D_MODEL, N_EXP), D_MODEL ** -0.5),
        'moe_w_gu': nrm(ks[26], (N_MOE, N_EXP, D_MODEL, 2 * D_FF_E), D_MODEL ** -0.5),
        'moe_w_down': nrm(ks[27], (N_MOE, N_EXP, D_FF_E, D_MODEL), D_FF_E ** -0.5),
        'final_norm': gain(ks[28], (D_MODEL,)),
    }

def reference(x_prompt, x_sample, state_delta, cache_gqa_k, cache_gqa_v, cache_diff_k, cache_diff_v, c, c_ctx,
              ada_w, ada_b, norm_mix, norm_ffn, w_in, conv_w, dn_a_log, dn_dt_bias, dn_norm, gqa_q_norm,
              gqa_k_norm, diff_lambda, diff_norm, w_out, ffn_w_gu, ffn_w_down, moe_router, moe_w_gu, moe_w_down,
              final_norm):
    p = {
        'ada_w': ada_w, 'ada_b': ada_b, 'norm_mix': norm_mix, 'norm_ffn': norm_ffn, 'w_in': w_in,
        'conv_w': conv_w, 'dn_a_log': dn_a_log, 'dn_dt_bias': dn_dt_bias, 'dn_norm': dn_norm,
        'gqa_q_norm': gqa_q_norm, 'gqa_k_norm': gqa_k_norm, 'diff_lambda': diff_lambda, 'diff_norm': diff_norm,
        'w_out': w_out, 'ffn_w_gu': ffn_w_gu, 'ffn_w_down': ffn_w_down, 'moe_router': moe_router,
        'moe_w_gu': moe_w_gu, 'moe_w_down': moe_w_down,
    }
    x = x_prompt
    cond_ctx = c_ctx[None, :]
    ctx_out = []
    for l in range(DEPTH):
        x, ctx_l = trunk_layer(x, cond_ctx, l, p, None, None)
        ctx_out.append(ctx_l)
    y_prompt = rmsnorm(x, final_norm)
    new_state_delta = jnp.stack([t[0] for t in ctx_out], axis=1).astype(x_prompt.dtype)
    new_gqa_k = jnp.stack([t[1] for t in ctx_out], axis=1)
    new_gqa_v = jnp.stack([t[2] for t in ctx_out], axis=1)
    new_diff_k = jnp.stack([t[3] for t in ctx_out], axis=1)
    new_diff_v = jnp.stack([t[4] for t in ctx_out], axis=1)
    rows = x_sample.shape[1] // GRID_W
    cos_b, sin_b = axial_rope_tables(rows, HEAD_DIM)
    cos_c, sin_c = axial_rope_tables(rows, DIFF_HD)
    rope = (cos_b, sin_b, cos_c, sin_c)
    xs = x_sample
    for l in range(DEPTH):
        cache_l = (state_delta[:, l], cache_gqa_k[:, l], cache_gqa_v[:, l], cache_diff_k[:, l], cache_diff_v[:, l])
        xs, _ = trunk_layer(xs, c, l, p, cache_l, rope)
    y_sample = rmsnorm(xs, final_norm)
    return (y_prompt, y_sample, new_state_delta, new_gqa_k, new_gqa_v, new_diff_k, new_diff_v)


_drawn_inputs = setup_inputs


def setup_inputs(seed=0):
    import zlib

    import numpy as np

    out = dict(_drawn_inputs(seed))
    spreads = {}
    factors = {'state_delta': 2.881,
     'cache_gqa_k': 6.544,
     'cache_gqa_v': 6.093,
     'dn_norm': 5.395,
     'gqa_q_norm': 8.0,
     'diff_lambda': 4.626,
     'diff_norm': 5.752}
    for name, (base, spread) in spreads.items():
        noise = np.random.default_rng([zlib.crc32(name.encode()), seed]).standard_normal(out[name].shape)
        drawn = base * np.exp(spread * noise) if base else spread * noise
        out[name] = jnp.asarray(drawn.astype(out[name].dtype))
    for name, factor in factors.items():
        out[name] = (out[name] * factor).astype(out[name].dtype)
    return out
```

```python
import math
from contextlib import ExitStack, contextmanager

import numpy as np

import concourse.bass as bass
from concourse import mybir

F32 = mybir.dt.float32
I32 = mybir.dt.int32
U32 = mybir.dt.uint32
ACT = mybir.ActivationFunctionType
ALU = mybir.AluOpType
AX = mybir.AxisListType

P = 128
D = 1024
KC = D // P
T = 640
NT = T // P
DEPTH = 2
HD = 64
HA = 6
AW = HA * HD
FM = 3 * AW
IN_COLS = 2968
TM = IN_COLS - FM
Z0, BE0, AR0, QB0, KB0, VB0, QC0, KCC0, VC0 = 0, 384, 396, 408, 792, 920, 1048, 1304, 1560
TMT = TM // 4
PAST = 256
HB, KVB = 6, 2
HC, DHC = 4, 32
DFF = 1408
FC = DFF // P
NE = 8
EPS = 1e-6
STREAMS = ((0, P), (P, T))
NLEV = 7
C_ID, C_ONE, C_U, C_SL, C_LV = 0, 1, 2, 4, 6
NCONST = C_LV + 2 * NLEV
KEYS = P + PAST + 4 * P


class Chain:

    def __init__(self, eng, sem):
        self.eng, self.sem, self.n = eng, sem, 0

    def __call__(self, ins):
        self.n += 1
        ins.then_inc(self.sem, 1)
        self.eng.wait_ge(self.sem, self.n)


@contextmanager
def stage(nc, names):
    at = nc.next_id()
    sems = {n: nc.alloc_semaphore(f"{n}_{at}") for n in names.split()}
    with nc.Block() as block:
        yield block, sems
    nc.clear_and_free_semaphores(list(sems.values()))
    nc.all_engine_barrier()


def bcast_mid(ap, n):
    return ap.unsqueeze(1).to_broadcast([ap.shape[0], n, ap.shape[1]])


def bcast_last(ap, n):
    return ap.unsqueeze(2).to_broadcast([ap.shape[0], ap.shape[1], n])


class Kernel:
    def __init__(self, nc, i, o, ctx):
        self.nc, self.i, self.o = nc, i, o

        def sb(name, shape, dt=F32):
            return ctx.enter_context(nc.sbuf_tensor(name, shape, dt))

        self.ps = ctx.enter_context(nc.psum_tensor("ps", [P, 8, 512], F32))
        self.xT = sb("xT", [P, KC, T])
        self.hT = sb("hT", [P, KC, T])
        self.cst = sb("cst", [P, NCONST, P])
        self.cols = sb("cols", [P, 112 + 94])
        self.condT = sb("condT", [P, KC, 2])
        self.mod = sb("mod", [P, DEPTH, 6, KC, 2])
        self.amul = sb("amul", [P, DEPTH, 2, KC, 2])
        self.ident = self.cst[:, C_ID, :]
        self.ones = self.cst[:, C_ONE, :]

    def c(self, n):
        return self.cst[:, n, :]

    def prologue(self):
        nc, i, ps = self.nc, self.i, self.ps
        NW = 24
        SL = 4
        with ExitStack() as scope:
            def sb(name, shape, dt=F32):
                return scope.enter_context(nc.sbuf_tensor(name, shape, dt))
            xin = sb("xin", [P, NT, D])
            rows = sb("rows", [P, 2, P])
            wr = sb("ada_ring", [P, SL, KC, 512])
            names = "consts_in x_in rows_in row_turned cols_out cond x_turned x_out mod_mm mod_out chain " + \
                " ".join(f"w_in{s}" for s in range(SL))
            with stage(nc, names) as (block, s):
                @block.sync
                def _(sp):
                    sp.dma_start(self.cst[:], i["consts"]).then_inc(s["consts_in"], 16)
                    for r0, n, src, half in (
                            (0, 96, i["ada_b"].rearrange("l (c p) -> (l c) p", p=P), 0),
                            (96, 8, i["c_ctx"].rearrange("(c p) -> c p", p=P), 0),
                            (104, 8, i["c"].rearrange("b (c p) -> (b c) p", p=P), 0),
                            (0, 16, i["norm_mix"].rearrange("l (c p) -> (l c) p", p=P), 1),
                            (16, 16, i["norm_ffn"].rearrange("l (c p) -> (l c) p", p=P), 1),
                            (32, 8, i["final_norm"].rearrange("(c p) -> c p", p=P), 1),
                            (40, 54, i["conv_w"].rearrange("l w (c p) -> (l w c) p", p=P), 1)):
                        sp.dma_start(rows[r0:r0 + n, half, :], src).then_inc(s["rows_in"], 16)
                    sp.dma_start(xin[:, 0, :], i["x_prompt"][0]).then_inc(s["x_in"], 16)
                    sp.dma_start(xin[:, 1:NT, :], i["x_sample"][0].rearrange("(t p) d -> p t d", p=P)
                                 ).then_inc(s["x_in"], 16)
                    for n in range(NW):
                        if n >= SL:
                            sp.wait_ge(s["mod_mm"], n - SL + 1)
                        l, j = divmod(n, 12)
                        sp.dma_start(wr[:, n % SL], i["ada_w"][l].rearrange("(c p) n -> p c n", p=P)
                                     [:, :, j * 512:(j + 1) * 512]).then_inc(s[f"w_in{n % SL}"], 16)

                @block.tensor
                def _(pe):
                    pe.wait_ge(s["consts_in"], 16)
                    pe.wait_ge(s["rows_in"], 7 * 16)
                    for half, n in ((0, 112), (1, 94)):
                        pe.transpose(ps[:, half, 0:n], rows[0:n, half, :], self.ident[0:n, 0:n]
                                     ).then_inc(s["row_turned"], 1)
                    pe.wait_ge(s["x_in"], 32)
                    for t in range(NT):
                        for g in range(2):
                            n = 2 * t + g
                            if n >= 4:
                                pe.wait_ge(s["x_out"], n - 3)
                            for c in range(4):
                                mm = pe.transpose(ps[:, 2 + n % 4, c * P:(c + 1) * P],
                                                  xin[:, t, (4 * g + c) * P:(4 * g + c + 1) * P], self.ident)
                            mm.then_inc(s["x_turned"], 1)
                    pe.wait_ge(s["cond"], 1)
                    for n in range(NW):
                        pe.wait_ge(s[f"w_in{n % SL}"], 16 * (n // SL + 1))
                        for m in range(4):
                            o = (4 * n + m) * 2
                            for k in range(KC):
                                mm = pe.matmul(ps[:, 6, o:o + 2], wr[:, n % SL, k, m * P:(m + 1) * P],
                                               self.condT[:, k, :], start=(k == 0), stop=(k == KC - 1))
                        mm.then_inc(s["mod_mm"], 1)

                @block.scalar
                def _(act):
                    act.wait_ge(s["cols_out"], 2)
                    act.activation(self.condT[:].rearrange("p k s -> p s k"),
                                   self.cols[:, 96:112].rearrange("p (s k) -> p s k", s=2),
                                   ACT.Silu).then_inc(s["cond"], 1)

                @block.vector
                def _(dve):
                    chain = Chain(dve, s["chain"])
                    dve.wait_ge(s["row_turned"], 2)
                    dve.tensor_copy(self.cols[:, 0:112], ps[:, 0, 0:112]).then_inc(s["cols_out"], 1)
                    dve.tensor_copy(self.cols[:, 112:206], ps[:, 1, 0:94]).then_inc(s["cols_out"], 1)
                    for t in range(NT):
                        for g in range(2):
                            n = 2 * t + g
                            dve.wait_ge(s["x_turned"], n + 1)
                            dve.tensor_copy(self.xT[:, 4 * g:4 * g + 4, t * P:(t + 1) * P],
                                            ps[:, 2 + n % 4, :].rearrange("p (c t) -> p c t", c=4)
                                            ).then_inc(s["x_out"], 1)
                    dve.wait_ge(s["mod_mm"], NW)
                    dve.wait_ge(s["cols_out"], 2)
                    chain(dve.tensor_tensor(self.mod[:].rearrange("p l m k s -> p (l m k) s"),
                                            ps[:, 6, 0:192].rearrange("p (a s) -> p a s", s=2),
                                            bcast_last(self.cols[:, 0:96], 2), ALU.add))
                    for l in range(DEPTH):
                        for w in range(2):
                            g0 = 112 + 16 * w + 8 * l
                            dve.scalar_tensor_tensor(
                                out=self.amul[:, l, w], in0=self.mod[:, l, 3 * w + 1], scalar=1.0,
                                in1=bcast_last(self.cols[:, g0:g0 + 8], 2), op0=ALU.add, op1=ALU.mult
                            ).then_inc(s["mod_out"], 1)

    def norm(self, mul, add):
        nc, ps, xT, hT = self.nc, self.ps, self.xT, self.hT
        with ExitStack() as scope:
            sq = scope.enter_context(nc.sbuf_tensor(f"sq_{nc.next_id()}", [P, KC, T], F32))
            rstd = scope.enter_context(nc.sbuf_tensor(f"rstd_{nc.next_id()}", [P, T], F32))
            with stage(nc, "squared summed ms root rstd scaled moved") as (block, s):
                @block.scalar
                def _(act):
                    for k in range(0, KC, 2):
                        act.activation(sq[:, k], xT[:, k], ACT.Square).then_inc(s["squared"], 1)
                    act.wait_ge(s["ms"], 2)
                    act.activation(rstd[:], rstd[:], ACT.Sqrt).then_inc(s["root"], 1)
                    for k in range(KC):
                        act.wait_ge(s["scaled"], KC + k + 1)
                        for j, (a, b) in enumerate(STREAMS):
                            act.activation(hT[:, k, a:b], sq[:, k, a:b], ACT.Identity, scale=mul(k, j),
                                           bias=add(k, j) if add else 0.0).then_inc(s["moved"], 1)

                @block.vector
                def _(dve):
                    for k in range(1, KC, 2):
                        dve.tensor_tensor(sq[:, k], xT[:, k], xT[:, k], ALU.mult).then_inc(s["scaled"], 1)
                    dve.wait_ge(s["summed"], 1)
                    for j, (a, b) in enumerate(STREAMS):
                        dve.tensor_scalar(rstd[:, a:b], ps[:, j, 0:b - a], 1.0 / D, EPS, ALU.mult, ALU.add
                                          ).then_inc(s["ms"], 1)
                    dve.wait_ge(s["root"], 1)
                    dve.reciprocal(rstd[:], rstd[:]).then_inc(s["rstd"], 1)
                    dve.wait_ge(s["rstd"], 1)
                    for k in range(KC // 2, KC):
                        dve.nop().then_inc(s["scaled"], 1)
                    for k in range(KC):
                        dve.tensor_tensor(sq[:, k], xT[:, k], rstd[:], ALU.mult).then_inc(s["scaled"], 1)

                @block.tensor
                def _(pe):
                    for k in range(KC):
                        if k % 2:
                            pe.wait_ge(s["scaled"], k // 2 + 1)
                        else:
                            pe.wait_ge(s["squared"], k // 2 + 1)
                        for j, (a, b) in enumerate(STREAMS):
                            mm = pe.matmul(ps[:, j, 0:b - a], self.ones, sq[:, k, a:b],
                                           start=(k == 0), stop=(k == KC - 1))
                    mm.then_inc(s["summed"], 1)

    def mixer(self, l):
        nc, i, ps = self.nc, self.i, self.ps
        with ExitStack() as scope:
            def sb(name, shape, dt=F32):
                return scope.enter_context(nc.sbuf_tensor(f"{name}_{l}", shape, dt))
            self.tm = sb("tm", [P, NT, TM])
            self.oA = sb("oA", [P, NT, AW])
            self.bg = sb("bg", [P, 2, NT, 2, HA])
            with ExitStack() as s2:
                self.qkv = s2.enter_context(nc.sbuf_tensor(f"qkv_{l}", [P, NT, 18, HD], F32))
                spare = self.hT[:].rearrange("p c t -> p (c t)")
                self.kqT = spare[:, 0:NT * 6 * P].rearrange("p (t h j n) -> p t h j n", t=NT, h=3, j=2)
                self.mt1 = spare[:, NT * 6 * P:(NT + 1) * 6 * P].rearrange("p (h n) -> p h n", h=HA)
                self.eg = s2.enter_context(nc.sbuf_tensor(f"eg_{l}", [P, 3, 2, NT, HA], F32))
                self.glp = s2.enter_context(nc.sbuf_tensor(f"glp_{l}", [P, 2, NT, 3], F32))
                self.in_proj(l)
                self.delta_prep(l)
                self.delta_scan(l)
            self.mixed = sb("mixed", [P, NT, D])
            self.attn_prep_and_attend(l)
            self.out_proj(l)

    def in_proj(self, l):
        nc, i, ps, tm = self.nc, self.i, self.ps, self.tm
        w = i["w_in"][l].rearrange("(c p) n -> p c n", p=P)
        SL = 3
        tiles = [("fm", n * 384, 384) for n in range(3)] + [("tm", FM + n * TMT, TMT) for n in range(4)]
        PADW = T + 4
        at = (1, 131)
        with ExitStack() as scope:
            def sb(name, shape, dt=F32):
                return scope.enter_context(nc.sbuf_tensor(f"{name}_{l}", shape, dt))
            ring = sb("w_ring", [P, SL, KC * TMT])
            pad = sb("conv_in", [P, 9, PADW])
            conv = sb("conv_out", [P, 2, PADW - 2])
            names = "fm_mm tm_mm fm_act fm_dve tm_out padded chain conv conv_used silu turned qkv_out " + \
                " ".join(f"w_in{s}" for s in range(SL))
            with stage(nc, names) as (block, s):
                def view(n):
                    return ring[:, n % SL, 0:KC * tiles[n][2]].rearrange("p (c n) -> p c n", c=KC)

                @block.sync
                def _(sp):
                    for n, (kind, c0, width) in enumerate(tiles):
                        m = n - SL
                        if m >= 0:
                            if m < 3:
                                sp.wait_ge(s["fm_mm"], 3 * (m + 1))
                            else:
                                sp.wait_ge(s["tm_mm"], NT * (m - 2))
                        sp.dma_start(view(n), w[:, :, c0:c0 + width]).then_inc(s[f"w_in{n % SL}"], 16)

                @block.gpsimd
                def _(pool):
                    pool.memset(pad[:, :, 0:1], 0.0).then_inc(s["padded"], 1)
                    pool.memset(pad[:, :, 129:131], 0.0).then_inc(s["padded"], 1)
                    pool.memset(pad[:, :, PADW - 1:PADW], 0.0).then_inc(s["padded"], 1)

                @block.tensor
                def _(pe):
                    for n in range(3):
                        pe.wait_ge(s[f"w_in{n % SL}"], 16 * (n // SL + 1))
                        for m in range(3):
                            c = 3 * n + m
                            if c >= 4:
                                pe.wait_ge(s["fm_act"], c - 3)
                                pe.wait_ge(s["fm_dve"], c - 3)
                            for k in range(KC):
                                for j, (a, b) in enumerate(STREAMS):
                                    mm = pe.matmul(ps[:, 2 * (c % 4) + j, 0:b - a], view(n)[:, k, m * P:(m + 1) * P],
                                                   self.hT[:, k, a:b], start=(k == 0), stop=(k == KC - 1))
                            mm.then_inc(s["fm_mm"], 1)
                    pe.wait_ge(s["fm_act"], 9)
                    pe.wait_ge(s["fm_dve"], 9)
                    for n in range(3, 7):
                        pe.wait_ge(s[f"w_in{n % SL}"], 16 * (n // SL + 1))
                        for t in range(NT):
                            q = NT * (n - 3) + t
                            if q >= 4:
                                pe.wait_ge(s["tm_out"], q - 3)
                            for k in range(KC):
                                mm = pe.matmul(ps[:, q % 4, 0:TMT], self.hT[:, k, t * P:(t + 1) * P],
                                               view(n)[:, k, :], start=(k == 0), stop=(k == KC - 1))
                            mm.then_inc(s["tm_mm"], 1)
                            if n >= 4 and q - NT < 9:
                                c = q - NT
                                pe.wait_ge(s["silu"], c + 1)
                                if c >= 2:
                                    pe.wait_ge(s["qkv_out"], c - 1)
                                for u in range(NT):
                                    x0 = 0 if u == 0 else 130 + (u - 1) * P
                                    b0 = 4 + 2 * (c % 2)
                                    mm = pe.transpose(ps[:, b0 + u // 4, (u % 4) * P:(u % 4 + 1) * P],
                                                      conv[:, c % 2, x0:x0 + P], self.ident)
                                mm.then_inc(s["turned"], 1)

                @block.scalar
                def _(act):
                    for c in range(9):
                        act.wait_ge(s["fm_mm"], c + 1)
                        act.copy(pad[:, c, at[0]:at[0] + P], ps[:, 2 * (c % 4), 0:P]).then_inc(s["fm_act"], 1)
                    for q in range(20):
                        act.wait_ge(s["tm_mm"], q + 1)
                        n, t = divmod(q, NT)
                        act.copy(tm[:, t, n * TMT:(n + 1) * TMT], ps[:, q % 4, 0:TMT]).then_inc(s["tm_out"], 1)
                        c = q - NT + 1
                        if 0 <= c < 9:
                            act.wait_ge(s["conv"], c + 1)
                            act.activation(conv[:, c % 2, :], conv[:, c % 2, :], ACT.Silu).then_inc(s["silu"], 1)

                @block.vector
                def _(dve):
                    chain = Chain(dve, s["chain"])
                    for c in range(9):
                        dve.wait_ge(s["fm_mm"], c + 1)
                        dve.tensor_copy(pad[:, c, at[1]:at[1] + 4 * P], ps[:, 2 * (c % 4) + 1, :]
                                        ).then_inc(s["fm_dve"], 1)
                    dve.wait_ge(s["padded"], 3)
                    dve.wait_ge(s["fm_act"], 9)
                    dve.wait_ge(s["fm_dve"], 9)

                    def convolve(c):
                        tap = [self.cols[:, 112 + 40 + (l * 3 + u) * 9 + c:][:, 0:1] for u in range(3)]
                        y = conv[:, c % 2, :]
                        if c >= 2:
                            dve.wait_ge(s["turned"], c - 1)
                        chain(dve.tensor_scalar(y, pad[:, c, 0:PADW - 2], tap[0], None, ALU.mult))
                        chain(dve.scalar_tensor_tensor(out=y, in0=pad[:, c, 1:PADW - 1], scalar=tap[1], in1=y,
                                                       op0=ALU.mult, op1=ALU.add))
                        dve.scalar_tensor_tensor(out=y, in0=pad[:, c, 2:PADW], scalar=tap[2], in1=y,
                                                 op0=ALU.mult, op1=ALU.add).then_inc(s["conv"], 1)
                    convolve(0)
                    convolve(1)
                    for c in range(9):
                        dve.wait_ge(s["turned"], c + 1)
                        b0 = 4 + 2 * (c % 2)
                        dve.tensor_copy(self.qkv[:, 0:NT, 2 * c:2 * c + 2, :].rearrange("p t h d -> p t (h d)"),
                                        ps[:, b0:b0 + 2, :].rearrange("p b (t d) -> p (b t) d", t=4)[:, 0:NT, :]
                                        ).then_inc(s["qkv_out"], 1)
                        if c + 2 < 9:
                            convolve(c + 2)

    def delta_prep(self, l):
        nc, i, ps, tm, qkv, bg = self.nc, self.i, self.ps, self.tm, self.qkv, self.bg
        with ExitStack() as scope:
            def sb(name, shape, dt=F32):
                return scope.enter_context(nc.sbuf_tensor(f"{name}_{l}", shape, dt))
            sq = sb("qk_sq", [P, NT, 12, HD])
            r = sb("qk_r", [P, NT, 12])
            ab = sb("a_log_dt", [P, 2, 2, HA])
            e1 = sb("e1", [P, NT, 2, HA])
            e2 = sb("e2", [P, NT, 2, HA])
            na = sb("na", [P, 12])
            with stage(nc, "par_in chain expd lnd neg g_done rooted qk_done turned kq_out cum eg_out half") as (block, s):
                @block.sync
                def _(sp):
                    for j, name in enumerate(("dn_a_log", "dn_dt_bias")):
                        sp.dma_start(ab[:, j], i[name][l].partition_broadcast(P)).then_inc(s["par_in"], 16)

                braw = tm[:, :, BE0:BE0 + 12]
                araw = tm[:, :, AR0:AR0 + 12]
                e1f = e1[:].rearrange("p t d h -> p t (d h)")
                e2f = e2[:].rearrange("p t d h -> p t (d h)")
                beta = bg[:, 0].rearrange("p t d h -> p t (d h)")
                g = bg[:, 1].rearrange("p t d h -> p t (d h)")
                abf = ab[:].rearrange("p j d h -> p j (d h)")

                @block.vector
                def _(dve):
                    chain = Chain(dve, s["chain"])
                    dve.wait_ge(s["par_in"], 32)
                    chain(dve.tensor_tensor(g, araw, bcast_mid(abf[:, 1], NT), ALU.add))
                    chain(dve.tensor_scalar(e2f, g, -1.0, None, ALU.mult))
                    dve.tensor_tensor(e2f, e2f, g, ALU.min).then_inc(s["neg"], 1)
                    dve.wait_ge(s["neg"], 1)
                    chain(dve.tensor_scalar(g, g, 0.0, None, ALU.max))
                    dve.wait_ge(s["expd"], 3)
                    chain(dve.tensor_scalar(e1f, e1f, 1.0, None, ALU.add))
                    chain(dve.reciprocal(beta, e1f))
                    dve.tensor_scalar(e2f, e2f, 1.0, None, ALU.add).then_inc(s["neg"], 1)
                    chain(dve.tensor_scalar(na[:], na[:], -1.0, None, ALU.mult))
                    dve.wait_ge(s["lnd"], 1)
                    chain(dve.tensor_tensor(g, g, e2f, ALU.add))
                    dve.tensor_tensor(g, g, bcast_mid(na[:], NT), ALU.mult).then_inc(s["g_done"], 1)
                    chain(dve.tensor_tensor(sq[:], qkv[:, :, 0:12, :], qkv[:, :, 0:12, :], ALU.mult))
                    chain(dve.tensor_reduce(r[:], sq[:], AX.X, ALU.add))
                    dve.tensor_scalar(r[:], r[:], EPS, None, ALU.add).then_inc(s["neg"], 1)
                    dve.wait_ge(s["rooted"], 1)
                    chain(dve.reciprocal(r[:], r[:]))
                    chain(dve.tensor_scalar(r[:, :, 0:HA], r[:, :, 0:HA], HD ** -0.5, None, ALU.mult))
                    for t in range(NT):
                        dve.tensor_tensor(qkv[:, t, 0:12, :], qkv[:, t, 0:12, :], bcast_last(r[:, t, :], HD),
                                          ALU.mult).then_inc(s["qk_done"], 1)
                    for t in range(NT):
                        dve.wait_ge(s["turned"], t + 1)
                        b0 = 2 * (t % 2)
                        dve.tensor_copy(self.kqT[:, t].rearrange("p h j n -> p (h j) n"),
                                        ps[:, b0:b0 + 2, :].rearrange("p b (t d) -> p (b t) d", t=4)[:, 0:6, :]
                                        ).then_inc(s["kq_out"], 1)
                    dve.wait_ge(s["eg_out"], 1)
                    for j in range(2):
                        dve.tensor_copy(self.glp[64 * j:64 * j + 64].rearrange("p d t h -> p (d t) h"),
                                        self.eg[64 * j:64 * j + 64, 2].rearrange("p d t (h j) -> p (d t) h j", j=2)
                                        [:, :, :, j]).then_inc(s["half"], 1)

                @block.scalar
                def _(act):
                    act.wait_ge(s["par_in"], 32)
                    act.activation(e1f, braw, ACT.Exp, scale=-1.0).then_inc(s["expd"], 1)
                    act.activation(na[:], abf[:, 0], ACT.Exp).then_inc(s["expd"], 1)
                    act.wait_ge(s["neg"], 1)
                    act.activation(e2f, e2f, ACT.Exp).then_inc(s["expd"], 1)
                    act.wait_ge(s["neg"], 2)
                    act.activation(e2f, e2f, ACT.Ln).then_inc(s["lnd"], 1)
                    act.wait_ge(s["cum"], 1)
                    act.activation(self.eg[:].rearrange("p k d t h -> p (k d t h)"), ps[:, 4, 0:180], ACT.Exp
                                   ).then_inc(s["eg_out"], 1)
                    act.wait_ge(s["neg"], 3)
                    act.activation(r[:], r[:], ACT.Sqrt).then_inc(s["rooted"], 1)

                @block.tensor
                def _(pe):
                    pe.wait_ge(s["g_done"], 1)
                    for k, table in enumerate((C_U, C_SL, None)):
                        for d in range(2):
                            o = (2 * k + d) * NT * HA
                            lhsT = self.ones if table is None else self.c(table + d)
                            mm = pe.matmul(ps[:, 4, o:o + NT * HA], lhsT, bg[:, 1, :, d, :], start=True, stop=True)
                    mm.then_inc(s["cum"], 1)
                    for t in range(NT):
                        pe.wait_ge(s["qk_done"], t + 1)
                        if t >= 2:
                            pe.wait_ge(s["kq_out"], t - 1)
                        for pr in range(3):
                            for j, h0 in enumerate((HA, 0)):
                                n = 2 * pr + j
                                mm = pe.transpose(ps[:, 2 * (t % 2) + n // 4, (n % 4) * P:(n % 4 + 1) * P],
                                                  qkv[:, t, h0 + 2 * pr:h0 + 2 * pr + 2, :], self.ident)
                        mm.then_inc(s["turned"], 1)

    def delta_scan(self, l):
        nc, i, ps, qkv, bg = self.nc, self.i, self.ps, self.qkv, self.bg
        kqT, eg = self.kqT, self.eg
        W = HA * P
        with ExitStack() as scope:
            def sb(name, shape, dt=F32):
                return scope.enter_context(nc.sbuf_tensor(f"{name}_{l}", shape, dt))
            XT = sb("XT", [P, NT, 2, HA, P])
            AT = sb("AT", [P, NT, 2, HA, P])
            with ExitStack() as inner:
                def sbi(name, shape, dt=F32):
                    return inner.enter_context(nc.sbuf_tensor(f"{name}_{l}", shape, dt))
                KQ = sbi("KQ", [P, HA, 2, P])
                MT = [sbi("MT", [P, HA, P])[:], self.mt1]
                DT = sbi("DT", [P, 2, HA, P])
                Y = sbi("Y", [P, 2, HA, P])
                X = sbi("X", [P, 2, HA, P])
                L = NLEV - 1
                with stage(nc, "gu dm dexp kq kq_out dmask mt xt0 ms y y_out p xt xturn x_out chain pchain") as (block, s):
                    def two(d, which):
                        return ps[:, 4 * d + 2 * which:4 * d + 2 * which + 2, :].rearrange("p b n -> p (b n)")[:, 0:W]

                    def head(ap, h):
                        return ap[:, h * P:(h + 1) * P]

                    def flat(ap):
                        return ap.rearrange("p h n -> p (h n)")

                    @block.tensor
                    def _(pe):
                        for t in range(NT):
                            for d in range(2):
                                pe.wait_ge(s["gu"], 2 * t + d + 1)
                                if t >= 1:
                                    pe.wait_ge(s["xt"], 2 * (t * L - 1) + d + 1)
                                    pe.wait_ge(s["x_out"], 2 * (t * L - 1) + d + 1)
                                for b, (c0, c1) in enumerate(((0, 512), (512, W))):
                                    mm = pe.matmul(two(d, 0)[:, c0:c1], self.c(C_SL + d), flat(Y[:, d])[:, c0:c1],
                                                   start=True, stop=True)
                                mm.then_inc(s["dm"], 1)
                            for h in range(HA):
                                q = 64 * (h % 2)
                                mm = pe.matmul(ps[:, 2 + 4 * (h % 2) + h // 4, (h // 2 % 2) * 256:(h // 2 % 2) * 256 + 256],
                                               kqT[q:q + 64, t, h // 2, 0, :], kqT[q:q + 64, t, h // 2, :, :],
                                               start=True, stop=True)
                            mm.then_inc(s["kq"], 1)
                            for lev in range(NLEV):
                                n = t * L + lev - 1
                                if lev:
                                    for d in range(2):
                                        pe.wait_ge(s["ms"], 2 * n + d + 1)
                                        pe.wait_ge(s["x_out"], 2 * n + d + 1)
                                        for h in range(HA):
                                            mm = pe.matmul(head(two(d, 1), h), DT[:, d, h], X[:, d, h],
                                                           start=True, stop=True)
                                        mm.then_inc(s["y"], 1)
                                    for d in range(2):
                                        pe.wait_ge(s["y_out"], 2 * n + d + 1)
                                        for h in range(HA):
                                            mm = pe.matmul(head(two(d, 0), h), Y[:, d, h], XT[:, t, d, h],
                                                           start=True, stop=True)
                                        mm.then_inc(s["p"], 1)
                                if lev < NLEV - 1:
                                    for d in range(2):
                                        if lev:
                                            pe.wait_ge(s["xt"], 2 * n + d + 1)
                                        else:
                                            pe.wait_ge(s["xt0"], 2 * t + d + 1)
                                            pe.wait_ge(s["kq_out"], t + 1)
                                            pe.wait_ge(s["pchain"], t + 1)
                                        for h in range(HA):
                                            mm = pe.transpose(head(two(d, 1), h), XT[:, t, d, h], self.ident)
                                        mm.then_inc(s["xturn"], 1)

                    @block.scalar
                    def _(act):
                        for t in range(NT):
                            for d in range(2):
                                act.wait_ge(s["dm"], 2 * t + d + 1)
                                act.activation(flat(DT[:, d]), two(d, 0), ACT.Exp).then_inc(s["dexp"], 1)
                            act.wait_ge(s["kq"], t + 1)
                            for par, done in ((0, "pchain"), (1, "kq_out")):
                                act.copy(KQ[:].rearrange("p (i r) j n -> p r i (j n)", r=2)[:, par],
                                         two(par, 1).rearrange("p (i n) -> p i n", i=3)).then_inc(s[done], 1)
                            for lev in range(NLEV):
                                n = t * L + lev - 1
                                if lev:
                                    for d in range(2):
                                        act.wait_ge(s["y"], 2 * n + d + 1)
                                        act.copy(flat(Y[:, d]), two(d, 1)).then_inc(s["y_out"], 1)
                                if lev < NLEV - 1:
                                    for d in range(2):
                                        act.wait_ge(s["xturn"], 2 * (n + 1) + d + 1)
                                        act.copy(flat(X[:, d]), two(d, 1)).then_inc(s["x_out"], 1)

                    @block.gpsimd
                    def _(pool):
                        for t in range(NT):
                            for lev in range(1, NLEV):
                                n = t * L + lev - 1
                                for d in range(2):
                                    if lev == 1:
                                        pool.wait_ge(s["xt0"], 2 * t + d + 1)
                                    else:
                                        pool.wait_ge(s["y"], 2 * (n - 1) + d + 1)
                                    pool.tensor_tensor(DT[:, d], MT[d], bcast_mid(self.c(C_LV + d * NLEV + lev), HA),
                                                       ALU.mult).then_inc(s["ms"], 1)

                    @block.vector
                    def _(dve):
                        chain = Chain(dve, s["chain"])
                        for t in range(NT):
                            for d in range(2):
                                if t:
                                    dve.wait_ge(s["p"], 2 * (t * L - 1) + d + 1)
                                dve.tensor_tensor(Y[:, d], bcast_mid(self.c(C_U + d), HA),
                                                  bcast_last(bg[:, 1, t, d, :], P), ALU.mult).then_inc(s["gu"], 1)
                            for d in range(2):
                                dve.wait_ge(s["dexp"], 2 * t + d + 1)
                                chain(dve.tensor_tensor(DT[:, d], DT[:, d], bcast_mid(self.c(C_U + d), HA), ALU.mult))
                                dve.wait_ge(s["kq_out"], t + 1)
                                dve.wait_ge(s["pchain"], t + 1)
                                dve.tensor_tensor(AT[:, t, d], KQ[:, :, 1, :], DT[:, d], ALU.mult).then_inc(s["mt"], 1)
                                chain(dve.tensor_tensor(MT[d], KQ[:, :, 0, :], DT[:, d], ALU.mult))
                                chain(dve.tensor_tensor(MT[d], MT[d], bcast_last(bg[:, 0, t, d, :], P), ALU.mult))
                                chain(dve.tensor_tensor(XT[:, t, d], MT[d], bcast_mid(self.c(C_LV + d * NLEV), HA),
                                                        ALU.mult))
                                dve.tensor_tensor(XT[:, t, d], bcast_mid(self.ident, HA), XT[:, t, d], ALU.subtract
                                                  ).then_inc(s["xt0"], 1)
                            for lev in range(1, NLEV):
                                n = t * L + lev - 1
                                for d in range(2):
                                    dve.wait_ge(s["p"], 2 * n + d + 1)
                                    if lev == 1:
                                        dve.wait_ge(s["xt0"], 2 * t + d + 1)
                                    else:
                                        dve.wait_ge(s["xt"], 2 * (n - 1) + d + 1)
                                    dve.tensor_tensor(flat(XT[:, t, d]), flat(XT[:, t, d]), two(d, 0), ALU.subtract
                                                      ).then_inc(s["xt"], 1)
            S = sb("S", [P, 2, 2, 3, HD])
            kd_b = sb("kd", [P, NT, HA, HD])
            kd = [qkv[:, :, 0:HA, :], kd_b[:]]
            tk = sb("tk", [P, 2, HA, HD])
            t1 = sb("t1", [P, 2, HA, HD])
            vn = sb("vn", [P, 2, HA, HD])
            tq = sb("tq", [P, 2, HA, HD])
            o = self.oA
            steps = [(0, 0, 0), (0, 0, 1)]
            for n in range(4):
                steps += [(1, 1 + n, 0), (1, 4 - n, 1)]
            names = "s_in s_zero kd o_zero ks t1 xt1 vn av s_new o_sum s_out chain sdec used"
            with stage(nc, names) as (block, s):
                @block.sync
                def _(sp):
                    for d in range(2):
                        for j in range(2):
                            sp.dma_start(S[64 * j:64 * j + 64, 1, d], i["state_delta"][0, l, d].rearrange(
                                "(h j) k v -> j k h v", j=2)[j]).then_inc(s["s_in"], 16)
                    for d in range(2):
                        sp.wait_ge(s["s_new"], d + 1)
                        for j in range(2):
                            sp.dma_start(self.o["state"][0, l, d].rearrange("(h j) k v -> j k h v", j=2)[j],
                                         S[64 * j:64 * j + 64, 0, d]).then_inc(s["s_out"], 16)
                    sp.wait_ge(s["s_out"], 64)

                @block.gpsimd
                def _(pool):
                    pool.memset(S[:, 0], 0.0).then_inc(s["s_zero"], 1)
                    for n, (st, t, d) in enumerate(steps):
                        pool.tensor_tensor(kd[d][:, t], qkv[:, t, HA:2 * HA, :], bcast_last(eg[:, 1, d, t, :], HD),
                                           ALU.mult).then_inc(s["kd"], 1)

                def bank(n, k, w=HA * HD):
                    return ps[:, 4 * (n % 2) + k, 0:w]

                @block.tensor
                def _(pe):
                    def read_state(n):
                        st, t, d = steps[n]
                        if n == 0:
                            pe.wait_ge(s["s_zero"], 1)
                        elif n == 2:
                            pe.wait_ge(s["s_in"], 64)
                        if n >= 4:
                            pe.wait_ge(s["s_new"], n - 1)
                        if n >= 2:
                            pe.wait_ge(s["o_sum"], n - 1)
                        for j in range(2):
                            for h in range(HA):
                                q = 64 * (h % 2)
                                o0 = (3 * j + h // 2) * HD
                                mm = pe.matmul(bank(n, h % 2)[:, o0:o0 + HD], kqT[q:q + 64, t, h // 2, j, :],
                                               S[q:q + 64, st, d, h // 2, :], start=True, stop=True)
                        mm.then_inc(s["ks"], 1)
                    for n0 in range(0, len(steps), 2):
                        for n in (n0, n0 + 1):
                            read_state(n)
                        for n in (n0, n0 + 1):
                            st, t, d = steps[n]
                            pe.wait_ge(s["t1"], n + 1)
                            for h in range(HA):
                                mm = pe.matmul(bank(n, 2)[:, h * HD:(h + 1) * HD], XT[:, t, d, h], t1[:, d, h],
                                               start=True, stop=True)
                            mm.then_inc(s["xt1"], 1)
                        for n in (n0, n0 + 1):
                            st, t, d = steps[n]
                            pe.wait_ge(s["vn"], n + 1)
                            pe.wait_ge(s["kd"], n + 1)
                            for h in range(HA):
                                q = 64 * (h % 2)
                                mm = pe.matmul(ps[q:q + 64, 4 * (n % 2) + 3, (h // 2) * HD:(h // 2 + 1) * HD],
                                               kd[d][:, t, h], vn[:, d, h], start=True, stop=True)
                            for h in range(HA):
                                mm = pe.matmul(bank(n, 2)[:, h * HD:(h + 1) * HD], AT[:, t, d, h], vn[:, d, h],
                                               start=True, stop=True)
                            mm.then_inc(s["av"], 1)

                @block.vector
                def _(dve):
                    chain = Chain(dve, s["chain"])

                    def v3(ap):
                        return ap.rearrange("p (h d) -> p h d", d=HD)

                    def by_parity(ap):
                        return ap.rearrange("p (i r) d -> p r i d", r=2)

                    def read_out(n, j):
                        b = 4 * (n % 2)
                        return ps[:, b:b + 2, 192 * j:192 * j + 192].rearrange("p r (i d) -> p r i d", d=HD)
                    for n0 in range(0, len(steps), 2):
                        for n in (n0, n0 + 1):
                            st, t, d = steps[n]
                            dve.wait_ge(s["ks"], n + 1)
                            chain(dve.tensor_tensor(by_parity(tk[:, d]), read_out(n, 0),
                                                    by_parity(bcast_last(eg[:, 0, d, t, :], HD)), ALU.mult))
                            dve.tensor_tensor(t1[:, d], qkv[:, t, 2 * HA:3 * HA, :], tk[:, d], ALU.subtract
                                              ).then_inc(s["t1"], 1)
                        for n in (n0, n0 + 1):
                            st, t, d = steps[n]
                            dve.tensor_tensor(by_parity(tq[:, d]), read_out(n, 1),
                                              by_parity(bcast_last(eg[:, 0, d, t, :], HD)), ALU.mult
                                              ).then_inc(s["used"], 1)
                            dve.tensor_tensor(S[:, st, d], S[:, st, d], bcast_last(self.glp[:, d, t, :], HD), ALU.mult
                                              ).then_inc(s["sdec"], 1)
                        for n in (n0, n0 + 1):
                            st, t, d = steps[n]
                            dve.wait_ge(s["xt1"], n + 1)
                            dve.tensor_tensor(vn[:, d], v3(bank(n, 2)), bcast_last(bg[:, 0, t, d, :], HD), ALU.mult
                                              ).then_inc(s["vn"], 1)
                        for n in (n0, n0 + 1):
                            st, t, d = steps[n]
                            dve.wait_ge(s["used"], n + 1)
                            ot = o[:, t, 0:AW]
                            if n < 2:
                                first = d == 0
                            else:
                                first = n0 < 6
                            if not first:
                                chain(dve.tensor_tensor(ot, ot, tq[:, d].rearrange("p h d -> p (h d)"), ALU.add))
                            dve.wait_ge(s["av"], n + 1)
                            dve.wait_ge(s["sdec"], n + 1)
                            dve.tensor_tensor(S[:, st, d], S[:, st, d], v3(bank(n, 3, 192)), ALU.add
                                              ).then_inc(s["s_new"], 1)
                            if first:
                                dve.tensor_tensor(ot, bank(n, 2), tq[:, d].rearrange("p h d -> p (h d)"), ALU.add
                                                  ).then_inc(s["o_sum"], 1)
                            else:
                                dve.tensor_tensor(ot, bank(n, 2), ot, ALU.add).then_inc(s["o_sum"], 1)
                            dve.wait_ge(s["o_sum"], n + 1)
                            dve.wait_ge(s["s_new"], n + 1)

    def attn_prep_and_attend(self, l):
        nc, i, ps, tm, mixed = self.nc, self.i, self.ps, self.tm, self.mixed
        lam_init = 0.8 - 0.6 * math.exp(-0.3 * l)
        with ExitStack() as scope:
            def sb(name, shape, dt=F32):
                return scope.enter_context(nc.sbuf_tensor(f"{name}_{l}", shape, dt))
            kBT = sb("kBT", [P, KEYS])
            qBT = sb("qBT", [P, 3, T])
            kCT = sb("kCT", [P, 2, KEYS])
            qCT = sb("qCT", [P, 2, T])
            vB = sb("vB", [P, 2, KVB * HD])
            vC = sb("vC", [P, 2, HC * HD])
            nlam = sb("nlam", [P, 1])
            gdiff = sb("gdiff", [P, HD])
            with ExitStack() as inner:
                def sbi(name, shape, dt=F32):
                    return inner.enter_context(nc.sbuf_tensor(f"{name}_{l}", shape, dt))
                sq = sbi("n_sq", [P, NT, 8, HD])
                r = sbi("n_r", [P, NT, 8])
                ro = sbi("n_ro", [P, NT, HA])
                gqk = sbi("gqk", [P, 8, HD])
                gdn = sbi("gdn", [P, HD])
                ta = sbi("rope_a", [P, 512])
                tb = sbi("rope_b", [P, 512])
                rope = sbi("rope", [P, 4, 192])
                ckB = sbi("ckB", [P, 2, KVB * HD])
                ckC = sbi("ckC", [P, 2, HC * HD])
                lv = sbi("lv", [P, 4, DHC])
                lp = sbi("lp", [P, 2, DHC])
                ls = sbi("ls", [P, 2])
                names = ("par_in cache_in chain ms root gate silu normed roped cturned c_out turned t_out ctx_out "
                         "lsum lexp lam o_done")
                with stage(nc, names) as (block, s):
                    @block.sync
                    def _(sp):
                        for h in range(HB):
                            sp.dma_start(gqk[:, h], i["gqa_q_norm"][l].partition_broadcast(P)).then_inc(s["par_in"], 16)
                        for h in range(KVB):
                            sp.dma_start(gqk[:, HB + h], i["gqa_k_norm"][l].partition_broadcast(P)).then_inc(s["par_in"], 16)
                        sp.dma_start(gdn[:], i["dn_norm"][l].partition_broadcast(P)).then_inc(s["par_in"], 16)
                        sp.dma_start(gdiff[:], i["diff_norm"][l].partition_broadcast(P)).then_inc(s["par_in"], 16)
                        sp.dma_start(lv[:], i["diff_lambda"][l].partition_broadcast(P)).then_inc(s["par_in"], 16)
                        sp.dma_start(ckB[:], i["cache_gqa_k"][0, l].rearrange("(t p) h d -> p t (h d)", p=P)).then_inc(s["cache_in"], 16)
                        sp.dma_start(ckC[:], i["cache_diff_k"][0, l].rearrange("(t p) h m d -> p t (h m d)", p=P)).then_inc(s["cache_in"], 16)
                        sp.dma_start(vB[:], i["cache_gqa_v"][0, l].rearrange("(t p) h d -> p t (h d)", p=P)).then_inc(s["cache_in"], 16)
                        sp.dma_start(vC[:], i["cache_diff_v"][0, l].rearrange("(t p) h d -> p t (h d)", p=P)).then_inc(s["cache_in"], 16)
                        sp.dma_start(rope[:], i["rope"]).then_inc(s["par_in"], 16)
                        for name, c0, n, pat in (("gv", VB0, KVB * HD, "t h d -> t (h d)"), ("dk", KCC0, HC * HD, "t h m d -> t (h m d)"),
                                                 ("dv", VC0, HC * HD, "t h d -> t (h d)")):
                            sp.dma_start(self.o[name][0, l].rearrange(pat), tm[:, 0, c0:c0 + n]).then_inc(s["ctx_out"], 16)
                        sp.wait_ge(s["normed"], 1)
                        sp.dma_start(self.o["gk"][0, l].rearrange("t h d -> t (h d)"), sq[:, 0, HB:8].rearrange("p h d -> p (h d)")).then_inc(s["ctx_out"], 16)
                        sp.wait_ge(s["ctx_out"], 64)
                        sp.wait_ge(s["cache_in"], 64)

                    qk = tm[:, :, QB0:VB0].rearrange("p t (h d) -> p t h d", d=HD)
                    oA = self.oA[:].rearrange("p t (h d) -> p t h d", d=HD)

                    @block.vector
                    def _(dve):
                        chain = Chain(dve, s["chain"])
                        dve.wait_ge(s["par_in"], 12 * 16)
                        chain(dve.tensor_tensor(sq[:], qk, qk, ALU.mult))
                        chain(dve.tensor_reduce(r[:], sq[:], AX.X, ALU.add))
                        dve.tensor_scalar(r[:], r[:], 1.0 / HD, EPS, ALU.mult, ALU.add).then_inc(s["ms"], 1)
                        dve.wait_ge(s["ms"], 1)
                        chain(dve.tensor_tensor(sq[:, :, 0:HA], oA, oA, ALU.mult))
                        chain(dve.tensor_reduce(ro[:], sq[:, :, 0:HA], AX.X, ALU.add))
                        dve.tensor_scalar(ro[:], ro[:], 1.0 / HD, EPS, ALU.mult, ALU.add).then_inc(s["ms"], 1)
                        for j in range(2):
                            chain(dve.tensor_tensor(lp[:, j], lv[:, 2 * j], lv[:, 2 * j + 1], ALU.mult))
                        dve.tensor_reduce(ls[:], lp[:], AX.X, ALU.add).then_inc(s["lsum"], 1)
                        dve.wait_ge(s["root"], 2)
                        chain(dve.reciprocal(r[:], r[:]))
                        chain(dve.reciprocal(ro[:], ro[:]))
                        for t in range(NT):
                            chain(dve.tensor_tensor(qk[:, t], qk[:, t], bcast_last(r[:, t, :], HD), ALU.mult))
                            chain(dve.tensor_tensor(sq[:, t, 0:HB].rearrange("p (h g) d -> p g h d", g=2),
                                                    qk[:, t, 0:HB].rearrange("p (g h) d -> p g h d", g=2),
                                                    gqk[:, 0:HB].rearrange("p (g h) d -> p g h d", g=2), ALU.mult))
                            dve.tensor_tensor(sq[:, t, HB:8], qk[:, t, HB:8], gqk[:, HB:8], ALU.mult
                                              ).then_inc(s["normed"], 1)
                        for t in range(1, NT):
                            dve.wait_ge(s["normed"], t + 1)
                            for kind, (x0, hd, tab) in enumerate(((QB0, HD, 0), (QC0, DHC, 128))):
                                nh, nf = 512 // hd, hd // 4
                                x = tm[:, t, x0:x0 + 512] if kind else sq[:, t].rearrange("p h d -> p (h d)")
                                cos = rope[:, t - 1, tab:tab + hd]
                                sin = rope[:, t - 1, tab + hd:tab + 2 * hd]

                                def quarters(ap, h):
                                    return ap.rearrange("p (n a h f) -> p n a h f", a=2, h=2, f=nf)[:, :, :, h, :]
                                dve.tensor_tensor(ta[:].rearrange("p (n d) -> p n d", d=hd), x.rearrange("p (n d) -> p n d", d=hd),
                                                  bcast_mid(cos, nh), ALU.mult).then_inc(s["gate"], 1)
                                for half in range(2):
                                    sn = sin.rearrange("p (a h f) -> p a h f", a=2, h=2)[:, :, half, :]
                                    dve.tensor_tensor(quarters(tb[:], half), quarters(x, 1 - half),
                                                      sn.unsqueeze(1).to_broadcast([P, nh, 2, nf]), ALU.mult).then_inc(s["gate"], 1)
                                dve.wait_ge(s["gate"], 6 * (t - 1) + 3 * kind + 3)
                                dve.tensor_tensor(x, ta[:], tb[:], ALU.add).then_inc(s["roped"], 1)
                                dve.wait_ge(s["roped"], 2 * (t - 1) + kind + 1)
                        dve.wait_ge(s["silu"], 1)
                        for t in range(NT):
                            chain(dve.tensor_tensor(oA[:, t], oA[:, t], bcast_last(ro[:, t, :], HD), ALU.mult))
                            chain(dve.tensor_tensor(oA[:, t], oA[:, t], bcast_mid(gdn[:], HA), ALU.mult))
                            chain(dve.tensor_tensor(mixed[:, t, 0:AW], self.oA[:, t], tm[:, t, Z0:Z0 + AW], ALU.mult))
                        dve.wait_ge(s["lexp"], 1)
                        chain(dve.tensor_tensor(nlam[:], ls[:, 1:2], ls[:, 0:1], ALU.subtract))
                        chain(dve.tensor_scalar(nlam[:], nlam[:], -lam_init, None, ALU.add))
                        chain(dve.tensor_scalar(gdiff[:], gdiff[:], 1.0 - lam_init, None, ALU.mult))

                    @block.scalar
                    def _(act):
                        act.wait_ge(s["ms"], 1)
                        act.activation(r[:], r[:], ACT.Sqrt).then_inc(s["root"], 1)
                        act.wait_ge(s["ms"], 2)
                        act.activation(ro[:], ro[:], ACT.Sqrt).then_inc(s["root"], 1)
                        act.wait_ge(s["lsum"], 1)
                        act.activation(ls[:], ls[:], ACT.Exp).then_inc(s["lexp"], 1)
                        act.activation(tm[:, :, Z0:Z0 + AW], tm[:, :, Z0:Z0 + AW], ACT.Silu).then_inc(s["silu"], 1)
                        act.wait_ge(s["cturned"], 1)
                        act.copy(kBT[:, P:P + PAST], ps[:, 0, 0:256]).then_inc(s["c_out"], 1)
                        for c in range(2):
                            act.copy(kCT[:, c, P:P + PAST], ps[:, 1, 256 * c:256 * c + 256]).then_inc(s["c_out"], 1)
                        for t in range(NT):
                            act.wait_ge(s["turned"], t + 1)
                            b = ps[:, 2 + 2 * (t % 2):4 + 2 * (t % 2), :].rearrange("p b (n q) -> p (b n) q", n=4)
                            k0 = 0 if t == 0 else P + PAST + (t - 1) * P
                            act.copy(kBT[:, k0:k0 + P], b[:, 0, :]).then_inc(s["t_out"], 1)
                            act.copy(qBT[:, :, t * P:(t + 1) * P], b[:, 1:4, :]).then_inc(s["t_out"], 1)
                            act.copy(kCT[:, :, k0:k0 + P], b[:, 4:6, :]).then_inc(s["t_out"], 1)
                            act.copy(qCT[:, :, t * P:(t + 1) * P], b[:, 6:8, :]).then_inc(s["t_out"], 1)

                    @block.tensor
                    def _(pe):
                        pe.wait_ge(s["cache_in"], 64)
                        for u in range(2):
                            pe.transpose(ps[:, 0, u * P:(u + 1) * P], ckB[:, u, :], self.ident)
                            for c in range(2):
                                mm = pe.transpose(ps[:, 1, 256 * c + u * P:256 * c + (u + 1) * P],
                                                  ckC[:, u, c * P:(c + 1) * P], self.ident)
                        mm.then_inc(s["cturned"], 1)
                        for t in range(NT):
                            if t == 0:
                                pe.wait_ge(s["normed"], 1)
                            else:
                                pe.wait_ge(s["roped"], 2 * t)
                            if t >= 2:
                                pe.wait_ge(s["t_out"], 4 * (t - 1))
                            b0 = 2 + 2 * (t % 2)
                            src = [sq[:, t, HB:8]] + [sq[:, t, 2 * h:2 * h + 2] for h in range(3)]
                            src += [tm[:, t, KCC0 + c * P:KCC0 + (c + 1) * P] for c in range(2)]
                            src += [tm[:, t, QC0 + c * P:QC0 + (c + 1) * P] for c in range(2)]
                            for n, a in enumerate(src):
                                mm = pe.transpose(ps[:, b0 + n // 4, (n % 4) * P:(n % 4 + 1) * P], a, self.ident)
                            mm.then_inc(s["turned"], 1)

            NP = 4
            pr = sb("probs", [P, NP, 768])
            pT = sb("probsT", [P, 2, 768])
            st = sb("softmax_stats", [P, 2 * NP, 4])
            oC = sb("oC", [P, NT, HC, HD])
            units, maps = [], []
            for t in range(NT):
                for h in range(HB):
                    units.append(("B", t, h, [len(maps)]))
                    maps.append(("B", t, h, 0))
                for h in range(HC):
                    units.append(("C", t, h, [len(maps), len(maps) + 1]))
                    maps += [("C", t, h, 0), ("C", t, h, 1)]

            def nkeys(t):
                return P if t == 0 else PAST + 4 * P

            def keys(t):
                return (0, P) if t == 0 else (P, KEYS)

            def values(t, kt, kind, h):
                c0 = (h // 3) * HD if kind == "B" else h * HD
                base = VB0 if kind == "B" else VC0
                if t == 0:
                    return tm[:, 0, base + c0:base + c0 + HD]
                if kt < 2:
                    return (vB if kind == "B" else vC)[:, kt, c0:c0 + HD]
                return tm[:, kt - 1, base + c0:base + c0 + HD]
            with stage(nc, "scores smax nmax probs rsum a_done pturn p_out pv o_out chain sc1") as (block, s):
                @block.tensor
                def _(pe):
                    def scores(m):
                        kind, t, h, mp = maps[m]
                        if m >= 2:
                            pe.wait_ge(s["probs"], m - 1)
                        k0, k1 = keys(t)
                        if kind == "B":
                            q = 64 * (h // 3)
                            lhsT, rhs = qBT[q:q + 64, h % 3, t * P:(t + 1) * P], kBT[q:q + 64, k0:k1]
                        else:
                            q = 64 * (h % 2) + 32 * mp
                            lhsT, rhs = qCT[q:q + 32, h // 2, t * P:(t + 1) * P], kCT[q:q + 32, h // 2, k0:k1]
                        for a in range(0, k1 - k0, 512):
                            b = min(a + 512, k1 - k0)
                            mm = pe.matmul(ps[:, 2 * (m % 2) + a // 512, 0:b - a], lhsT, rhs[:, a:b], start=True, stop=True,
                                           **({"tile_position": (q, 0)} if q == 96 else {}))
                        mm.then_inc(s["scores"], 1)

                    def finish(u):
                        kind, t, h, ms = units[u]
                        n = nkeys(t) // P
                        pe.wait_ge(s["a_done"], u + 1)
                        if u >= 1:
                            pe.wait_ge(s["p_out"], u)
                        for kt in range(n):
                            mm = pe.transpose(ps[:, 4 + kt // 4, (kt % 4) * P:(kt % 4 + 1) * P],
                                              pr[:, ms[0] % NP, kt * P:(kt + 1) * P], self.ident)
                        mm.then_inc(s["pturn"], 1)

                    def weigh(u):
                        kind, t, h, ms = units[u]
                        n = nkeys(t) // P
                        pe.wait_ge(s["p_out"], u + 1)
                        if u >= 2:
                            pe.wait_ge(s["o_out"], u - 1)
                        for kt in range(n):
                            mm = pe.matmul(ps[:, 6 + u % 2, 0:HD], pT[:, u % 2, kt * P:(kt + 1) * P], values(t, kt, kind, h),
                                           start=(kt == 0), stop=(kt == n - 1))
                        mm.then_inc(s["pv"], 1)
                    done = 0
                    for u in range(len(units) + 2):
                        if u < len(units):
                            for m in units[u][3]:
                                scores(m)
                        if 1 <= u <= len(units):
                            finish(u - 1)
                        if u >= 2:
                            weigh(u - 2)

                @block.vector
                def _(dve):
                    chain = Chain(dve, s["chain"])

                    def smax(m):
                        kind, t, h, mp = maps[m]
                        n = nkeys(t)
                        scale = HD ** -0.5 if kind == "B" else DHC ** -0.5
                        dve.wait_ge(s["scores"], m + 1)
                        sc = ps[:, 2 * (m % 2):2 * (m % 2) + 2, :].rearrange("p b n -> p (b n)")[:, 0:n]
                        dve.tensor_reduce(st[:, m % 8, 0:1], sc, AX.X, ALU.max).then_inc(s["smax"], 1)
                        dve.wait_ge(s["smax"], m + 1)
                        dve.tensor_scalar(st[:, m % 8, 1:2], st[:, m % 8, 0:1], -scale, None, ALU.mult).then_inc(s["nmax"], 1)

                    def combine(u):
                        kind, t, h, ms = units[u]
                        dve.wait_ge(s["probs"], ms[-1] + 1)
                        for m in ms:
                            chain(dve.reciprocal(st[:, m % 8, 3:4], st[:, m % 8, 2:3]))
                        if kind == "B":
                            dve.nop().then_inc(s["a_done"], 1)
                            return
                        n = nkeys(t)
                        a, b = ms[0] % NP, ms[1] % NP
                        chain(dve.tensor_scalar(pr[:, b, 0:n], pr[:, b, 0:n], st[:, ms[1] % 8, 3:4], nlam[:, 0:1], ALU.mult, ALU.mult))
                        dve.scalar_tensor_tensor(out=pr[:, a, 0:n], in0=pr[:, a, 0:n], scalar=st[:, ms[0] % 8, 3:4],
                                                 in1=pr[:, b, 0:n], op0=ALU.mult, op1=ALU.add).then_inc(s["a_done"], 1)

                    def out(u):
                        kind, t, h, ms = units[u]
                        dve.wait_ge(s["pv"], u + 1)
                        if kind == "B":
                            dve.tensor_scalar(mixed[:, t, AW + h * HD:AW + (h + 1) * HD], ps[:, 6 + u % 2, 0:HD],
                                              st[:, ms[0] % 8, 3:4], None, ALU.mult).then_inc(s["o_out"], 1)
                        else:
                            dve.tensor_copy(oC[:, t, h], ps[:, 6 + u % 2, 0:HD]).then_inc(s["o_out"], 1)
                    for u in range(len(units) + 2):
                        if u < len(units):
                            for m in units[u][3]:
                                smax(m)
                        if 1 <= u <= len(units):
                            pass
                        if u < len(units):
                            combine(u)
                        if u >= 2:
                            out(u - 2)

                @block.scalar
                def _(act):
                    def probs(m, u):
                        kind, t, h, mp = maps[m]
                        n = nkeys(t)
                        scale = HD ** -0.5 if kind == "B" else DHC ** -0.5
                        act.wait_ge(s["nmax"], m + 1)
                        if u >= NP // 2:
                            act.wait_ge(s["pturn"], u - 1)
                        sc = ps[:, 2 * (m % 2):2 * (m % 2) + 2, :].rearrange("p b n -> p (b n)")[:, 0:n]
                        act.activation(pr[:, m % NP, 0:n], sc, ACT.Exp, bias=st[:, m % 8, 1:2], scale=scale,
                                       accum_out=st[:, m % 8, 2:3]).then_inc(s["probs"], 1)

                    def evac(u):
                        n = nkeys(units[u][1])
                        act.wait_ge(s["pturn"], u + 1)
                        if u >= 2:
                            act.wait_ge(s["pv"], u - 1)
                        act.copy(pT[:, u % 2, 0:n], ps[:, 4:6, :].rearrange("p b n -> p (b n)")[:, 0:n]).then_inc(s["p_out"], 1)
                    for u in range(len(units) + 1):
                        if u < len(units):
                            for m in units[u][3]:
                                probs(m, u)
                        if u >= 1:
                            evac(u - 1)
            dsq = sb("d_sq", [P, NT, HC, HD])
            dr = sb("d_r", [P, NT, HC])
            with stage(nc, "chain ms root o_done turned act_out dve_out") as (block, s):
                mc = mixed[:, :, 2 * AW:D].rearrange("p t (h d) -> p t h d", d=HD)

                @block.vector
                def _(dve):
                    chain = Chain(dve, s["chain"])
                    chain(dve.tensor_tensor(dsq[:], oC[:], oC[:], ALU.mult))
                    chain(dve.tensor_reduce(dr[:], dsq[:], AX.X, ALU.add))
                    dve.tensor_scalar(dr[:], dr[:], 1.0 / HD, EPS, ALU.mult, ALU.add).then_inc(s["ms"], 1)
                    dve.wait_ge(s["root"], 1)
                    chain(dve.reciprocal(dr[:], dr[:]))
                    for t in range(NT):
                        chain(dve.tensor_tensor(oC[:, t], oC[:, t], bcast_last(dr[:, t, :], HD), ALU.mult))
                        dve.tensor_tensor(mc[:, t], oC[:, t], bcast_mid(gdiff[:], HC), ALU.mult).then_inc(s["o_done"], 1)
                    for n in range(1, 2 * NT, 2):
                        self.mix_out(dve.tensor_copy, dve, s, n)

                @block.scalar
                def _(act):
                    act.wait_ge(s["ms"], 1)
                    act.activation(dr[:], dr[:], ACT.Sqrt).then_inc(s["root"], 1)
                    for n in range(0, 2 * NT, 2):
                        self.mix_out(act.copy, act, s, n)

                @block.tensor
                def _(pe):
                    for n in range(2 * NT):
                        t, g = divmod(n, 2)
                        if n >= 8:
                            pe.wait_ge(s["dve_out" if g else "act_out"], t - 3)
                        if g:
                            pe.wait_ge(s["o_done"], t + 1)
                        for c in range(4):
                            mm = pe.transpose(ps[:, n % 8, c * P:(c + 1) * P], mixed[:, t, (4 * g + c) * P:(4 * g + c + 1) * P], self.ident)
                        mm.then_inc(s["turned"], 1)

    def mix_out(self, copy, eng, s, n):
        t, g = divmod(n, 2)
        eng.wait_ge(s["turned"], n + 1)
        copy(self.hT[:, 4 * g:4 * g + 4, t * P:(t + 1) * P],
             self.ps[:, n % 8, :].rearrange("p (c q) -> p c q", c=4)).then_inc(s["dve_out" if g else "act_out"], 1)

    def out_proj(self, l):
        nc, i, ps = self.nc, self.i, self.ps
        with ExitStack() as scope:
            w = scope.enter_context(nc.sbuf_tensor(f"w_out_{l}", [P, KC, D], F32))
            with stage(nc, "w0 w1 w2 w3 mm added") as (block, s):
                @block.sync
                def _(sp):
                    for q in range(4):
                        sp.dma_start(w[:, :, q * 256:(q + 1) * 256], i["w_out"][l].rearrange("(c p) n -> p c n", p=P)
                                     [:, :, q * 256:(q + 1) * 256]).then_inc(s[f"w{q}"], 16)

                @block.tensor
                def _(pe):
                    for m in range(KC):
                        pe.wait_ge(s[f"w{m // 2}"], 16)
                        if m >= 4:
                            pe.wait_ge(s["added"], 2 * (m - 3))
                        for k in range(KC):
                            for j, (a, b) in enumerate(STREAMS):
                                mm = pe.matmul(ps[:, 2 * (m % 4) + j, 0:b - a], w[:, k, m * P:(m + 1) * P], self.hT[:, k, a:b],
                                               start=(k == 0), stop=(k == KC - 1))
                        mm.then_inc(s["mm"], 1)

                @block.vector
                def _(dve):
                    for m in range(KC):
                        dve.wait_ge(s["mm"], m + 1)
                        for j, (a, b) in enumerate(STREAMS):
                            x = self.xT[:, m, a:b]
                            dve.scalar_tensor_tensor(out=x, in0=ps[:, 2 * (m % 4) + j, 0:b - a], scalar=self.mod[:, l, 2, m, j:j + 1],
                                                     in1=x, op0=ALU.mult, op1=ALU.add).then_inc(s["added"], 1)

    def router(self, gT):
        nc, i, ps = self.nc, self.i, self.ps
        with ExitStack() as scope:
            def sb(name, shape, dt=F32):
                return scope.enter_context(nc.sbuf_tensor(name, shape, dt))
            rw = sb("router_w", [P, KC, NE])
            lg = sb("logits", [P, NT, NE])
            top = sb("top", [P, NT, 8])
            idx = sb("top_idx", [P, NT, 8], U32)
            idf = sb("top_idx_f", [P, NT, 2])
            w = sb("top_w", [P, NT, 2])
            e = sb("top_e", [P, NT, 1])
            io = sb("iota8", [P, NE])
            ga = sb("gate_a", [P, NT, NE])
            gb = sb("gate_b", [P, NT, NE])
            with stage(nc, "w_in mm chain diff expd gate turned io") as (block, s):
                @block.sync
                def _(sp):
                    sp.dma_start(rw[:], i["moe_router"][0].rearrange("(c p) e -> p c e", p=P)).then_inc(s["w_in"], 16)
                    sp.dma_start(io[:], i["iota"].partition_broadcast(P)).then_inc(s["io"], 16)

                @block.tensor
                def _(pe):
                    pe.wait_ge(s["w_in"], 16)
                    for t in range(NT):
                        for k in range(KC):
                            mm = pe.matmul(ps[:, 0, t * NE:(t + 1) * NE], self.hT[:, k, t * P:(t + 1) * P], rw[:, k, :],
                                           start=(k == 0), stop=(k == KC - 1))
                    mm.then_inc(s["mm"], 1)
                    pe.wait_ge(s["gate"], 1)
                    for t in range(NT):
                        mm = pe.transpose(ps[0:NE, 1 + t // 4, (t % 4) * P:(t % 4 + 1) * P], ga[:, t, :], self.ident)
                    mm.then_inc(s["turned"], 1)

                @block.scalar
                def _(act):
                    act.wait_ge(s["diff"], 1)
                    act.activation(e[:], e[:], ACT.Exp).then_inc(s["expd"], 1)

                @block.vector
                def _(dve):
                    chain = Chain(dve, s["chain"])
                    dve.wait_ge(s["mm"], 1)
                    dve.wait_ge(s["io"], 16)
                    chain(dve.tensor_copy(lg[:].rearrange("p t e -> p (t e)"), ps[:, 0, 0:NT * NE]))
                    for t in range(NT):
                        chain(dve.max(top[:, t], lg[:, t]))
                        chain(dve.max_index(idx[:, t], top[:, t], lg[:, t]))
                    chain(dve.tensor_copy(idf[:], idx[:, :, 0:2]))
                    dve.tensor_tensor(e[:], top[:, :, 1:2], top[:, :, 0:1], ALU.subtract).then_inc(s["diff"], 1)
                    dve.wait_ge(s["expd"], 1)
                    chain(dve.tensor_scalar(w[:, :, 1:2], e[:], 1.0, None, ALU.add))
                    chain(dve.reciprocal(w[:, :, 0:1], w[:, :, 1:2]))
                    chain(dve.tensor_tensor(w[:, :, 1:2], w[:, :, 0:1], e[:], ALU.mult))
                    for t in range(NT):
                        chain(dve.tensor_scalar(ga[:, t], io[:], idf[:, t, 0:1], w[:, t, 0:1], ALU.is_equal, ALU.mult))
                        chain(dve.tensor_scalar(gb[:, t], io[:], idf[:, t, 1:2], w[:, t, 1:2], ALU.is_equal, ALU.mult))
                    dve.tensor_tensor(ga[:], ga[:], gb[:], ALU.add).then_inc(s["gate"], 1)
                    dve.wait_ge(s["turned"], 1)
                    chain(dve.tensor_copy(gT[0:NE, 0:512], ps[0:NE, 1, :]))
                    chain(dve.tensor_copy(gT[0:NE, 512:T], ps[0:NE, 2, 0:P]))

    def ffn(self, l, n_exp, w_gu, w_dn, gT=None):
        nc, i, ps = self.nc, self.i, self.ps
        SG = 4
        with ExitStack() as scope:
            def sb(name, shape, dt=F32):
                return scope.enter_context(nc.sbuf_tensor(f"{name}_{l}", shape, dt))
            wg = sb("w_gu_ring", [P, FC, 2, KC, P])
            wd = sb("w_dn_ring", [P, 4, FC, P])
            act_t = sb("act", [P, FC, T])
            names = "gu silu prod dn added chain gb gbo " + " ".join(f"g{j}" for j in range(FC)) + \
                " " + " ".join(f"d{j}" for j in range(4))
            gb = sb("gate_bc", [P, T]) if gT is not None else None
            sel = sb("sel", [NE, NE, P]) if gT is not None else None
            if gT is not None:
                names += " sel"
            with stage(nc, names) as (block, s):
                @block.sync
                def _(sp):
                    if gT is not None:
                        sp.dma_start(sel[:], i["sel"]).then_inc(s["sel"], 16)
                    def load(e, j):
                        for half in range(2):
                            sp.dma_start(wg[:, j, half], w_gu(e, half, j)).then_inc(s[f"g{j}"], 16)

                    for j in range(FC):
                        load(0, j)
                    def load_dn(e, m):
                        sp.dma_start(wd[:, m % 4], w_dn(e, m)).then_inc(s[f"d{m % 4}"], 16)

                    for m in range(4):
                        load_dn(0, m)
                    with sp.Fori(1, n_exp) as e:
                        for j in range(FC):
                            sp.wait_ge(s["gu"], e * FC - FC + j + 1)
                            load(e, j)
                        for m in range(4):
                            sp.wait_ge(s["dn"], e * KC - KC + m + 1)
                            load_dn(e - 1, m + 4)
                        for m in range(4):
                            sp.wait_ge(s["dn"], e * KC - KC + m + 5)
                            load_dn(e, m)
                    for m in range(4):
                        sp.wait_ge(s["dn"], n_exp * KC - KC + m + 1)
                        load_dn(n_exp - 1, m + 4)

                @block.tensor
                def _(pe):
                    def body(e, first):
                        if gT is not None:
                            if first:
                                pe.wait_ge(s["sel"], 16)
                            else:
                                pe.wait_ge(s["added"], e * (2 * KC))
                            for j2, (a, b) in enumerate(STREAMS):
                                mm = pe.matmul(ps[:, j2, 0:b - a], sel[:, self.e_static, :], gT[0:NE, a:b], start=True, stop=True)
                            mm.then_inc(s["gb"], 1)
                        for j in range(FC):
                            pe.wait_ge(s[f"g{j}"], 32 * e + 32)
                            if j >= 2:
                                pe.wait_ge(s["prod"], (e * FC + j - 1) * 2)
                            elif j == 0 and gT is not None:
                                pe.wait_ge(s["gbo"], 2 * e + 2)
                            if j < 2 and not first:
                                pe.wait_ge(s["added"], e * (2 * KC))
                            for half in range(2):
                                for k in range(KC):
                                    for q, (a, b) in enumerate(STREAMS):
                                        mm = pe.matmul(ps[:, 4 * (j % 2) + 2 * half + q, 0:b - a], wg[:, j, half, k, :],
                                                       self.hT[:, k, a:b], start=(k == 0), stop=(k == KC - 1))
                            mm.then_inc(s["gu"], 1)
                        for m in range(KC):
                            if m == 0:
                                pe.wait_ge(s["prod"], (e * FC + FC) * 2)
                            pe.wait_ge(s[f"d{m % 4}"], 32 * e + 16 * (m // 4) + 16)
                            if m >= 4:
                                pe.wait_ge(s["added"], e * (2 * KC) + (m - 3) * 2)
                            for j in range(FC):
                                for q, (a, b) in enumerate(STREAMS):
                                    mm = pe.matmul(ps[:, 2 * (m % 4) + q, 0:b - a], wd[:, m % 4, j, :],
                                                   act_t[:, j, a:b], start=(j == 0), stop=(j == FC - 1))
                            mm.then_inc(s["dn"], 1)
                    if gT is None:
                        body(0, True)
                        with pe.Fori(1, n_exp) as e:
                            body(e, False)
                    else:
                        for e in range(n_exp):
                            self.e_static = e
                            body(e, e == 0)

                @block.scalar
                def _(act):
                    def body(e):
                        for j in range(FC):
                            act.wait_ge(s["gu"], e * FC + j + 1)
                            if j == 0:
                                act.wait_ge(s["dn"], e * KC + 0) if not isinstance(e, int) or e else None
                            for q, (a, b) in enumerate(STREAMS):
                                act.activation(act_t[:, j, a:b], ps[:, 4 * (j % 2) + q, 0:b - a], ACT.Silu).then_inc(s["silu"], 1)
                    body(0)
                    with act.Fori(1, n_exp) as e:
                        body(e)

                @block.vector
                def _(dve):
                    def body(e):
                        if gT is not None:
                            dve.wait_ge(s["gb"], e + 1)
                            for q, (a, b) in enumerate(STREAMS):
                                dve.tensor_copy(gb[:, a:b], ps[:, q, 0:b - a]).then_inc(s["gbo"], 1)
                            dve.wait_ge(s["gbo"], 2 * e + 2)
                        for j in range(FC):
                            for q, (a, b) in enumerate(STREAMS):
                                dve.wait_ge(s["silu"], (e * FC + j) * 2 + q + 1)
                                y = act_t[:, j, a:b]
                                ins = dve.tensor_tensor(y, y, ps[:, 4 * (j % 2) + 2 + q, 0:b - a], ALU.mult)
                                if gT is not None:
                                    ins.then_inc(s["chain"], 1)
                                    dve.wait_ge(s["chain"], (e * FC + j) * 2 + q + 1)
                                    ins = dve.tensor_tensor(y, y, gb[:, a:b], ALU.mult)
                                ins.then_inc(s["prod"], 1)
                        for m in range(KC):
                            dve.wait_ge(s["dn"], e * KC + m + 1)
                            for q, (a, b) in enumerate(STREAMS):
                                x = self.xT[:, m, a:b]
                                dve.scalar_tensor_tensor(out=x, in0=ps[:, 2 * (m % 4) + q, 0:b - a], scalar=self.mod[:, l, 5, m, q:q + 1],
                                                         in1=x, op0=ALU.mult, op1=ALU.add).then_inc(s["added"], 1)
                        dve.wait_ge(s["added"], e * (2 * KC) + 2 * KC)
                    body(0)
                    with dve.Fori(1, n_exp) as e:
                        body(e)

    def store(self):
        nc, ps = self.nc, self.ps
        with ExitStack() as scope:
            y = scope.enter_context(nc.sbuf_tensor("y_out", [P, NT, D], F32))
            with stage(nc, "turned out_act out_dve stored") as (block, s):
                @block.tensor
                def _(pe):
                    for n in range(2 * NT):
                        t, g = divmod(n, 2)
                        if n >= 8:
                            pe.wait_ge(s["out_dve" if g else "out_act"], t - 3)
                        for c in range(4):
                            mm = pe.transpose(ps[:, n % 8, c * P:(c + 1) * P], self.hT[:, 4 * g + c, t * P:(t + 1) * P], self.ident)
                        mm.then_inc(s["turned"], 1)

                @block.scalar
                def _(act):
                    for t in range(NT):
                        act.wait_ge(s["turned"], 2 * t + 1)
                        act.copy(y[:, t, 0:512], ps[:, (2 * t) % 8, :]).then_inc(s["out_act"], 1)

                @block.vector
                def _(dve):
                    for t in range(NT):
                        dve.wait_ge(s["turned"], 2 * t + 2)
                        dve.tensor_copy(y[:, t, 512:D], ps[:, (2 * t + 1) % 8, :]).then_inc(s["out_dve"], 1)

                @block.sync
                def _(sp):
                    for t in range(NT):
                        sp.wait_ge(s["out_act"], t + 1)
                        sp.wait_ge(s["out_dve"], t + 1)
                        dst = self.o["yp"][0] if t == 0 else self.o["ys"][0, (t - 1) * P:t * P, :]
                        sp.dma_start(dst, y[:, t]).then_inc(s["stored"], 16)
                    sp.wait_ge(s["stored"], 16 * NT)


def build_program(nc, i, o, stop=None):
    with ExitStack() as ctx:
        k = Kernel(nc, i, o, ctx)
        k.prologue()
        for l in range(DEPTH):
            k.norm(lambda c, j: k.amul[:, l, 0, c, j:j + 1], lambda c, j: k.mod[:, l, 0, c, j:j + 1])
            k.mixer(l)
            k.norm(lambda c, j: k.amul[:, l, 1, c, j:j + 1], lambda c, j: k.mod[:, l, 3, c, j:j + 1])
            if l == 0:
                w1 = i["ffn_w_gu"][0].rearrange("(c p) (h e j n) -> p h e j c n", p=P, h=2, e=2, n=P)
                w2 = i["ffn_w_down"][0].rearrange("(e j p) (m n) -> e m p j n", e=2, p=P, n=P)
                k.ffn(l, 2, lambda e, half, j: w1[:, half, e, j], lambda e, m: w2[e, m])
            else:
                w1 = i["moe_w_gu"][0].rearrange("e (c p) (h j n) -> e p h j c n", p=P, h=2, n=P)
                w2 = i["moe_w_down"][0].rearrange("e (j p) (m n) -> e m p j n", p=P, n=P)
                with nc.sbuf_tensor("gate_rows", [NE, T], F32) as gT:
                    k.router(gT)
                    k.ffn(l, NE, lambda e, half, j: w1[e, :, half, j], lambda e, m: w2[e, m], gT)
        k.norm(lambda c, j: k.cols[:, 112 + 32 + c:][:, 0:1], None)
        k.store()


def shape_constants():
    a = np.arange(P)
    r, c = a[:, None], a[None, :]
    t = [r == c, np.ones((P, P)), r <= c, r >= c, r > c, r < c]
    for d in range(2):
        j, i_ = r, c
        for lev in range(NLEV):
            b = 1 << lev
            same = j // (2 * b) == i_ // (2 * b)
            lo, hi = (j, i_) if d == 0 else (i_, j)
            t.append(same & (lo % (2 * b) < b) & (hi % (2 * b) >= b))
    consts = np.stack([np.asarray(x, np.float32) for x in t], axis=1)
    pos = np.arange(4 * P)
    row, col = (pos // 64).astype(np.float32), (pos % 64).astype(np.float32)
    parts = []
    for hd in (HD, DHC):
        nf = hd // 4
        inv = np.float32(10000.0) ** (-np.arange(nf, dtype=np.float32) / np.float32(nf))
        ang = np.stack([row[:, None] * inv, col[:, None] * inv], axis=1)
        cs, sn = np.cos(ang), np.sin(ang)
        parts.append(np.stack([cs, cs], axis=2).reshape(4 * P, hd))
        parts.append(np.stack([-sn, sn], axis=2).reshape(4 * P, hd))
    rope = np.concatenate(parts, axis=1).astype(np.float32).reshape(4, P, 192).transpose(1, 0, 2)
    sel = np.zeros((NE, NE, P), np.float32)
    for e in range(NE):
        sel[e, e] = 1.0
    return {"consts": np.ascontiguousarray(consts), "rope": np.ascontiguousarray(rope),
            "iota": np.arange(NE, dtype=np.float32), "sel": sel}


_INS = ["x_prompt", "x_sample", "state_delta", "cache_gqa_k", "cache_gqa_v", "cache_diff_k", "cache_diff_v", "c",
        "c_ctx", "ada_w", "ada_b", "norm_mix", "norm_ffn", "w_in", "conv_w", "dn_a_log", "dn_dt_bias", "dn_norm",
        "gqa_q_norm", "gqa_k_norm", "diff_lambda", "diff_norm", "w_out", "ffn_w_gu", "ffn_w_down", "moe_router",
        "moe_w_gu", "moe_w_down", "final_norm"]
_OUTS = {"yp": (1, P, D), "ys": (1, 4 * P, D), "state": (1, DEPTH, 2, HA, HD, HD), "gk": (1, DEPTH, P, KVB, HD),
         "gv": (1, DEPTH, P, KVB, HD), "dk": (1, DEPTH, P, HC, 2, DHC), "dv": (1, DEPTH, P, HC, HD)}


def kernel(**inputs):
    import concourse.bacc as bacc
    from concourse.bass_utils import run_bass_kernel_spmd

    nc = bacc.Bacc("TRN2", target_bir_lowering=False, num_devices=1)
    arrays, ins, outs = {}, {}, {}
    given = {n: np.ascontiguousarray(inputs[n]) for n in _INS}
    given.update(shape_constants())
    for name, a in given.items():
        arrays[f"in_{name}"] = a
        ins[name] = nc.dram_tensor(f"in_{name}", a.shape, mybir.dt.from_np(a.dtype), kind="ExternalInput").ap()
    for name, shape in _OUTS.items():
        outs[name] = nc.dram_tensor(f"out_{name}", shape, F32, kind="ExternalOutput").ap()
    build_program(nc, ins, outs)
    r = run_bass_kernel_spmd(nc, [arrays], core_ids=[0])
    return tuple(r.results[0][f"out_{name}"] for name in _OUTS)
```

```python
import math
from contextlib import ExitStack, contextmanager

import numpy as np

import concourse.bass as bass
from concourse import mybir

F32 = mybir.dt.float32
I32 = mybir.dt.int32
U32 = mybir.dt.uint32
F32R = mybir.dt.float32r
ACT = mybir.ActivationFunctionType
ALU = mybir.AluOpType
AX = mybir.AxisListType

P = 128
D = 1024
KC = D // P
T = 640
NT = T // P
DEPTH = 2
HD = 64
HA = 6
AW = HA * HD
FM = 3 * AW
IN_COLS = 2968
TM = IN_COLS - FM
Z0, BE0, AR0, QB0, KB0, VB0, QC0, KCC0, VC0 = 0, 384, 396, 408, 792, 920, 1048, 1304, 1560
TMT = TM // 4
PAST = 256
HB, KVB = 6, 2
HC, DHC = 4, 32
DFF = 1408
FC = DFF // P
NE = 8
BLK = 256
RMAX = 2 * T // BLK + NE - 1
EPS = 1e-6
STREAMS = ((0, P), (P, T))
NLEV = 7
C_ID, C_ONE, C_U, C_SL, C_LV = 0, 1, 2, 4, 6
NCONST = C_LV + 2 * NLEV
KEYS = P + PAST + 4 * P


class Chain:

    def __init__(self, eng, sem):
        self.eng, self.sem, self.n = eng, sem, 0

    def __call__(self, ins, wait=True):
        self.n += 1
        ins.then_inc(self.sem, 1)
        if wait:
            self.eng.wait_ge(self.sem, self.n)


@contextmanager
def stage(nc, names):
    at = nc.next_id()
    sems = {n: nc.alloc_semaphore(f"{n}_{at}") for n in names.split()}
    with nc.Block() as block:
        yield block, sems
    nc.clear_and_free_semaphores(list(sems.values()))
    nc.all_engine_barrier()


def bcast_mid(ap, n):
    return ap.unsqueeze(1).to_broadcast([ap.shape[0], n, ap.shape[1]])


def bcast_last(ap, n):
    return ap.unsqueeze(2).to_broadcast([ap.shape[0], ap.shape[1], n])


class Kernel:
    def __init__(self, nc, i, o, ctx):
        self.nc, self.i, self.o = nc, i, o

        def sb(name, shape, dt=F32):
            return ctx.enter_context(nc.sbuf_tensor(name, shape, dt))

        self.ps = ctx.enter_context(nc.psum_tensor("ps", [P, 8, 512], F32))
        self.xT = sb("xT", [P, KC, T])
        self.hT = sb("hT", [P, KC, T])
        self.cst = sb("cst", [P, NCONST, P])
        self.cols = sb("cols", [P, 112 + 94])
        self.condT = sb("condT", [P, KC, 2])
        self.mod = sb("mod", [P, DEPTH, 6, KC, 2])
        self.amul = sb("amul", [P, DEPTH, 2, KC, 2])
        self.slots_h = nc.dram_tensor("slots_h", [(RMAX + 1) * BLK, D], F32).ap()
        self.slots_y = nc.dram_tensor("slots_y", [RMAX * BLK, D], F32).ap()
        self.ident = self.cst[:, C_ID, :]
        self.ones = self.cst[:, C_ONE, :]

    def c(self, n):
        return self.cst[:, n, :]

    def prologue(self):
        nc, i, ps = self.nc, self.i, self.ps
        NW = 24
        SL = 4
        with ExitStack() as scope:
            def sb(name, shape, dt=F32):
                return scope.enter_context(nc.sbuf_tensor(name, shape, dt))
            xin = sb("xin", [P, NT, D])
            rows = sb("rows", [P, 2, P])
            wr = sb("ada_ring", [P, SL, KC, 512])
            modr = sb("mod_row", [2, 2, 512])
            names = "mod_row mod_col consts_in x_in rows_in row_turned cols_out cond x_turned x_out mod_mm mod_out chain " + \
                " ".join(f"w_in{s}" for s in range(SL))
            with stage(nc, names) as (block, s):
                @block.sync
                def _(sp):
                    sp.dma_start(self.cst[:], i["consts"]).then_inc(s["consts_in"], 16)
                    for r0, n, src, half in (
                            (0, 96, i["ada_b"].rearrange("l (c p) -> (l c) p", p=P), 0),
                            (96, 8, i["c_ctx"].rearrange("(c p) -> c p", p=P), 0),
                            (104, 8, i["c"].rearrange("b (c p) -> (b c) p", p=P), 0),
                            (0, 16, i["norm_mix"].rearrange("l (c p) -> (l c) p", p=P), 1),
                            (16, 16, i["norm_ffn"].rearrange("l (c p) -> (l c) p", p=P), 1),
                            (32, 8, i["final_norm"].rearrange("(c p) -> c p", p=P), 1),
                            (40, 54, i["conv_w"].rearrange("l w (c p) -> (l w c) p", p=P), 1)):
                        sp.dma_start(rows[r0:r0 + n, half, :], src).then_inc(s["rows_in"], 16)
                    sp.dma_start(xin[:, 0, :], i["x_prompt"][0]).then_inc(s["x_in"], 16)
                    sp.dma_start(xin[:, 1:NT, :], i["x_sample"][0].rearrange("(t p) d -> p t d", p=P)
                                 ).then_inc(s["x_in"], 16)
                    for n in range(NW):
                        if n >= SL:
                            sp.wait_ge(s["mod_mm"], n - SL + 1)
                        l, j = divmod(n, 12)
                        sp.dma_start(wr[:, n % SL], i["ada_w"][l].rearrange("(c p) n -> p c n", p=P)
                                     [:, :, j * 512:(j + 1) * 512]).then_inc(s[f"w_in{n % SL}"], 16)

                @block.tensor
                def _(pe):
                    pe.wait_ge(s["consts_in"], 16)
                    pe.wait_ge(s["rows_in"], 7 * 16)
                    for half, n in ((0, 112), (1, 94)):
                        pe.transpose(ps[:, half, 0:n], rows[0:n, half, :], self.ident[0:n, 0:n]
                                     ).then_inc(s["row_turned"], 1)
                    pe.wait_ge(s["x_in"], 32)
                    for t in range(NT):
                        for g in range(2):
                            n = 2 * t + g
                            if n >= 4:
                                pe.wait_ge(s["x_out"], n - 3)
                            for c in range(4):
                                mm = pe.transpose(ps[:, 2 + n % 4, c * P:(c + 1) * P],
                                                  xin[:, t, (4 * g + c) * P:(4 * g + c + 1) * P], self.ident)
                            mm.then_inc(s["x_turned"], 1)
                    pe.wait_ge(s["cond"], 1)
                    for n in range(NW + 1):
                        if n < NW:
                            pe.wait_ge(s[f"w_in{n % SL}"], 16 * (n // SL + 1))
                            if n >= 2:
                                pe.wait_ge(s["mod_row"], n - 1)
                            for k in range(KC):
                                mm = pe.matmul(ps[0:2, n % 2, :], self.condT[:, k, :], wr[:, n % SL, k, :],
                                               start=(k == 0), stop=(k == KC - 1))
                            mm.then_inc(s["mod_mm"], 1)
                        if n:
                            pe.wait_ge(s["mod_row"], n)
                            for m in range(4):
                                o = (4 * (n - 1) + m) * 2
                                mm = pe.transpose(ps[:, 6, o:o + 2], modr[:, (n - 1) % 2, m * P:(m + 1) * P], self.ident[0:2, 0:2])
                            mm.then_inc(s["mod_col"], 1)

                @block.scalar
                def _(act):
                    act.wait_ge(s["cols_out"], 2)
                    act.activation(self.condT[:].rearrange("p k s -> p s k"),
                                   self.cols[:, 96:112].rearrange("p (s k) -> p s k", s=2),
                                   ACT.Silu).then_inc(s["cond"], 1)
                    for n in range(NW):
                        act.wait_ge(s["mod_mm"], n + 1)
                        if n >= 2:
                            act.wait_ge(s["mod_col"], n - 1)
                        act.copy(modr[:, n % 2, :], ps[0:2, n % 2, :]).then_inc(s["mod_row"], 1)

                @block.vector
                def _(dve):
                    chain = Chain(dve, s["chain"])
                    dve.wait_ge(s["row_turned"], 2)
                    dve.tensor_copy(self.cols[:, 0:112], ps[:, 0, 0:112]).then_inc(s["cols_out"], 1)
                    dve.tensor_copy(self.cols[:, 112:206], ps[:, 1, 0:94]).then_inc(s["cols_out"], 1)
                    for t in range(NT):
                        for g in range(2):
                            n = 2 * t + g
                            dve.wait_ge(s["x_turned"], n + 1)
                            dve.tensor_copy(self.xT[:, 4 * g:4 * g + 4, t * P:(t + 1) * P],
                                            ps[:, 2 + n % 4, :].rearrange("p (c t) -> p c t", c=4)
                                            ).then_inc(s["x_out"], 1)
                    dve.wait_ge(s["mod_col"], NW)
                    dve.wait_ge(s["cols_out"], 2)
                    chain(dve.tensor_tensor(self.mod[:].rearrange("p l m k s -> p (l m k) s"),
                                            ps[:, 6, 0:192].rearrange("p (a s) -> p a s", s=2),
                                            bcast_last(self.cols[:, 0:96], 2), ALU.add))
                    for l in range(DEPTH):
                        for w in range(2):
                            g0 = 112 + 16 * w + 8 * l
                            dve.scalar_tensor_tensor(
                                out=self.amul[:, l, w], in0=self.mod[:, l, 3 * w + 1], scalar=1.0,
                                in1=bcast_last(self.cols[:, g0:g0 + 8], 2), op0=ALU.add, op1=ALU.mult
                            ).then_inc(s["mod_out"], 1)

    def norm(self, mul, add):
        nc, ps, xT, hT = self.nc, self.ps, self.xT, self.hT
        with ExitStack() as scope:
            sq = scope.enter_context(nc.sbuf_tensor(f"sq_{nc.next_id()}", [P, KC, T], F32))
            rstd = scope.enter_context(nc.sbuf_tensor(f"rstd_{nc.next_id()}", [P, T], F32))
            with stage(nc, "squared summed ms root rstd scaled moved") as (block, s):
                @block.scalar
                def _(act):
                    for k in range(0, KC, 2):
                        act.activation(sq[:, k], xT[:, k], ACT.Square).then_inc(s["squared"], 1)
                    act.wait_ge(s["ms"], 2)
                    act.activation(rstd[:], rstd[:], ACT.Sqrt).then_inc(s["root"], 1)
                    for k in range(KC):
                        act.wait_ge(s["scaled"], KC + k + 1)
                        for j, (a, b) in enumerate(STREAMS):
                            act.activation(hT[:, k, a:b], sq[:, k, a:b], ACT.Identity, scale=mul(k, j),
                                           bias=add(k, j) if add else 0.0).then_inc(s["moved"], 1)

                @block.vector
                def _(dve):
                    for k in range(1, KC, 2):
                        dve.tensor_tensor(sq[:, k], xT[:, k], xT[:, k], ALU.mult).then_inc(s["scaled"], 1)
                    dve.wait_ge(s["summed"], 1)
                    for j, (a, b) in enumerate(STREAMS):
                        dve.tensor_scalar(rstd[:, a:b], ps[:, j, 0:b - a], 1.0 / D, EPS, ALU.mult, ALU.add
                                          ).then_inc(s["ms"], 1)
                    dve.wait_ge(s["root"], 1)
                    dve.reciprocal(rstd[:], rstd[:]).then_inc(s["rstd"], 1)
                    dve.wait_ge(s["rstd"], 1)
                    for k in range(KC // 2, KC):
                        dve.nop().then_inc(s["scaled"], 1)
                    for k in range(KC):
                        dve.tensor_tensor(sq[:, k], xT[:, k], rstd[:], ALU.mult).then_inc(s["scaled"], 1)

                @block.tensor
                def _(pe):
                    for k in range(KC):
                        if k % 2:
                            pe.wait_ge(s["scaled"], k // 2 + 1)
                        else:
                            pe.wait_ge(s["squared"], k // 2 + 1)
                        for j, (a, b) in enumerate(STREAMS):
                            mm = pe.matmul(ps[:, j, 0:b - a], self.ones, sq[:, k, a:b],
                                           start=(k == 0), stop=(k == KC - 1))
                    mm.then_inc(s["summed"], 1)

    def mixer(self, l):
        nc, i, ps = self.nc, self.i, self.ps
        with ExitStack() as scope:
            def sb(name, shape, dt=F32):
                return scope.enter_context(nc.sbuf_tensor(f"{name}_{l}", shape, dt))
            self.tm = sb("tm", [P, NT, TM])
            self.oA = sb("oA", [P, NT, AW])
            self.bg = sb("bg", [P, 2, NT, 2, HA])
            with ExitStack() as s2:
                self.qkv = s2.enter_context(nc.sbuf_tensor(f"qkv_{l}", [P, NT, 18, HD], F32))
                spare = self.hT[:].rearrange("p c t -> p (c t)")
                self.kqT = spare[:, 0:NT * 6 * P].rearrange("p (t h j n) -> p t h j n", t=NT, h=3, j=2)
                self.mt1 = spare[:, NT * 6 * P:(NT + 1) * 6 * P].rearrange("p (h n) -> p h n", h=HA)
                self.eg = s2.enter_context(nc.sbuf_tensor(f"eg_{l}", [P, 3, 2, NT, HA], F32))
                self.glp = s2.enter_context(nc.sbuf_tensor(f"glp_{l}", [P, 2, NT, 3], F32))
                self.in_proj(l)
                self.delta_prep(l)
                self.delta_scan(l)
            self.mixed = sb("mixed", [P, NT, D])
            self.attn_prep_and_attend(l)
            self.out_proj(l)

    def in_proj(self, l):
        nc, i, ps, tm = self.nc, self.i, self.ps, self.tm
        w = i["w_in"][l].rearrange("(c p) n -> p c n", p=P)
        SL = 3
        tiles = [("fm", n * 384, 384) for n in range(3)] + [("tm", FM + n * TMT, TMT) for n in range(4)]
        PADW = T + 4
        at = (1, 131)
        with ExitStack() as scope:
            def sb(name, shape, dt=F32):
                return scope.enter_context(nc.sbuf_tensor(f"{name}_{l}", shape, dt))
            ring = sb("w_ring", [P, SL, KC * TMT])
            pad = sb("conv_in", [P, 9, PADW])
            conv = sb("conv_out", [P, 2, PADW - 2])
            names = "fm_mm tm_mm fm_act fm_dve tm_out padded chain conv conv_used silu turned qkv_out " + \
                " ".join(f"w_in{s}" for s in range(SL))
            with stage(nc, names) as (block, s):
                def view(n):
                    return ring[:, n % SL, 0:KC * tiles[n][2]].rearrange("p (c n) -> p c n", c=KC)

                @block.sync
                def _(sp):
                    for n, (kind, c0, width) in enumerate(tiles):
                        m = n - SL
                        if m >= 0:
                            if m < 3:
                                sp.wait_ge(s["fm_mm"], 3 * (m + 1))
                            else:
                                sp.wait_ge(s["tm_mm"], NT * (m - 2))
                        sp.dma_start(view(n), w[:, :, c0:c0 + width]).then_inc(s[f"w_in{n % SL}"], 16)

                @block.gpsimd
                def _(pool):
                    pool.memset(pad[:, :, 0:1], 0.0).then_inc(s["padded"], 1)
                    pool.memset(pad[:, :, 129:131], 0.0).then_inc(s["padded"], 1)
                    pool.memset(pad[:, :, PADW - 1:PADW], 0.0).then_inc(s["padded"], 1)

                @block.tensor
                def _(pe):
                    for n in range(3):
                        pe.wait_ge(s[f"w_in{n % SL}"], 16 * (n // SL + 1))
                        for m in range(3):
                            c = 3 * n + m
                            if c >= 4:
                                pe.wait_ge(s["fm_act"], c - 3)
                                pe.wait_ge(s["fm_dve"], c - 3)
                            for k in range(KC):
                                for j, (a, b) in enumerate(STREAMS):
                                    mm = pe.matmul(ps[:, 2 * (c % 4) + j, 0:b - a], view(n)[:, k, m * P:(m + 1) * P],
                                                   self.hT[:, k, a:b], start=(k == 0), stop=(k == KC - 1))
                            mm.then_inc(s["fm_mm"], 1)
                    pe.wait_ge(s["fm_act"], 9)
                    pe.wait_ge(s["fm_dve"], 9)
                    for n in range(3, 7):
                        pe.wait_ge(s[f"w_in{n % SL}"], 16 * (n // SL + 1))
                        for t in range(NT):
                            q = NT * (n - 3) + t
                            if q >= 4:
                                pe.wait_ge(s["tm_out"], q - 3)
                            for k in range(KC):
                                mm = pe.matmul(ps[:, q % 4, 0:TMT], self.hT[:, k, t * P:(t + 1) * P],
                                               view(n)[:, k, :], start=(k == 0), stop=(k == KC - 1))
                            mm.then_inc(s["tm_mm"], 1)
                            if n >= 4 and q - NT < 9:
                                c = q - NT
                                pe.wait_ge(s["silu"], c + 1)
                                if c >= 2:
                                    pe.wait_ge(s["qkv_out"], c - 1)
                                for u in range(NT):
                                    x0 = 0 if u == 0 else 130 + (u - 1) * P
                                    b0 = 4 + 2 * (c % 2)
                                    mm = pe.transpose(ps[:, b0 + u // 4, (u % 4) * P:(u % 4 + 1) * P],
                                                      conv[:, c % 2, x0:x0 + P], self.ident)
                                mm.then_inc(s["turned"], 1)

                @block.scalar
                def _(act):
                    for c in range(9):
                        act.wait_ge(s["fm_mm"], c + 1)
                        act.copy(pad[:, c, at[0]:at[0] + P], ps[:, 2 * (c % 4), 0:P]).then_inc(s["fm_act"], 1)
                    for q in range(20):
                        act.wait_ge(s["tm_mm"], q + 1)
                        n, t = divmod(q, NT)
                        act.copy(tm[:, t, n * TMT:(n + 1) * TMT], ps[:, q % 4, 0:TMT]).then_inc(s["tm_out"], 1)
                        c = q - NT + 1
                        if 0 <= c < 9:
                            act.wait_ge(s["conv"], c + 1)
                            act.activation(conv[:, c % 2, :], conv[:, c % 2, :], ACT.Silu).then_inc(s["silu"], 1)

                @block.vector
                def _(dve):
                    chain = Chain(dve, s["chain"])
                    for c in range(9):
                        dve.wait_ge(s["fm_mm"], c + 1)
                        dve.tensor_copy(pad[:, c, at[1]:at[1] + 4 * P], ps[:, 2 * (c % 4) + 1, :]
                                        ).then_inc(s["fm_dve"], 1)
                    dve.wait_ge(s["padded"], 3)
                    dve.wait_ge(s["fm_act"], 9)
                    dve.wait_ge(s["fm_dve"], 9)

                    def convolve(c):
                        tap = [self.cols[:, 112 + 40 + (l * 3 + u) * 9 + c:][:, 0:1] for u in range(3)]
                        y = conv[:, c % 2, :]
                        if c >= 2:
                            dve.wait_ge(s["turned"], c - 1)
                        chain(dve.tensor_scalar(y, pad[:, c, 0:PADW - 2], tap[0], None, ALU.mult))
                        chain(dve.scalar_tensor_tensor(out=y, in0=pad[:, c, 1:PADW - 1], scalar=tap[1], in1=y,
                                                       op0=ALU.mult, op1=ALU.add))
                        dve.scalar_tensor_tensor(out=y, in0=pad[:, c, 2:PADW], scalar=tap[2], in1=y,
                                                 op0=ALU.mult, op1=ALU.add).then_inc(s["conv"], 1)
                    convolve(0)
                    convolve(1)
                    for c in range(9):
                        dve.wait_ge(s["turned"], c + 1)
                        b0 = 4 + 2 * (c % 2)
                        dve.tensor_copy(self.qkv[:, 0:NT, 2 * c:2 * c + 2, :].rearrange("p t h d -> p t (h d)"),
                                        ps[:, b0:b0 + 2, :].rearrange("p b (t d) -> p (b t) d", t=4)[:, 0:NT, :]
                                        ).then_inc(s["qkv_out"], 1)
                        if c + 2 < 9:
                            convolve(c + 2)

    def delta_prep(self, l):
        nc, i, ps, tm, qkv, bg = self.nc, self.i, self.ps, self.tm, self.qkv, self.bg
        with ExitStack() as scope:
            def sb(name, shape, dt=F32):
                return scope.enter_context(nc.sbuf_tensor(f"{name}_{l}", shape, dt))
            sq = sb("qk_sq", [P, NT, 12, HD])
            r = sb("qk_r", [P, NT, 12])
            ab = sb("a_log_dt", [P, 2, 2, HA])
            e1 = sb("e1", [P, NT, 2, HA])
            e2 = sb("e2", [P, NT, 2, HA])
            na = sb("na", [P, 12])
            with stage(nc, "par_in chain expd lnd neg g_done rooted qk_done turned kq_out cum eg_out half") as (block, s):
                @block.sync
                def _(sp):
                    for j, name in enumerate(("dn_a_log", "dn_dt_bias")):
                        sp.dma_start(ab[:, j], i[name][l].partition_broadcast(P)).then_inc(s["par_in"], 16)

                braw = tm[:, :, BE0:BE0 + 12]
                araw = tm[:, :, AR0:AR0 + 12]
                e1f = e1[:].rearrange("p t d h -> p t (d h)")
                e2f = e2[:].rearrange("p t d h -> p t (d h)")
                beta = bg[:, 0].rearrange("p t d h -> p t (d h)")
                g = bg[:, 1].rearrange("p t d h -> p t (d h)")
                abf = ab[:].rearrange("p j d h -> p j (d h)")

                @block.vector
                def _(dve):
                    chain = Chain(dve, s["chain"])
                    dve.wait_ge(s["par_in"], 32)
                    chain(dve.tensor_tensor(g, araw, bcast_mid(abf[:, 1], NT), ALU.add))
                    chain(dve.tensor_scalar(e2f, g, -1.0, None, ALU.mult))
                    dve.tensor_tensor(e2f, e2f, g, ALU.min).then_inc(s["neg"], 1)
                    dve.wait_ge(s["neg"], 1)
                    chain(dve.tensor_scalar(g, g, 0.0, None, ALU.max))
                    dve.wait_ge(s["expd"], 3)
                    chain(dve.tensor_scalar(e1f, e1f, 1.0, None, ALU.add))
                    chain(dve.reciprocal(beta, e1f))
                    dve.tensor_scalar(e2f, e2f, 1.0, None, ALU.add).then_inc(s["neg"], 1)
                    chain(dve.tensor_scalar(na[:], na[:], -1.0, None, ALU.mult))
                    dve.wait_ge(s["lnd"], 1)
                    chain(dve.tensor_tensor(g, g, e2f, ALU.add))
                    dve.tensor_tensor(g, g, bcast_mid(na[:], NT), ALU.mult).then_inc(s["g_done"], 1)
                    chain(dve.tensor_tensor(sq[:], qkv[:, :, 0:12, :], qkv[:, :, 0:12, :], ALU.mult))
                    chain(dve.tensor_reduce(r[:], sq[:], AX.X, ALU.add))
                    dve.tensor_scalar(r[:], r[:], EPS, None, ALU.add).then_inc(s["neg"], 1)
                    dve.wait_ge(s["rooted"], 1)
                    chain(dve.reciprocal(r[:], r[:]))
                    chain(dve.tensor_scalar(r[:, :, 0:HA], r[:, :, 0:HA], HD ** -0.5, None, ALU.mult))
                    for t in range(NT):
                        dve.tensor_tensor(qkv[:, t, 0:12, :], qkv[:, t, 0:12, :], bcast_last(r[:, t, :], HD),
                                          ALU.mult).then_inc(s["qk_done"], 1)
                    for t in range(NT):
                        dve.wait_ge(s["turned"], t + 1)
                        b0 = 2 * (t % 2)
                        dve.tensor_copy(self.kqT[:, t].rearrange("p h j n -> p (h j) n"),
                                        ps[:, b0:b0 + 2, :].rearrange("p b (t d) -> p (b t) d", t=4)[:, 0:6, :]
                                        ).then_inc(s["kq_out"], 1)
                    dve.wait_ge(s["eg_out"], 1)
                    for j in range(2):
                        dve.tensor_copy(self.glp[64 * j:64 * j + 64].rearrange("p d t h -> p (d t) h"),
                                        self.eg[64 * j:64 * j + 64, 2].rearrange("p d t (h j) -> p (d t) h j", j=2)
                                        [:, :, :, j]).then_inc(s["half"], 1)

                @block.scalar
                def _(act):
                    act.wait_ge(s["par_in"], 32)
                    act.activation(e1f, braw, ACT.Exp, scale=-1.0).then_inc(s["expd"], 1)
                    act.activation(na[:], abf[:, 0], ACT.Exp).then_inc(s["expd"], 1)
                    act.wait_ge(s["neg"], 1)
                    act.activation(e2f, e2f, ACT.Exp).then_inc(s["expd"], 1)
                    act.wait_ge(s["neg"], 2)
                    act.activation(e2f, e2f, ACT.Ln).then_inc(s["lnd"], 1)
                    act.wait_ge(s["cum"], 1)
                    act.activation(self.eg[:].rearrange("p k d t h -> p (k d t h)"), ps[:, 4, 0:180], ACT.Exp
                                   ).then_inc(s["eg_out"], 1)
                    act.wait_ge(s["neg"], 3)
                    act.activation(r[:], r[:], ACT.Sqrt).then_inc(s["rooted"], 1)

                @block.tensor
                def _(pe):
                    pe.wait_ge(s["g_done"], 1)
                    for k, table in enumerate((C_U, C_SL, None)):
                        for d in range(2):
                            o = (2 * k + d) * NT * HA
                            lhsT = self.ones if table is None else self.c(table + d)
                            mm = pe.matmul(ps[:, 4, o:o + NT * HA], lhsT, bg[:, 1, :, d, :], start=True, stop=True)
                    mm.then_inc(s["cum"], 1)
                    for t in range(NT):
                        pe.wait_ge(s["qk_done"], t + 1)
                        if t >= 2:
                            pe.wait_ge(s["kq_out"], t - 1)
                        for pr in range(3):
                            for j, h0 in enumerate((HA, 0)):
                                n = 2 * pr + j
                                mm = pe.transpose(ps[:, 2 * (t % 2) + n // 4, (n % 4) * P:(n % 4 + 1) * P],
                                                  qkv[:, t, h0 + 2 * pr:h0 + 2 * pr + 2, :], self.ident)
                        mm.then_inc(s["turned"], 1)

    def delta_scan(self, l):
        nc, i, ps, qkv, bg = self.nc, self.i, self.ps, self.qkv, self.bg
        kqT, eg = self.kqT, self.eg
        W = HA * P
        with ExitStack() as scope:
            def sb(name, shape, dt=F32):
                return scope.enter_context(nc.sbuf_tensor(f"{name}_{l}", shape, dt))
            XT = sb("XT", [P, NT, 2, HA, P])
            AT = sb("AT", [P, NT, 2, HA, P])
            with ExitStack() as inner:
                def sbi(name, shape, dt=F32):
                    return inner.enter_context(nc.sbuf_tensor(f"{name}_{l}", shape, dt))
                KQ = sbi("KQ", [P, HA, 2, P])
                MT = [sbi("MT", [P, HA, P])[:], self.mt1]
                DT = sbi("DT", [P, 2, HA, P])
                Y = sbi("Y", [P, 2, HA, P])
                X = sbi("X", [P, 2, HA, P])
                L = NLEV - 1
                with stage(nc, "gu dm dexp kq kq_out dmask mt xt0 ms y y_out p xt xturn x_out chain pchain") as (block, s):
                    def two(d, which):
                        return ps[:, 4 * d + 2 * which:4 * d + 2 * which + 2, :].rearrange("p b n -> p (b n)")[:, 0:W]

                    def head(ap, h):
                        return ap[:, h * P:(h + 1) * P]

                    def flat(ap):
                        return ap.rearrange("p h n -> p (h n)")

                    @block.tensor
                    def _(pe):
                        for t in range(NT):
                            for d in range(2):
                                pe.wait_ge(s["gu"], 2 * t + d + 1)
                                if t >= 1:
                                    pe.wait_ge(s["xt"], 2 * (t * L - 1) + d + 1)
                                    pe.wait_ge(s["x_out"], 2 * (t * L - 1) + d + 1)
                                for b, (c0, c1) in enumerate(((0, 512), (512, W))):
                                    mm = pe.matmul(two(d, 0)[:, c0:c1], self.c(C_SL + d), flat(Y[:, d])[:, c0:c1],
                                                   start=True, stop=True)
                                mm.then_inc(s["dm"], 1)
                            for h in range(HA):
                                q = 64 * (h % 2)
                                mm = pe.matmul(ps[:, 2 + 4 * (h % 2) + h // 4, (h // 2 % 2) * 256:(h // 2 % 2) * 256 + 256],
                                               kqT[q:q + 64, t, h // 2, 0, :], kqT[q:q + 64, t, h // 2, :, :],
                                               start=True, stop=True)
                            mm.then_inc(s["kq"], 1)
                            for lev in range(NLEV):
                                n = t * L + lev - 1
                                if lev:
                                    for d in range(2):
                                        pe.wait_ge(s["ms"], 2 * n + d + 1)
                                        pe.wait_ge(s["x_out"], 2 * n + d + 1)
                                        for h in range(HA):
                                            mm = pe.matmul(head(two(d, 1), h), DT[:, d, h], X[:, d, h],
                                                           start=True, stop=True)
                                        mm.then_inc(s["y"], 1)
                                    for d in range(2):
                                        pe.wait_ge(s["y_out"], 2 * n + d + 1)
                                        for h in range(HA):
                                            mm = pe.matmul(head(two(d, 0), h), Y[:, d, h], XT[:, t, d, h],
                                                           start=True, stop=True)
                                        mm.then_inc(s["p"], 1)
                                if lev < NLEV - 1:
                                    for d in range(2):
                                        if lev:
                                            pe.wait_ge(s["xt"], 2 * n + d + 1)
                                        else:
                                            pe.wait_ge(s["xt0"], 2 * t + d + 1)
                                            pe.wait_ge(s["kq_out"], t + 1)
                                            pe.wait_ge(s["pchain"], t + 1)
                                        for h in range(HA):
                                            mm = pe.transpose(head(two(d, 1), h), XT[:, t, d, h], self.ident)
                                        mm.then_inc(s["xturn"], 1)

                    @block.scalar
                    def _(act):
                        for t in range(NT):
                            for d in range(2):
                                act.wait_ge(s["dm"], 2 * t + d + 1)
                                act.activation(flat(DT[:, d]), two(d, 0), ACT.Exp).then_inc(s["dexp"], 1)
                            act.wait_ge(s["kq"], t + 1)
                            for par, done in ((0, "pchain"), (1, "kq_out")):
                                act.copy(KQ[:].rearrange("p (i r) j n -> p r i (j n)", r=2)[:, par],
                                         two(par, 1).rearrange("p (i n) -> p i n", i=3)).then_inc(s[done], 1)
                            for lev in range(NLEV):
                                n = t * L + lev - 1
                                if lev:
                                    for d in range(2):
                                        act.wait_ge(s["y"], 2 * n + d + 1)
                                        act.copy(flat(Y[:, d]), two(d, 1)).then_inc(s["y_out"], 1)
                                if lev < NLEV - 1:
                                    for d in range(2):
                                        act.wait_ge(s["xturn"], 2 * (n + 1) + d + 1)
                                        act.copy(flat(X[:, d]), two(d, 1)).then_inc(s["x_out"], 1)

                    @block.gpsimd
                    def _(pool):
                        for t in range(NT):
                            for lev in range(1, NLEV):
                                n = t * L + lev - 1
                                for d in range(2):
                                    if lev == 1:
                                        pool.wait_ge(s["xt0"], 2 * t + d + 1)
                                    else:
                                        pool.wait_ge(s["y"], 2 * (n - 1) + d + 1)
                                    pool.tensor_tensor(DT[:, d], MT[d], bcast_mid(self.c(C_LV + d * NLEV + lev), HA),
                                                       ALU.mult).then_inc(s["ms"], 1)

                    @block.vector
                    def _(dve):
                        chain = Chain(dve, s["chain"])
                        for t in range(NT):
                            for d in range(2):
                                if t:
                                    dve.wait_ge(s["p"], 2 * (t * L - 1) + d + 1)
                                dve.tensor_tensor(Y[:, d], bcast_mid(self.c(C_U + d), HA),
                                                  bcast_last(bg[:, 1, t, d, :], P), ALU.mult).then_inc(s["gu"], 1)
                            for d in range(2):
                                dve.wait_ge(s["dexp"], 2 * t + d + 1)
                                chain(dve.tensor_tensor(DT[:, d], DT[:, d], bcast_mid(self.c(C_U + d), HA), ALU.mult))
                                dve.wait_ge(s["kq_out"], t + 1)
                                dve.wait_ge(s["pchain"], t + 1)
                                dve.tensor_tensor(AT[:, t, d], KQ[:, :, 1, :], DT[:, d], ALU.mult).then_inc(s["mt"], 1)
                                chain(dve.tensor_tensor(MT[d], KQ[:, :, 0, :], DT[:, d], ALU.mult))
                                chain(dve.tensor_tensor(MT[d], MT[d], bcast_last(bg[:, 0, t, d, :], P), ALU.mult))
                                chain(dve.tensor_tensor(XT[:, t, d], MT[d], bcast_mid(self.c(C_LV + d * NLEV), HA),
                                                        ALU.mult))
                                dve.tensor_tensor(XT[:, t, d], bcast_mid(self.ident, HA), XT[:, t, d], ALU.subtract
                                                  ).then_inc(s["xt0"], 1)
                            for lev in range(1, NLEV):
                                n = t * L + lev - 1
                                for d in range(2):
                                    dve.wait_ge(s["p"], 2 * n + d + 1)
                                    if lev == 1:
                                        dve.wait_ge(s["xt0"], 2 * t + d + 1)
                                    else:
                                        dve.wait_ge(s["xt"], 2 * (n - 1) + d + 1)
                                    dve.tensor_tensor(flat(XT[:, t, d]), flat(XT[:, t, d]), two(d, 0), ALU.subtract
                                                      ).then_inc(s["xt"], 1)
            S = sb("S", [P, 2, 2, 3, HD])
            kd_b = sb("kd", [P, NT, HA, HD])
            kd = [qkv[:, :, 0:HA, :], kd_b[:]]
            tk = sb("tk", [P, 2, HA, HD])
            t1 = sb("t1", [P, 2, HA, HD])
            vn = sb("vn", [P, 2, HA, HD])
            tq = sb("tq", [P, 2, HA, HD])
            o = self.oA
            steps = [(0, 0, 0), (0, 0, 1)]
            for n in range(4):
                steps += [(1, 1 + n, 0), (1, 4 - n, 1)]
            names = "s_in s_zero kd o_zero ks t1 xt1 vn av s_new o_sum s_out chain sdec used"
            with stage(nc, names) as (block, s):
                @block.sync
                def _(sp):
                    for d in range(2):
                        for j in range(2):
                            sp.dma_start(S[64 * j:64 * j + 64, 1, d], i["state_delta"][0, l, d].rearrange(
                                "(h j) k v -> j k h v", j=2)[j]).then_inc(s["s_in"], 16)
                    for d in range(2):
                        sp.wait_ge(s["s_new"], d + 1)
                        for j in range(2):
                            sp.dma_start(self.o["state"][0, l, d].rearrange("(h j) k v -> j k h v", j=2)[j],
                                         S[64 * j:64 * j + 64, 0, d]).then_inc(s["s_out"], 16)
                    sp.wait_ge(s["s_out"], 64)

                @block.gpsimd
                def _(pool):
                    pool.memset(S[:, 0], 0.0).then_inc(s["s_zero"], 1)
                    for n, (st, t, d) in enumerate(steps):
                        pool.tensor_tensor(kd[d][:, t], qkv[:, t, HA:2 * HA, :], bcast_last(eg[:, 1, d, t, :], HD),
                                           ALU.mult).then_inc(s["kd"], 1)

                def bank(n, k, w=HA * HD):
                    return ps[:, 4 * (n % 2) + k, 0:w]

                @block.tensor
                def _(pe):
                    def read_state(n):
                        st, t, d = steps[n]
                        if n == 0:
                            pe.wait_ge(s["s_zero"], 1)
                        elif n == 2:
                            pe.wait_ge(s["s_in"], 64)
                        if n >= 4:
                            pe.wait_ge(s["s_new"], n - 1)
                        if n >= 2:
                            pe.wait_ge(s["o_sum"], n - 1)
                        for j in range(2):
                            for h in range(HA):
                                q = 64 * (h % 2)
                                o0 = (3 * j + h // 2) * HD
                                mm = pe.matmul(bank(n, h % 2)[:, o0:o0 + HD], kqT[q:q + 64, t, h // 2, j, :],
                                               S[q:q + 64, st, d, h // 2, :], start=True, stop=True)
                        mm.then_inc(s["ks"], 1)
                    for n0 in range(0, len(steps), 2):
                        for n in (n0, n0 + 1):
                            read_state(n)
                        for n in (n0, n0 + 1):
                            st, t, d = steps[n]
                            pe.wait_ge(s["t1"], n + 1)
                            for h in range(HA):
                                mm = pe.matmul(bank(n, 2)[:, h * HD:(h + 1) * HD], XT[:, t, d, h], t1[:, d, h],
                                               start=True, stop=True)
                            mm.then_inc(s["xt1"], 1)
                        for n in (n0, n0 + 1):
                            st, t, d = steps[n]
                            pe.wait_ge(s["vn"], n + 1)
                            pe.wait_ge(s["kd"], n + 1)
                            for h in range(HA):
                                q = 64 * (h % 2)
                                mm = pe.matmul(ps[q:q + 64, 4 * (n % 2) + 3, (h // 2) * HD:(h // 2 + 1) * HD],
                                               kd[d][:, t, h], vn[:, d, h], start=True, stop=True)
                            for h in range(HA):
                                mm = pe.matmul(bank(n, 2)[:, h * HD:(h + 1) * HD], AT[:, t, d, h], vn[:, d, h],
                                               start=True, stop=True)
                            mm.then_inc(s["av"], 1)

                @block.vector
                def _(dve):
                    chain = Chain(dve, s["chain"])

                    def v3(ap):
                        return ap.rearrange("p (h d) -> p h d", d=HD)

                    def by_parity(ap):
                        return ap.rearrange("p (i r) d -> p r i d", r=2)

                    def read_out(n, j):
                        b = 4 * (n % 2)
                        return ps[:, b:b + 2, 192 * j:192 * j + 192].rearrange("p r (i d) -> p r i d", d=HD)
                    for n0 in range(0, len(steps), 2):
                        for n in (n0, n0 + 1):
                            st, t, d = steps[n]
                            dve.wait_ge(s["ks"], n + 1)
                            chain(dve.tensor_tensor(by_parity(tk[:, d]), read_out(n, 0),
                                                    by_parity(bcast_last(eg[:, 0, d, t, :], HD)), ALU.mult))
                            dve.tensor_tensor(t1[:, d], qkv[:, t, 2 * HA:3 * HA, :], tk[:, d], ALU.subtract
                                              ).then_inc(s["t1"], 1)
                        for n in (n0, n0 + 1):
                            st, t, d = steps[n]
                            dve.tensor_tensor(by_parity(tq[:, d]), read_out(n, 1),
                                              by_parity(bcast_last(eg[:, 0, d, t, :], HD)), ALU.mult
                                              ).then_inc(s["used"], 1)
                            dve.tensor_tensor(S[:, st, d], S[:, st, d], bcast_last(self.glp[:, d, t, :], HD), ALU.mult
                                              ).then_inc(s["sdec"], 1)
                        for n in (n0, n0 + 1):
                            st, t, d = steps[n]
                            dve.wait_ge(s["xt1"], n + 1)
                            dve.tensor_tensor(vn[:, d], v3(bank(n, 2)), bcast_last(bg[:, 0, t, d, :], HD), ALU.mult
                                              ).then_inc(s["vn"], 1)
                        for n in (n0, n0 + 1):
                            st, t, d = steps[n]
                            dve.wait_ge(s["used"], n + 1)
                            ot = o[:, t, 0:AW]
                            if n < 2:
                                first = d == 0
                            else:
                                first = n0 < 6
                            if not first:
                                chain(dve.tensor_tensor(ot, ot, tq[:, d].rearrange("p h d -> p (h d)"), ALU.add))
                            dve.wait_ge(s["av"], n + 1)
                            dve.wait_ge(s["sdec"], n + 1)
                            dve.tensor_tensor(S[:, st, d], S[:, st, d], v3(bank(n, 3, 192)), ALU.add
                                              ).then_inc(s["s_new"], 1)
                            if first:
                                dve.tensor_tensor(ot, bank(n, 2), tq[:, d].rearrange("p h d -> p (h d)"), ALU.add
                                                  ).then_inc(s["o_sum"], 1)
                            else:
                                dve.tensor_tensor(ot, bank(n, 2), ot, ALU.add).then_inc(s["o_sum"], 1)
                            dve.wait_ge(s["o_sum"], n + 1)
                            dve.wait_ge(s["s_new"], n + 1)

    def attn_prep_and_attend(self, l):
        nc, i, ps, tm, mixed = self.nc, self.i, self.ps, self.tm, self.mixed
        lam_init = 0.8 - 0.6 * math.exp(-0.3 * l)
        with ExitStack() as scope:
            def sb(name, shape, dt=F32):
                return scope.enter_context(nc.sbuf_tensor(f"{name}_{l}", shape, dt))
            kBT = sb("kBT", [P, KEYS])
            qBT = sb("qBT", [P, 3, T])
            kCT = sb("kCT", [P, 2, KEYS])
            qCT = sb("qCT", [P, 2, T])
            vB = sb("vB", [P, 2, KVB * HD])
            vC = sb("vC", [P, 2, HC * HD])
            nlam = sb("nlam", [P, 1])
            gdiff = sb("gdiff", [P, HD])
            with ExitStack() as inner:
                def sbi(name, shape, dt=F32):
                    return inner.enter_context(nc.sbuf_tensor(f"{name}_{l}", shape, dt))
                sq = sbi("n_sq", [P, NT, 8, HD])
                r = sbi("n_r", [P, NT, 8])
                ro = sbi("n_ro", [P, NT, HA])
                gqk = sbi("gqk", [P, 8, HD])
                gdn = sbi("gdn", [P, HD])
                ta = sbi("rope_a", [P, 512])
                tb = sbi("rope_b", [P, 512])
                rope = sbi("rope", [P, 4, 192])
                ckB = sbi("ckB", [P, 2, KVB * HD])
                ckC = sbi("ckC", [P, 2, HC * HD])
                lv = sbi("lv", [P, 4, DHC])
                lp = sbi("lp", [P, 2, DHC])
                ls = sbi("ls", [P, 2])
                names = ("par_in cache_in chain ms root gate silu normed roped cturned c_out turned t_out ctx_out "
                         "lsum lexp lam o_done")
                with stage(nc, names) as (block, s):
                    @block.sync
                    def _(sp):
                        for h in range(HB):
                            sp.dma_start(gqk[:, h], i["gqa_q_norm"][l].partition_broadcast(P)).then_inc(s["par_in"], 16)
                        for h in range(KVB):
                            sp.dma_start(gqk[:, HB + h], i["gqa_k_norm"][l].partition_broadcast(P)).then_inc(s["par_in"], 16)
                        sp.dma_start(gdn[:], i["dn_norm"][l].partition_broadcast(P)).then_inc(s["par_in"], 16)
                        sp.dma_start(gdiff[:], i["diff_norm"][l].partition_broadcast(P)).then_inc(s["par_in"], 16)
                        sp.dma_start(lv[:], i["diff_lambda"][l].partition_broadcast(P)).then_inc(s["par_in"], 16)
                        sp.dma_start(ckB[:], i["cache_gqa_k"][0, l].rearrange("(t p) h d -> p t (h d)", p=P)).then_inc(s["cache_in"], 16)
                        sp.dma_start(ckC[:], i["cache_diff_k"][0, l].rearrange("(t p) h m d -> p t (h m d)", p=P)).then_inc(s["cache_in"], 16)
                        sp.dma_start(vB[:], i["cache_gqa_v"][0, l].rearrange("(t p) h d -> p t (h d)", p=P)).then_inc(s["cache_in"], 16)
                        sp.dma_start(vC[:], i["cache_diff_v"][0, l].rearrange("(t p) h d -> p t (h d)", p=P)).then_inc(s["cache_in"], 16)
                        sp.dma_start(rope[:], i["rope"]).then_inc(s["par_in"], 16)
                        for name, c0, n, pat in (("gv", VB0, KVB * HD, "t h d -> t (h d)"), ("dk", KCC0, HC * HD, "t h m d -> t (h m d)"),
                                                 ("dv", VC0, HC * HD, "t h d -> t (h d)")):
                            sp.dma_start(self.o[name][0, l].rearrange(pat), tm[:, 0, c0:c0 + n]).then_inc(s["ctx_out"], 16)
                        sp.wait_ge(s["normed"], 1)
                        sp.dma_start(self.o["gk"][0, l].rearrange("t h d -> t (h d)"), sq[:, 0, HB:8].rearrange("p h d -> p (h d)")).then_inc(s["ctx_out"], 16)
                        sp.wait_ge(s["ctx_out"], 64)
                        sp.wait_ge(s["cache_in"], 64)

                    qk = tm[:, :, QB0:VB0].rearrange("p t (h d) -> p t h d", d=HD)
                    oA = self.oA[:].rearrange("p t (h d) -> p t h d", d=HD)

                    @block.vector
                    def _(dve):
                        chain = Chain(dve, s["chain"])
                        dve.wait_ge(s["par_in"], 12 * 16)
                        chain(dve.tensor_tensor(sq[:], qk, qk, ALU.mult))
                        chain(dve.tensor_reduce(r[:], sq[:], AX.X, ALU.add))
                        dve.tensor_scalar(r[:], r[:], 1.0 / HD, EPS, ALU.mult, ALU.add).then_inc(s["ms"], 1)
                        dve.wait_ge(s["ms"], 1)
                        chain(dve.tensor_tensor(sq[:, :, 0:HA], oA, oA, ALU.mult))
                        chain(dve.tensor_reduce(ro[:], sq[:, :, 0:HA], AX.X, ALU.add))
                        dve.tensor_scalar(ro[:], ro[:], 1.0 / HD, EPS, ALU.mult, ALU.add).then_inc(s["ms"], 1)
                        for j in range(2):
                            chain(dve.tensor_tensor(lp[:, j], lv[:, 2 * j], lv[:, 2 * j + 1], ALU.mult))
                        dve.tensor_reduce(ls[:], lp[:], AX.X, ALU.add).then_inc(s["lsum"], 1)
                        dve.wait_ge(s["root"], 2)
                        chain(dve.reciprocal(r[:], r[:]))
                        chain(dve.reciprocal(ro[:], ro[:]))
                        for t in range(NT):
                            chain(dve.tensor_tensor(qk[:, t], qk[:, t], bcast_last(r[:, t, :], HD), ALU.mult))
                            chain(dve.tensor_tensor(sq[:, t, 0:HB].rearrange("p (h g) d -> p g h d", g=2),
                                                    qk[:, t, 0:HB].rearrange("p (g h) d -> p g h d", g=2),
                                                    gqk[:, 0:HB].rearrange("p (g h) d -> p g h d", g=2), ALU.mult))
                            dve.tensor_tensor(sq[:, t, HB:8], qk[:, t, HB:8], gqk[:, HB:8], ALU.mult
                                              ).then_inc(s["normed"], 1)
                        for t in range(1, NT):
                            dve.wait_ge(s["normed"], t + 1)
                            for kind, (x0, hd, tab) in enumerate(((QB0, HD, 0), (QC0, DHC, 128))):
                                nh, nf = 512 // hd, hd // 4
                                x = tm[:, t, x0:x0 + 512] if kind else sq[:, t].rearrange("p h d -> p (h d)")
                                cos = rope[:, t - 1, tab:tab + hd]
                                sin = rope[:, t - 1, tab + hd:tab + 2 * hd]

                                def quarters(ap, h):
                                    return ap.rearrange("p (n a h f) -> p n a h f", a=2, h=2, f=nf)[:, :, :, h, :]
                                dve.tensor_tensor(ta[:].rearrange("p (n d) -> p n d", d=hd), x.rearrange("p (n d) -> p n d", d=hd),
                                                  bcast_mid(cos, nh), ALU.mult).then_inc(s["gate"], 1)
                                for half in range(2):
                                    sn = sin.rearrange("p (a h f) -> p a h f", a=2, h=2)[:, :, half, :]
                                    dve.tensor_tensor(quarters(tb[:], half), quarters(x, 1 - half),
                                                      sn.unsqueeze(1).to_broadcast([P, nh, 2, nf]), ALU.mult).then_inc(s["gate"], 1)
                                dve.wait_ge(s["gate"], 6 * (t - 1) + 3 * kind + 3)
                                dve.tensor_tensor(x, ta[:], tb[:], ALU.add).then_inc(s["roped"], 1)
                                dve.wait_ge(s["roped"], 2 * (t - 1) + kind + 1)
                        dve.wait_ge(s["silu"], 1)
                        for t in range(NT):
                            chain(dve.tensor_tensor(oA[:, t], oA[:, t], bcast_last(ro[:, t, :], HD), ALU.mult))
                            chain(dve.tensor_tensor(oA[:, t], oA[:, t], bcast_mid(gdn[:], HA), ALU.mult))
                            chain(dve.tensor_tensor(mixed[:, t, 0:AW], self.oA[:, t], tm[:, t, Z0:Z0 + AW], ALU.mult))
                        dve.wait_ge(s["lexp"], 1)
                        chain(dve.tensor_tensor(nlam[:], ls[:, 1:2], ls[:, 0:1], ALU.subtract))
                        chain(dve.tensor_scalar(nlam[:], nlam[:], -lam_init, None, ALU.add))
                        chain(dve.tensor_scalar(gdiff[:], gdiff[:], 1.0 - lam_init, None, ALU.mult))

                    @block.scalar
                    def _(act):
                        act.wait_ge(s["ms"], 1)
                        act.activation(r[:], r[:], ACT.Sqrt).then_inc(s["root"], 1)
                        act.wait_ge(s["ms"], 2)
                        act.activation(ro[:], ro[:], ACT.Sqrt).then_inc(s["root"], 1)
                        act.wait_ge(s["lsum"], 1)
                        act.activation(ls[:], ls[:], ACT.Exp).then_inc(s["lexp"], 1)
                        act.activation(tm[:, :, Z0:Z0 + AW], tm[:, :, Z0:Z0 + AW], ACT.Silu).then_inc(s["silu"], 1)
                        act.wait_ge(s["cturned"], 1)
                        act.copy(kBT[:, P:P + PAST], ps[:, 0, 0:256]).then_inc(s["c_out"], 1)
                        for c in range(2):
                            act.copy(kCT[:, c, P:P + PAST], ps[:, 1, 256 * c:256 * c + 256]).then_inc(s["c_out"], 1)
                        for t in range(NT):
                            act.wait_ge(s["turned"], t + 1)
                            b = ps[:, 2 + 2 * (t % 2):4 + 2 * (t % 2), :].rearrange("p b (n q) -> p (b n) q", n=4)
                            k0 = 0 if t == 0 else P + PAST + (t - 1) * P
                            act.copy(kBT[:, k0:k0 + P], b[:, 0, :]).then_inc(s["t_out"], 1)
                            act.copy(qBT[:, :, t * P:(t + 1) * P], b[:, 1:4, :]).then_inc(s["t_out"], 1)
                            act.copy(kCT[:, :, k0:k0 + P], b[:, 4:6, :]).then_inc(s["t_out"], 1)
                            act.copy(qCT[:, :, t * P:(t + 1) * P], b[:, 6:8, :]).then_inc(s["t_out"], 1)

                    @block.tensor
                    def _(pe):
                        pe.wait_ge(s["cache_in"], 64)
                        for u in range(2):
                            pe.transpose(ps[:, 0, u * P:(u + 1) * P], ckB[:, u, :], self.ident)
                            for c in range(2):
                                mm = pe.transpose(ps[:, 1, 256 * c + u * P:256 * c + (u + 1) * P],
                                                  ckC[:, u, c * P:(c + 1) * P], self.ident)
                        mm.then_inc(s["cturned"], 1)
                        for t in range(NT):
                            if t == 0:
                                pe.wait_ge(s["normed"], 1)
                            else:
                                pe.wait_ge(s["roped"], 2 * t)
                            if t >= 2:
                                pe.wait_ge(s["t_out"], 4 * (t - 1))
                            b0 = 2 + 2 * (t % 2)
                            src = [sq[:, t, HB:8]] + [sq[:, t, 2 * h:2 * h + 2] for h in range(3)]
                            src += [tm[:, t, KCC0 + c * P:KCC0 + (c + 1) * P] for c in range(2)]
                            src += [tm[:, t, QC0 + c * P:QC0 + (c + 1) * P] for c in range(2)]
                            for n, a in enumerate(src):
                                mm = pe.transpose(ps[:, b0 + n // 4, (n % 4) * P:(n % 4 + 1) * P], a, self.ident)
                            mm.then_inc(s["turned"], 1)

            NP = 4
            pr = sb("probs", [P, NP, 768])
            pT = sb("probsT", [P, 2, 768])
            st = sb("softmax_stats", [P, 2 * NP, 4])
            oC = sb("oC", [P, NT, HC, HD])
            units, maps = [], []
            for t in range(NT):
                for h in range(HB):
                    units.append(("B", t, h, [len(maps)]))
                    maps.append(("B", t, h, 0))
                for h in range(HC):
                    units.append(("C", t, h, [len(maps), len(maps) + 1]))
                    maps += [("C", t, h, 0), ("C", t, h, 1)]

            def nkeys(t):
                return P if t == 0 else PAST + 4 * P

            def keys(t):
                return (0, P) if t == 0 else (P, KEYS)

            def values(t, kt, kind, h):
                c0 = (h // 3) * HD if kind == "B" else h * HD
                base = VB0 if kind == "B" else VC0
                if t == 0:
                    return tm[:, 0, base + c0:base + c0 + HD]
                if kt < 2:
                    return (vB if kind == "B" else vC)[:, kt, c0:c0 + HD]
                return tm[:, kt - 1, base + c0:base + c0 + HD]
            zero = sb("zeros", [P, 2 * D])
            with stage(nc, "scores smax nmax probs a_done pturn p_out pv o_out chain zeroed filled") as (block, s):
                if l == 0:
                    @block.gpsimd
                    def _(pool):
                        pool.memset(zero[:], 0.0).then_inc(s["zeroed"], 1)

                    @block.sync
                    def _(sp):
                        sp.wait_ge(s["zeroed"], 1)
                        n = 0
                        for slots in (self.slots_h, self.slots_y):
                            for r in range(slots.shape[0] // BLK):
                                sp.dma_start(slots[r * BLK:(r + 1) * BLK].rearrange("(p a) d -> p (a d)", a=2), zero[:]
                                             ).then_inc(s["filled"], 16)
                                n += 1
                        sp.wait_ge(s["filled"], 16 * n)

                @block.tensor
                def _(pe):
                    def scores(m):
                        kind, t, h, mp = maps[m]
                        if m >= 2:
                            pe.wait_ge(s["probs"], m - 1)
                        k0, k1 = keys(t)
                        if kind == "B":
                            q = 64 * (h // 3)
                            lhsT, rhs = qBT[q:q + 64, h % 3, t * P:(t + 1) * P], kBT[q:q + 64, k0:k1]
                        else:
                            q = 64 * (h % 2) + 32 * mp
                            lhsT, rhs = qCT[q:q + 32, h // 2, t * P:(t + 1) * P], kCT[q:q + 32, h // 2, k0:k1]
                        for a in range(0, k1 - k0, 512):
                            b = min(a + 512, k1 - k0)
                            mm = pe.matmul(ps[:, 2 * (m % 2) + a // 512, 0:b - a], lhsT, rhs[:, a:b], start=True, stop=True,
                                           **({"tile_position": (q, 0)} if q == 96 else {}))
                        mm.then_inc(s["scores"], 1)

                    def finish(u):
                        kind, t, h, ms = units[u]
                        n = nkeys(t) // P
                        pe.wait_ge(s["a_done"], u + 1)
                        if u >= 1:
                            pe.wait_ge(s["p_out"], u)
                        for kt in range(n):
                            mm = pe.transpose(ps[:, 4 + kt // 4, (kt % 4) * P:(kt % 4 + 1) * P],
                                              pr[:, ms[0] % NP, kt * P:(kt + 1) * P], self.ident)
                        mm.then_inc(s["pturn"], 1)

                    def weigh(u):
                        kind, t, h, ms = units[u]
                        n = nkeys(t) // P
                        pe.wait_ge(s["p_out"], u + 1)
                        if u >= 2:
                            pe.wait_ge(s["o_out"], u - 1)
                        for kt in range(n):
                            mm = pe.matmul(ps[:, 6 + u % 2, 0:HD], pT[:, u % 2, kt * P:(kt + 1) * P], values(t, kt, kind, h),
                                           start=(kt == 0), stop=(kt == n - 1))
                        mm.then_inc(s["pv"], 1)
                    done = 0
                    for u in range(len(units) + 2):
                        if u < len(units):
                            for m in units[u][3]:
                                scores(m)
                        if 1 <= u <= len(units):
                            finish(u - 1)
                        if u >= 2:
                            weigh(u - 2)

                @block.vector
                def _(dve):
                    chain = Chain(dve, s["chain"])

                    def smax(m):
                        kind, t, h, mp = maps[m]
                        n = nkeys(t)
                        scale = HD ** -0.5 if kind == "B" else DHC ** -0.5
                        dve.wait_ge(s["scores"], m + 1)
                        sc = ps[:, 2 * (m % 2):2 * (m % 2) + 2, :].rearrange("p b n -> p (b n)")[:, 0:n]
                        dve.tensor_reduce(st[:, m % 8, 0:1], sc, AX.X, ALU.max).then_inc(s["smax"], 1)
                        dve.wait_ge(s["smax"], m + 1)
                        dve.tensor_scalar(st[:, m % 8, 1:2], st[:, m % 8, 0:1], -scale, None, ALU.mult).then_inc(s["nmax"], 1)

                    def combine(u):
                        kind, t, h, ms = units[u]
                        dve.wait_ge(s["probs"], ms[-1] + 1)
                        for m in ms:
                            chain(dve.reciprocal(st[:, m % 8, 3:4], st[:, m % 8, 2:3]))
                        if kind == "B":
                            dve.nop().then_inc(s["a_done"], 1)
                            return
                        n = nkeys(t)
                        a, b = ms[0] % NP, ms[1] % NP
                        chain(dve.tensor_scalar(pr[:, b, 0:n], pr[:, b, 0:n], st[:, ms[1] % 8, 3:4], nlam[:, 0:1], ALU.mult, ALU.mult))
                        dve.scalar_tensor_tensor(out=pr[:, a, 0:n], in0=pr[:, a, 0:n], scalar=st[:, ms[0] % 8, 3:4],
                                                 in1=pr[:, b, 0:n], op0=ALU.mult, op1=ALU.add).then_inc(s["a_done"], 1)

                    def out(u):
                        kind, t, h, ms = units[u]
                        dve.wait_ge(s["pv"], u + 1)
                        if kind == "B":
                            dve.tensor_scalar(mixed[:, t, AW + h * HD:AW + (h + 1) * HD], ps[:, 6 + u % 2, 0:HD],
                                              st[:, ms[0] % 8, 3:4], None, ALU.mult).then_inc(s["o_out"], 1)
                        else:
                            dve.tensor_copy(oC[:, t, h], ps[:, 6 + u % 2, 0:HD]).then_inc(s["o_out"], 1)
                    for u in range(len(units) + 2):
                        if u < len(units):
                            for m in units[u][3]:
                                smax(m)
                        if 1 <= u <= len(units):
                            pass
                        if u < len(units):
                            combine(u)
                        if u >= 2:
                            out(u - 2)

                @block.scalar
                def _(act):
                    def probs(m, u):
                        kind, t, h, mp = maps[m]
                        n = nkeys(t)
                        scale = HD ** -0.5 if kind == "B" else DHC ** -0.5
                        act.wait_ge(s["nmax"], m + 1)
                        if u >= NP // 2:
                            act.wait_ge(s["pturn"], u - 1)
                        sc = ps[:, 2 * (m % 2):2 * (m % 2) + 2, :].rearrange("p b n -> p (b n)")[:, 0:n]
                        act.activation(pr[:, m % NP, 0:n], sc, ACT.Exp, bias=st[:, m % 8, 1:2], scale=scale,
                                       accum_out=st[:, m % 8, 2:3]).then_inc(s["probs"], 1)

                    def evac(u):
                        n = nkeys(units[u][1])
                        act.wait_ge(s["pturn"], u + 1)
                        if u >= 2:
                            act.wait_ge(s["pv"], u - 1)
                        act.copy(pT[:, u % 2, 0:n], ps[:, 4:6, :].rearrange("p b n -> p (b n)")[:, 0:n]).then_inc(s["p_out"], 1)
                    for u in range(len(units) + 1):
                        if u < len(units):
                            for m in units[u][3]:
                                probs(m, u)
                        if u >= 1:
                            evac(u - 1)
            dsq = sb("d_sq", [P, NT, HC, HD])
            dr = sb("d_r", [P, NT, HC])
            with stage(nc, "chain ms root o_done turned act_out dve_out") as (block, s):
                mc = mixed[:, :, 2 * AW:D].rearrange("p t (h d) -> p t h d", d=HD)

                @block.vector
                def _(dve):
                    chain = Chain(dve, s["chain"])
                    chain(dve.tensor_tensor(dsq[:], oC[:], oC[:], ALU.mult))
                    chain(dve.tensor_reduce(dr[:], dsq[:], AX.X, ALU.add))
                    dve.tensor_scalar(dr[:], dr[:], 1.0 / HD, EPS, ALU.mult, ALU.add).then_inc(s["ms"], 1)
                    dve.wait_ge(s["root"], 1)
                    chain(dve.reciprocal(dr[:], dr[:]))
                    for t in range(NT):
                        chain(dve.tensor_tensor(oC[:, t], oC[:, t], bcast_last(dr[:, t, :], HD), ALU.mult))
                        dve.tensor_tensor(mc[:, t], oC[:, t], bcast_mid(gdiff[:], HC), ALU.mult).then_inc(s["o_done"], 1)
                    for n in range(1, 2 * NT, 2):
                        self.mix_out(dve.tensor_copy, dve, s, n)

                @block.scalar
                def _(act):
                    act.wait_ge(s["ms"], 1)
                    act.activation(dr[:], dr[:], ACT.Sqrt).then_inc(s["root"], 1)
                    for n in range(0, 2 * NT, 2):
                        self.mix_out(act.copy, act, s, n)

                @block.tensor
                def _(pe):
                    for n in range(2 * NT):
                        t, g = divmod(n, 2)
                        if n >= 8:
                            pe.wait_ge(s["dve_out" if g else "act_out"], t - 3)
                        if g:
                            pe.wait_ge(s["o_done"], t + 1)
                        for c in range(4):
                            mm = pe.transpose(ps[:, n % 8, c * P:(c + 1) * P], mixed[:, t, (4 * g + c) * P:(4 * g + c + 1) * P], self.ident)
                        mm.then_inc(s["turned"], 1)

    def mix_out(self, copy, eng, s, n):
        t, g = divmod(n, 2)
        eng.wait_ge(s["turned"], n + 1)
        copy(self.hT[:, 4 * g:4 * g + 4, t * P:(t + 1) * P],
             self.ps[:, n % 8, :].rearrange("p (c q) -> p c q", c=4)).then_inc(s["dve_out" if g else "act_out"], 1)

    def out_proj(self, l):
        nc, i, ps = self.nc, self.i, self.ps
        with ExitStack() as scope:
            w = scope.enter_context(nc.sbuf_tensor(f"w_out_{l}", [P, KC, D], F32))
            with stage(nc, "w0 w1 w2 w3 mm added") as (block, s):
                @block.sync
                def _(sp):
                    for q in range(4):
                        sp.dma_start(w[:, :, q * 256:(q + 1) * 256], i["w_out"][l].rearrange("(c p) n -> p c n", p=P)
                                     [:, :, q * 256:(q + 1) * 256]).then_inc(s[f"w{q}"], 16)

                @block.tensor
                def _(pe):
                    for m in range(KC):
                        pe.wait_ge(s[f"w{m // 2}"], 16)
                        if m >= 4:
                            pe.wait_ge(s["added"], 2 * (m - 3))
                        for k in range(KC):
                            for j, (a, b) in enumerate(STREAMS):
                                mm = pe.matmul(ps[:, 2 * (m % 4) + j, 0:b - a], w[:, k, m * P:(m + 1) * P], self.hT[:, k, a:b],
                                               start=(k == 0), stop=(k == KC - 1))
                        mm.then_inc(s["mm"], 1)

                @block.vector
                def _(dve):
                    for m in range(KC):
                        dve.wait_ge(s["mm"], m + 1)
                        for j, (a, b) in enumerate(STREAMS):
                            x = self.xT[:, m, a:b]
                            dve.scalar_tensor_tensor(out=x, in0=ps[:, 2 * (m % 4) + j, 0:b - a], scalar=self.mod[:, l, 2, m, j:j + 1],
                                                     in1=x, op0=ALU.mult, op1=ALU.add).then_inc(s["added"], 1)

    def moe(self, l):
        nc, i, ps = self.nc, self.i, self.ps
        slots_h, slots_y = self.slots_h, self.slots_y
        with ExitStack() as outer:
            def sbo(name, shape, dt=F32):
                return outer.enter_context(nc.sbuf_tensor(name, shape, dt))
            pos = sbo("slot_of_choice", [P, 2, NT], U32)
            w = sbo("choice_weight", [P, NT, 2])
            meta = sbo("round_table", [P, RMAX + 2], I32)
            self.route(pos, w, meta)
            self.rounds(meta)
            self.combine(l, pos, w)

    def route(self, pos, w, meta):
        nc, i, ps = self.nc, self.i, self.ps
        with ExitStack() as scope:
            def sb(name, shape, dt=F32):
                return scope.enter_context(nc.sbuf_tensor(name, shape, dt))
            rw = sb("router_w", [P, KC, NE])
            htok = sb("h_tokens", [P, NT, D])
            lg = sb("logits", [P, NT, NE])
            top = sb("top", [P, NT, 8])
            idx = sb("top_idx", [P, NT, 8], U32)
            idf = sb("top_idx_f", [P, NT, 2])
            e = sb("top_e", [P, NT, 1])
            io = sb("iota", [P, 16])
            oh = sb("chosen", [P, 2, NT, NE])
            both = sb("chosen_both", [P, NT, NE])
            blocks = sb("blocks", [P, NE])
            ends = sb("block_ends", [P, 2, NE])
            tmp = sb("route_tmp", [P, 16, NE])
            posf = sb("slot_f", [P, 2, NT])
            metaf = sb("round_table_f", [P, RMAX + 2])
            with stage(nc, "w_in io mm chain diff expd both count turned h_act h_dve slots scattered") as (block, s):
                @block.sync
                def _(sp):
                    sp.dma_start(rw[:], i["moe_router"][0].rearrange("(c p) e -> p c e", p=P)).then_inc(s["w_in"], 16)
                    sp.dma_start(io[:], i["iota"].partition_broadcast(P)).then_inc(s["io"], 16)

                @block.tensor
                def _(pe):
                    pe.wait_ge(s["w_in"], 16)
                    for t in range(NT):
                        for k in range(KC):
                            mm = pe.matmul(ps[:, 0, t * NE:(t + 1) * NE], self.hT[:, k, t * P:(t + 1) * P], rw[:, k, :],
                                           start=(k == 0), stop=(k == KC - 1))
                    mm.then_inc(s["mm"], 1)
                    for n in range(2 * NT):
                        t, g = divmod(n, 2)
                        if n >= 6:
                            pe.wait_ge(s["h_dve" if g else "h_act"], t - 2)
                        for c in range(4):
                            mm = pe.transpose(ps[:, 2 + n % 6, c * P:(c + 1) * P], self.hT[:, 4 * g + c, t * P:(t + 1) * P], self.ident)
                        mm.then_inc(s["turned"], 1)
                    pe.wait_ge(s["both"], 1)
                    for t in range(NT + 1):
                        for u in range(min(t + 1, NT)):
                            mm = pe.matmul(ps[:, 1, t * NE:(t + 1) * NE], self.c(C_SL + 1) if u == t else self.ones, both[:, u, :],
                                           start=(u == 0), stop=(u == min(t, NT - 1)))
                    mm.then_inc(s["count"], 1)

                @block.scalar
                def _(act):
                    act.wait_ge(s["diff"], 1)
                    act.activation(e[:], e[:], ACT.Exp).then_inc(s["expd"], 1)
                    for t in range(NT):
                        act.wait_ge(s["turned"], 2 * t + 1)
                        act.copy(htok[:, t, 0:512], ps[:, 2 + (2 * t) % 6, :]).then_inc(s["h_act"], 1)

                @block.vector
                def _(dve):
                    chain = Chain(dve, s["chain"])
                    dve.wait_ge(s["mm"], 1)
                    dve.wait_ge(s["io"], 16)
                    chain(dve.tensor_copy(lg[:].rearrange("p t e -> p (t e)"), ps[:, 0, 0:NT * NE]))
                    for t in range(NT):
                        chain(dve.max(top[:, t], lg[:, t]), wait=t == NT - 1)
                    for t in range(NT):
                        chain(dve.max_index(idx[:, t], top[:, t], lg[:, t]), wait=t == NT - 1)
                    dve.tensor_tensor(e[:], top[:, :, 1:2], top[:, :, 0:1], ALU.subtract).then_inc(s["diff"], 1)
                    dve.wait_ge(s["diff"], 1)
                    chain(dve.tensor_copy(idf[:], idx[:, :, 0:2]))
                    for t in range(NT):
                        for q in range(2):
                            chain(dve.tensor_scalar(oh[:, q, t], io[:, 0:NE], idf[:, t, q:q + 1], None, ALU.is_equal),
                                  wait=t == NT - 1 and q)
                    dve.tensor_tensor(both[:], oh[:, 0], oh[:, 1], ALU.add).then_inc(s["both"], 1)
                    dve.wait_ge(s["expd"], 1)
                    chain(dve.tensor_scalar(w[:, :, 1:2], e[:], 1.0, None, ALU.add))
                    chain(dve.reciprocal(w[:, :, 0:1], w[:, :, 1:2]))
                    chain(dve.tensor_tensor(w[:, :, 1:2], w[:, :, 0:1], e[:], ALU.mult))
                    for t in range(NT):
                        dve.wait_ge(s["turned"], 2 * t + 2)
                        dve.tensor_copy(htok[:, t, 512:D], ps[:, 2 + (2 * t + 1) % 6, :]).then_inc(s["h_dve"], 1)
                    dve.wait_ge(s["count"], 1)
                    cnt = ps[:, 1, NT * NE:(NT + 1) * NE]
                    chain(dve.tensor_scalar(blocks[:], cnt, 0.0, None, ALU.is_gt))
                    for q in range(1, -(-T // BLK)):
                        chain(dve.tensor_scalar(ends[:, 0], cnt, float(q * BLK), None, ALU.is_gt))
                        chain(dve.tensor_tensor(blocks[:], blocks[:], ends[:, 0], ALU.add))
                    chain(dve.tensor_copy(ends[:, 0], blocks[:]))
                    for n, step in enumerate((1, 2, 4)):
                        a, b = n % 2, 1 - n % 2
                        chain(dve.tensor_copy(ends[:, b, 0:step], ends[:, a, 0:step]))
                        chain(dve.tensor_tensor(ends[:, b, step:], ends[:, a, step:], ends[:, a, 0:NE - step], ALU.add))
                    chain(dve.tensor_tensor(tmp[:, 0:16], bcast_mid(ends[:, 1], 16), bcast_last(io[:], NE), ALU.is_le))
                    chain(dve.tensor_reduce(metaf[:, 0:RMAX + 1], tmp[:, 0:RMAX + 1], AX.X, ALU.add))
                    chain(dve.tensor_scalar(metaf[:, 0:RMAX + 1], metaf[:, 0:RMAX + 1], float(NE - 1), None, ALU.min))
                    chain(dve.tensor_copy(metaf[:, RMAX + 1:RMAX + 2], ends[:, 1, NE - 1:NE]))
                    chain(dve.tensor_copy(meta[:], metaf[:]))
                    chain(dve.tensor_tensor(blocks[:], ends[:, 1], blocks[:], ALU.subtract))
                    chain(dve.tensor_scalar(blocks[:], blocks[:], float(BLK), None, ALU.mult))
                    chain(dve.tensor_tensor(tmp[:, 0:NT], ps[:, 1, 0:NT * NE].rearrange("p (t e) -> p t e", e=NE),
                                            bcast_mid(blocks[:], NT), ALU.add))
                    for q in range(2):
                        chain(dve.tensor_tensor(oh[:, q], oh[:, q], tmp[:, 0:NT], ALU.mult))
                        chain(dve.tensor_reduce(posf[:, q], oh[:, q], AX.X, ALU.add))
                    dve.tensor_copy(pos[:], posf[:]).then_inc(s["slots"], 1)

                @block.gpsimd
                def _(pool):
                    pool.wait_ge(s["slots"], 1)
                    for t in range(NT):
                        pool.wait_ge(s["h_act"], t + 1)
                        pool.wait_ge(s["h_dve"], t + 1)
                        for q in range(2):
                            pool.indirect_dma_start(self.slots_h, bass.IndirectOffsetOnAxis(pos[:, q, t:t + 1], 0),
                                                    htok[:, t, :], None).then_inc(s["scattered"], 16)
                    pool.wait_ge(s["scattered"], 16 * 2 * NT)

    def rounds(self, meta):
        nc, i, ps = self.nc, self.i, self.ps
        SL = 3
        GU, W3 = 2 * KC * P, 2 * KC * P + D
        last = [9, 10, 8]
        loads = [4, 4, 3]
        wgu = i["moe_w_gu"][0].rearrange("e (c p) (h j n) -> e p h j c n", p=P, h=2, n=P)
        wdn = i["moe_w_down"][0].rearrange("e (j p) n -> e j p n", p=P)
        yv = self.slots_y.rearrange("(r a p) d -> r p a d", a=2, p=P)
        hv = self.slots_h.rearrange("(r a p) d -> r p a d", a=2, p=P)
        with ExitStack() as scope:
            def sb(name, shape, dt=F32):
                return scope.enter_context(nc.sbuf_tensor(name, shape, dt))
            raw = sb("w_raw", [P, SL, W3])
            whi = sb("w_hi", [P, SL, W3], F32R)
            wlo = sb("w_lo", [P, SL, W3], F32R)
            hblk = sb("h_block", [P, 2, D])
            hhi = sb("h_hi", [P, KC, BLK], F32R)
            hlo = sb("h_lo", [P, KC, BLK], F32R)
            sg = sb("silu_g", [P, 2, BLK])
            ahi = sb("act_hi", [P, 2, BLK], F32R)
            alo = sb("act_lo", [P, 2, BLK], F32R)
            y = sb("y_block", [P, 2, D])
            TB = (2, 3, 0, 1)
            names = ("blk_in turned h_hi h_lo w_hi w_lo gu silu prod a_hi a_lo dn y_act y_dve y_store y_free "
                     + " ".join(f"raw{q}" for q in range(SL)))

            def gu(t, j, half, k):
                o = (half * KC + k) * P
                return t[:, j % SL, o:o + P]

            def dn(t, j, half):
                return t[:, j % SL, GU + 512 * half:GU + 512 * half + 512]

            def quarter(n):
                return n // 2, 4 * (n % 2)
            with stage(nc, names) as (block, s):
                @block.sync
                def _(sp):
                    def load_w(e, j):
                        q = j % SL
                        for half in range(2):
                            o = half * KC * P
                            sp.dma_start(raw[:, q, o:o + KC * P].rearrange("p (c n) -> p c n", c=KC),
                                         wgu[e, :, half, j]).then_inc(s[f"raw{q}"], 16)
                        sp.dma_start(raw[:, q, GU:W3], wdn[e, j]).then_inc(s[f"raw{q}"], 16)
                    rounds = sp.value_load(meta[0:1, RMAX + 1:RMAX + 2], min_val=1, max_val=RMAX)
                    e0 = sp.value_load(meta[0:1, 0:1], min_val=0, max_val=NE - 1)
                    sp.dma_start(hblk[:], hv[0]).then_inc(s["blk_in"], 16)
                    for j in range(SL):
                        load_w(e0, j)
                    with sp.Fori(0, rounds) as r:
                        sp.wait_ge(s["turned"], 4 * r + 4)
                        sp.dma_start(hblk[:], hv[r + 1]).then_inc(s["blk_in"], 16)
                        e = sp.value_load(meta[0:1, bass.ds(r, 1)], min_val=0, max_val=NE - 1)
                        for j in range(SL, FC):
                            sp.wait_ge(s["w_hi"], 11 * r + (j - SL) + 1)
                            sp.wait_ge(s["w_lo"], 11 * r + (j - SL) + 1)
                            load_w(e, j)
                        en = sp.value_load(meta[0:1, bass.ds(r + 1, 1)], min_val=0, max_val=NE - 1)
                        for j in range(SL):
                            sp.wait_ge(s["w_hi"], 11 * r + last[j] + 1)
                            sp.wait_ge(s["w_lo"], 11 * r + last[j] + 1)
                            load_w(en, j)

                @block.tensor
                def _(pe):
                    rounds = pe.value_load(meta[0:1, RMAX + 1:RMAX + 2], min_val=1, max_val=RMAX)
                    pe.nop().then_inc(s["dn"], 11)

                    def turn(r):
                        pe.wait_ge(s["blk_in"], 16 * r + 16)
                        for n in range(4):
                            if n == 2:
                                pe.wait_ge(s["prod"], 11 * r + 11)
                            a, c0 = quarter(n)
                            for c in range(4):
                                mm = pe.transpose(ps[:, TB[n], c * P:(c + 1) * P], hblk[:, a, (c0 + c) * P:(c0 + c + 1) * P], self.ident)
                            mm.then_inc(s["turned"], 1)

                    def down(r, j):
                        pe.wait_ge(s["a_lo"], 11 * r + j + 1)
                        if j == 0:
                            pe.wait_ge(s["y_act"], 2 * r + 2)
                            pe.wait_ge(s["y_dve"], 2 * r + 2)
                        for a in range(2):
                            for n, (x, wt) in enumerate(((ahi, whi), (ahi, wlo), (alo, whi))):
                                for half in range(2):
                                    mm = pe.matmul(ps[:, 4 + 2 * a + half, :], x[:, j % 2, a * P:(a + 1) * P], dn(wt, j, half),
                                                   start=(j == 0 and n == 0), stop=(j == FC - 1 and n == 2))
                        mm.then_inc(s["dn"], 1)
                    turn(0)
                    with pe.Fori(0, rounds) as r:
                        pe.wait_ge(s["h_lo"], 4 * r + 4)
                        for j in range(FC):
                            pe.wait_ge(s["w_lo"], 11 * r + j + 1)
                            pe.wait_ge(s["prod"], 11 * r + (11, 10)[j] if j < 2 else 11 * r + 11 + j - 1)
                            for half in range(2):
                                for k in range(KC):
                                    for n, (wt, x) in enumerate(((whi, hhi), (whi, hlo), (wlo, hhi))):
                                        mm = pe.matmul(ps[:, j % 2, half * BLK:(half + 1) * BLK], gu(wt, j, half, k), x[:, k, :],
                                                       start=(k == 0 and n == 0), stop=(k == KC - 1 and n == 2))
                            mm.then_inc(s["gu"], 1)
                            if j:
                                down(r, j - 1)
                        turn(r + 1)
                        down(r, FC - 1)

                @block.scalar
                def _(act):
                    rounds = act.value_load(meta[0:1, RMAX + 1:RMAX + 2], min_val=1, max_val=RMAX)
                    act.nop().then_inc(s["y_act"], 2)

                    def take_block(r):
                        for n in range(4):
                            a, c0 = quarter(n)
                            act.wait_ge(s["turned"], 4 * r + n + 1)
                            act.copy(hhi[:, c0:c0 + 4, a * P:(a + 1) * P], ps[:, TB[n], :].rearrange("p (c q) -> p c q", c=4)
                                     ).then_inc(s["h_hi"], 1)

                    def split(r, j):
                        q = j % SL
                        act.wait_ge(s[f"raw{q}"], 48 * (loads[q] * r + j // SL + 1))
                        act.wait_ge(s["dn"], 11 * r + last[q] + 1 if j < SL else 11 * r + 11 + j - SL + 1)
                        act.copy(whi[:, q, :], raw[:, q, :]).then_inc(s["w_hi"], 1)
                    take_block(0)
                    split(0, 0)
                    split(0, 1)
                    with act.Fori(0, rounds) as r:
                        for j in range(FC):
                            act.wait_ge(s["gu"], 11 * r + j + 1)
                            if j == 0:
                                act.wait_ge(s["prod"], 11 * r + 11)
                            else:
                                act.wait_ge(s["prod"], 11 * r + 11 + max(j - 1, 0))
                            act.activation(sg[:, j % 2, :], ps[:, j % 2, 0:BLK], ACT.Silu).then_inc(s["silu"], 1)
                            act.wait_ge(s["prod"], 11 * r + 11 + j + 1)
                            act.wait_ge(s["dn"], 11 * r + 11 + max(j - 1, 0))
                            act.copy(ahi[:, j % 2, :], sg[:, j % 2, :]).then_inc(s["a_hi"], 1)
                            if j + 2 < FC:
                                split(r, j + 2)
                        split(r + 1, 0)
                        take_block(r + 1)
                        split(r + 1, 1)
                        act.wait_ge(s["dn"], 11 * r + 22)
                        act.wait_ge(s["y_free"], r + 1)
                        for half in range(2):
                            act.copy(y[:, 0, 512 * half:512 * half + 512], ps[:, 4 + half, :]).then_inc(s["y_act"], 1)

                @block.vector
                def _(dve):
                    rounds = dve.value_load(meta[0:1, RMAX + 1:RMAX + 2], min_val=1, max_val=RMAX)
                    dve.nop().then_inc(s["prod"], 11)
                    dve.nop().then_inc(s["y_dve"], 2)

                    def take_block(r):
                        for n in range(4):
                            a, c0 = quarter(n)
                            dve.wait_ge(s["h_hi"], 4 * r + n + 1)
                            dve.tensor_tensor(hlo[:, c0:c0 + 4, a * P:(a + 1) * P], ps[:, TB[n], :].rearrange("p (c q) -> p c q", c=4),
                                              hhi[:, c0:c0 + 4, a * P:(a + 1) * P].bitcast(F32), ALU.subtract).then_inc(s["h_lo"], 1)

                    def split(r, j):
                        q = j % SL
                        dve.wait_ge(s["w_hi"], 11 * r + j + 1)
                        dve.tensor_tensor(wlo[:, q, :], raw[:, q, :], whi[:, q, :].bitcast(F32), ALU.subtract).then_inc(s["w_lo"], 1)
                    take_block(0)
                    split(0, 0)
                    split(0, 1)
                    with dve.Fori(0, rounds) as r:
                        for j in range(FC):
                            dve.wait_ge(s["silu"], 11 * r + j + 1)
                            g = sg[:, j % 2, :]
                            dve.tensor_tensor(g, g, ps[:, j % 2, BLK:2 * BLK], ALU.mult).then_inc(s["prod"], 1)
                            dve.wait_ge(s["a_hi"], 11 * r + j + 1)
                            dve.tensor_tensor(alo[:, j % 2, :], g, ahi[:, j % 2, :].bitcast(F32), ALU.subtract).then_inc(s["a_lo"], 1)
                            if j + 2 < FC:
                                split(r, j + 2)
                        split(r + 1, 0)
                        take_block(r + 1)
                        split(r + 1, 1)
                        dve.wait_ge(s["dn"], 11 * r + 22)
                        dve.wait_ge(s["y_free"], r + 1)
                        for half in range(2):
                            dve.tensor_copy(y[:, 1, 512 * half:512 * half + 512], ps[:, 6 + half, :]).then_inc(s["y_dve"], 1)

                @block.gpsimd
                def _(pool):
                    rounds = pool.value_load(meta[0:1, RMAX + 1:RMAX + 2], min_val=1, max_val=RMAX)
                    pool.nop().then_inc(s["y_free"], 1)
                    with pool.Fori(0, rounds) as r:
                        pool.wait_ge(s["y_act"], 2 * r + 4)
                        pool.wait_ge(s["y_dve"], 2 * r + 4)
                        pool.dma_start(yv[r], y[:]).then_inc(s["y_store"], 16)
                        pool.wait_ge(s["y_store"], 16 * r + 16)
                        pool.nop().then_inc(s["y_free"], 1)
                    pool.wait_ge(s["blk_in"], 16 * rounds + 16)
                    for q in range(SL):
                        pool.wait_ge(s[f"raw{q}"], 48 * (loads[q] * rounds + 1))

    def combine(self, l, pos, w):
        nc, i, ps = self.nc, self.i, self.ps
        with ExitStack() as scope:
            y1 = scope.enter_context(nc.sbuf_tensor("y_first", [P, NT, D], F32))
            y2 = scope.enter_context(nc.sbuf_tensor("y_second", [P, NT, D], F32))
            with stage(nc, "first scaled summed turned added " + " ".join(f"g{t}" for t in range(NT))) as (block, s):
                @block.gpsimd
                def _(pool):
                    for t in range(NT):
                        for q, y in ((0, y1), (1, y2)):
                            pool.indirect_dma_start(y[:, t, :], None, self.slots_y, bass.IndirectOffsetOnAxis(pos[:, q, t:t + 1], 0)
                                                    ).then_inc(s[f"g{t}"], 16)
                    for t in range(NT):
                        pool.wait_ge(s[f"g{t}"], 32)

                @block.scalar
                def _(act):
                    for t in range(NT):
                        act.wait_ge(s[f"g{t}"], 32)
                        act.activation(y1[:, t, :], y1[:, t, :], ACT.Copy, scale=w[:, t, 0:1]).then_inc(s["scaled"], 1)

                @block.vector
                def _(dve):
                    def add(n):
                        t, g = divmod(n, 2)
                        dve.wait_ge(s["turned"], n + 1)
                        for c in range(4):
                            x = self.xT[:, 4 * g + c, t * P:(t + 1) * P]
                            ins = dve.scalar_tensor_tensor(out=x, in0=ps[:, n % 8, c * P:(c + 1) * P],
                                                           scalar=self.mod[:, l, 5, 4 * g + c, min(t, 1):min(t, 1) + 1],
                                                           in1=x, op0=ALU.mult, op1=ALU.add)
                        ins.then_inc(s["added"], 1)
                    for t in range(NT):
                        dve.wait_ge(s["scaled"], t + 1)
                        dve.scalar_tensor_tensor(out=y1[:, t, :], in0=y2[:, t, :], scalar=w[:, t, 1:2], in1=y1[:, t, :],
                                                 op0=ALU.mult, op1=ALU.add).then_inc(s["summed"], 1)
                        if t:
                            add(2 * t - 2)
                            add(2 * t - 1)
                    add(2 * NT - 2)
                    add(2 * NT - 1)

                @block.tensor
                def _(pe):
                    for n in range(2 * NT):
                        t, g = divmod(n, 2)
                        pe.wait_ge(s["summed"], t + 1)
                        if n >= 8:
                            pe.wait_ge(s["added"], n - 7)
                        for c in range(4):
                            mm = pe.transpose(ps[:, n % 8, c * P:(c + 1) * P], y1[:, t, (4 * g + c) * P:(4 * g + c + 1) * P], self.ident)
                        mm.then_inc(s["turned"], 1)

    def ffn(self, l, n_exp, w_gu, w_dn, gT=None):
        nc, i, ps = self.nc, self.i, self.ps
        SG = 4
        with ExitStack() as scope:
            def sb(name, shape, dt=F32):
                return scope.enter_context(nc.sbuf_tensor(f"{name}_{l}", shape, dt))
            wg = sb("w_gu_ring", [P, FC, 2, KC, P])
            wd = sb("w_dn_ring", [P, 4, FC, P])
            act_t = sb("act", [P, FC, T])
            names = "gu silu prod dn added chain gb gbo " + " ".join(f"g{j}" for j in range(FC)) + \
                " " + " ".join(f"d{j}" for j in range(4))
            gb = sb("gate_bc", [P, T]) if gT is not None else None
            sel = sb("sel", [NE, NE, P]) if gT is not None else None
            if gT is not None:
                names += " sel"
            with stage(nc, names) as (block, s):
                @block.sync
                def _(sp):
                    if gT is not None:
                        sp.dma_start(sel[:], i["sel"]).then_inc(s["sel"], 16)
                    def load(e, j):
                        for half in range(2):
                            sp.dma_start(wg[:, j, half], w_gu(e, half, j)).then_inc(s[f"g{j}"], 16)

                    for j in range(FC):
                        load(0, j)
                    def load_dn(e, m):
                        sp.dma_start(wd[:, m % 4], w_dn(e, m)).then_inc(s[f"d{m % 4}"], 16)

                    for m in range(4):
                        load_dn(0, m)
                    with sp.Fori(1, n_exp) as e:
                        for j in range(FC):
                            sp.wait_ge(s["gu"], e * FC - FC + j + 1)
                            load(e, j)
                        for m in range(4):
                            sp.wait_ge(s["dn"], e * KC - KC + m + 1)
                            load_dn(e - 1, m + 4)
                        for m in range(4):
                            sp.wait_ge(s["dn"], e * KC - KC + m + 5)
                            load_dn(e, m)
                    for m in range(4):
                        sp.wait_ge(s["dn"], n_exp * KC - KC + m + 1)
                        load_dn(n_exp - 1, m + 4)

                @block.tensor
                def _(pe):
                    def body(e, first):
                        if gT is not None:
                            if first:
                                pe.wait_ge(s["sel"], 16)
                            else:
                                pe.wait_ge(s["added"], e * (2 * KC))
                            for j2, (a, b) in enumerate(STREAMS):
                                mm = pe.matmul(ps[:, j2, 0:b - a], sel[:, self.e_static, :], gT[0:NE, a:b], start=True, stop=True)
                            mm.then_inc(s["gb"], 1)
                        for j in range(FC):
                            pe.wait_ge(s[f"g{j}"], 32 * e + 32)
                            if j >= 2:
                                pe.wait_ge(s["prod"], (e * FC + j - 1) * 2)
                            elif j == 0 and gT is not None:
                                pe.wait_ge(s["gbo"], 2 * e + 2)
                            if j < 2 and not first:
                                pe.wait_ge(s["added"], e * (2 * KC))
                            for half in range(2):
                                for k in range(KC):
                                    for q, (a, b) in enumerate(STREAMS):
                                        mm = pe.matmul(ps[:, 4 * (j % 2) + 2 * half + q, 0:b - a], wg[:, j, half, k, :],
                                                       self.hT[:, k, a:b], start=(k == 0), stop=(k == KC - 1))
                            mm.then_inc(s["gu"], 1)
                        for m in range(KC):
                            if m == 0:
                                pe.wait_ge(s["prod"], (e * FC + FC) * 2)
                            pe.wait_ge(s[f"d{m % 4}"], 32 * e + 16 * (m // 4) + 16)
                            if m >= 4:
                                pe.wait_ge(s["added"], e * (2 * KC) + (m - 3) * 2)
                            for j in range(FC):
                                for q, (a, b) in enumerate(STREAMS):
                                    mm = pe.matmul(ps[:, 2 * (m % 4) + q, 0:b - a], wd[:, m % 4, j, :],
                                                   act_t[:, j, a:b], start=(j == 0), stop=(j == FC - 1))
                            mm.then_inc(s["dn"], 1)
                    if gT is None:
                        body(0, True)
                        with pe.Fori(1, n_exp) as e:
                            body(e, False)
                    else:
                        for e in range(n_exp):
                            self.e_static = e
                            body(e, e == 0)

                @block.scalar
                def _(act):
                    def body(e):
                        for j in range(FC):
                            act.wait_ge(s["gu"], e * FC + j + 1)
                            if j == 0:
                                act.wait_ge(s["dn"], e * KC + 0) if not isinstance(e, int) or e else None
                            for q, (a, b) in enumerate(STREAMS):
                                act.activation(act_t[:, j, a:b], ps[:, 4 * (j % 2) + q, 0:b - a], ACT.Silu).then_inc(s["silu"], 1)
                    body(0)
                    with act.Fori(1, n_exp) as e:
                        body(e)

                @block.vector
                def _(dve):
                    def body(e):
                        if gT is not None:
                            dve.wait_ge(s["gb"], e + 1)
                            for q, (a, b) in enumerate(STREAMS):
                                dve.tensor_copy(gb[:, a:b], ps[:, q, 0:b - a]).then_inc(s["gbo"], 1)
                            dve.wait_ge(s["gbo"], 2 * e + 2)
                        for j in range(FC):
                            for q, (a, b) in enumerate(STREAMS):
                                dve.wait_ge(s["silu"], (e * FC + j) * 2 + q + 1)
                                y = act_t[:, j, a:b]
                                ins = dve.tensor_tensor(y, y, ps[:, 4 * (j % 2) + 2 + q, 0:b - a], ALU.mult)
                                if gT is not None:
                                    ins.then_inc(s["chain"], 1)
                                    dve.wait_ge(s["chain"], (e * FC + j) * 2 + q + 1)
                                    ins = dve.tensor_tensor(y, y, gb[:, a:b], ALU.mult)
                                ins.then_inc(s["prod"], 1)
                        for m in range(KC):
                            dve.wait_ge(s["dn"], e * KC + m + 1)
                            for q, (a, b) in enumerate(STREAMS):
                                x = self.xT[:, m, a:b]
                                dve.scalar_tensor_tensor(out=x, in0=ps[:, 2 * (m % 4) + q, 0:b - a], scalar=self.mod[:, l, 5, m, q:q + 1],
                                                         in1=x, op0=ALU.mult, op1=ALU.add).then_inc(s["added"], 1)
                        dve.wait_ge(s["added"], e * (2 * KC) + 2 * KC)
                    body(0)
                    with dve.Fori(1, n_exp) as e:
                        body(e)

    def store(self):
        nc, ps = self.nc, self.ps
        with ExitStack() as scope:
            y = scope.enter_context(nc.sbuf_tensor("y_out", [P, NT, D], F32))
            with stage(nc, "turned out_act out_dve stored") as (block, s):
                @block.tensor
                def _(pe):
                    for n in range(2 * NT):
                        t, g = divmod(n, 2)
                        if n >= 8:
                            pe.wait_ge(s["out_dve" if g else "out_act"], t - 3)
                        for c in range(4):
                            mm = pe.transpose(ps[:, n % 8, c * P:(c + 1) * P], self.hT[:, 4 * g + c, t * P:(t + 1) * P], self.ident)
                        mm.then_inc(s["turned"], 1)

                @block.scalar
                def _(act):
                    for t in range(NT):
                        act.wait_ge(s["turned"], 2 * t + 1)
                        act.copy(y[:, t, 0:512], ps[:, (2 * t) % 8, :]).then_inc(s["out_act"], 1)

                @block.vector
                def _(dve):
                    for t in range(NT):
                        dve.wait_ge(s["turned"], 2 * t + 2)
                        dve.tensor_copy(y[:, t, 512:D], ps[:, (2 * t + 1) % 8, :]).then_inc(s["out_dve"], 1)

                @block.sync
                def _(sp):
                    for t in range(NT):
                        sp.wait_ge(s["out_act"], t + 1)
                        sp.wait_ge(s["out_dve"], t + 1)
                        dst = self.o["yp"][0] if t == 0 else self.o["ys"][0, (t - 1) * P:t * P, :]
                        sp.dma_start(dst, y[:, t]).then_inc(s["stored"], 16)
                    sp.wait_ge(s["stored"], 16 * NT)


def build_program(nc, i, o, stop=None):
    with ExitStack() as ctx:
        k = Kernel(nc, i, o, ctx)
        k.prologue()
        for l in range(DEPTH):
            k.norm(lambda c, j: k.amul[:, l, 0, c, j:j + 1], lambda c, j: k.mod[:, l, 0, c, j:j + 1])
            k.mixer(l)
            k.norm(lambda c, j: k.amul[:, l, 1, c, j:j + 1], lambda c, j: k.mod[:, l, 3, c, j:j + 1])
            if l == 0:
                w1 = i["ffn_w_gu"][0].rearrange("(c p) (h e j n) -> p h e j c n", p=P, h=2, e=2, n=P)
                w2 = i["ffn_w_down"][0].rearrange("(e j p) (m n) -> e m p j n", e=2, p=P, n=P)
                k.ffn(l, 2, lambda e, half, j: w1[:, half, e, j], lambda e, m: w2[e, m])
            else:
                k.moe(l)
        k.norm(lambda c, j: k.cols[:, 112 + 32 + c:][:, 0:1], None)
        k.store()


def shape_constants():
    a = np.arange(P)
    r, c = a[:, None], a[None, :]
    t = [r == c, np.ones((P, P)), r <= c, r >= c, r > c, r < c]
    for d in range(2):
        j, i_ = r, c
        for lev in range(NLEV):
            b = 1 << lev
            same = j // (2 * b) == i_ // (2 * b)
            lo, hi = (j, i_) if d == 0 else (i_, j)
            t.append(same & (lo % (2 * b) < b) & (hi % (2 * b) >= b))
    consts = np.stack([np.asarray(x, np.float32) for x in t], axis=1)
    pos = np.arange(4 * P)
    row, col = (pos // 64).astype(np.float32), (pos % 64).astype(np.float32)
    parts = []
    for hd in (HD, DHC):
        nf = hd // 4
        inv = np.float32(10000.0) ** (-np.arange(nf, dtype=np.float32) / np.float32(nf))
        ang = np.stack([row[:, None] * inv, col[:, None] * inv], axis=1)
        cs, sn = np.cos(ang), np.sin(ang)
        parts.append(np.stack([cs, cs], axis=2).reshape(4 * P, hd))
        parts.append(np.stack([-sn, sn], axis=2).reshape(4 * P, hd))
    rope = np.concatenate(parts, axis=1).astype(np.float32).reshape(4, P, 192).transpose(1, 0, 2)
    sel = np.zeros((NE, NE, P), np.float32)
    for e in range(NE):
        sel[e, e] = 1.0
    return {"consts": np.ascontiguousarray(consts), "rope": np.ascontiguousarray(rope),
            "iota": np.arange(16, dtype=np.float32), "sel": sel}


_INS = ["x_prompt", "x_sample", "state_delta", "cache_gqa_k", "cache_gqa_v", "cache_diff_k", "cache_diff_v", "c",
        "c_ctx", "ada_w", "ada_b", "norm_mix", "norm_ffn", "w_in", "conv_w", "dn_a_log", "dn_dt_bias", "dn_norm",
        "gqa_q_norm", "gqa_k_norm", "diff_lambda", "diff_norm", "w_out", "ffn_w_gu", "ffn_w_down", "moe_router",
        "moe_w_gu", "moe_w_down", "final_norm"]
_OUTS = {"yp": (1, P, D), "ys": (1, 4 * P, D), "state": (1, DEPTH, 2, HA, HD, HD), "gk": (1, DEPTH, P, KVB, HD),
         "gv": (1, DEPTH, P, KVB, HD), "dk": (1, DEPTH, P, HC, 2, DHC), "dv": (1, DEPTH, P, HC, HD)}


def kernel(**inputs):
    import concourse.bacc as bacc
    from concourse.bass_utils import run_bass_kernel_spmd

    nc = bacc.Bacc("TRN2", target_bir_lowering=False, num_devices=1)
    arrays, ins, outs = {}, {}, {}
    given = {n: np.ascontiguousarray(inputs[n]) for n in _INS}
    given.update(shape_constants())
    for name, a in given.items():
        arrays[f"in_{name}"] = a
        ins[name] = nc.dram_tensor(f"in_{name}", a.shape, mybir.dt.from_np(a.dtype), kind="ExternalInput").ap()
    for name, shape in _OUTS.items():
        outs[name] = nc.dram_tensor(f"out_{name}", shape, F32, kind="ExternalOutput").ap()
    build_program(nc, ins, outs)
    r = run_bass_kernel_spmd(nc, [arrays], core_ids=[0])
    return tuple(r.results[0][f"out_{name}"] for name in _OUTS)
```

```python
import math
from contextlib import ExitStack, contextmanager

import numpy as np

import concourse.bass as bass
from concourse import mybir

F32 = mybir.dt.float32
I32 = mybir.dt.int32
U32 = mybir.dt.uint32
F32R = mybir.dt.float32r
ACT = mybir.ActivationFunctionType
ALU = mybir.AluOpType
AX = mybir.AxisListType

P = 128
D = 1024
KC = D // P
T = 640
NT = T // P
DEPTH = 2
HD = 64
HA = 6
AW = HA * HD
FM = 3 * AW
IN_COLS = 2968
TM = IN_COLS - FM
Z0, BE0, AR0, QB0, KB0, VB0, QC0, KCC0, VC0 = 0, 384, 396, 408, 792, 920, 1048, 1304, 1560
TMT = TM // 4
PAST = 256
HB, KVB = 6, 2
HC, DHC = 4, 32
DFF = 1408
FC = DFF // P
NE = 8
BLK = 256
RMAX = 2 * T // BLK + NE - 1
EPS = 1e-6
STREAMS = ((0, P), (P, T))
HALVES = ((0, T // 2), (T // 2, T))
PIECES = ((0, P, 0, 0), (P, T // 2, 0, 1), (T // 2, T, 1, 1))
NLEV = 7
C_ID, C_ONE, C_U, C_SL, C_LV = 0, 1, 2, 4, 6
NCONST = C_LV + 2 * NLEV
KEYS = P + PAST + 4 * P


class Chain:

    def __init__(self, eng, sem):
        self.eng, self.sem, self.n = eng, sem, 0

    def __call__(self, ins, wait=True):
        self.n += 1
        ins.then_inc(self.sem, 1)
        if wait:
            self.eng.wait_ge(self.sem, self.n)


@contextmanager
def stage(nc, names):
    at = nc.next_id()
    sems = {n: nc.alloc_semaphore(f"{n}_{at}") for n in names.split()}
    with nc.Block() as block:
        yield block, sems
    nc.clear_and_free_semaphores(list(sems.values()))
    nc.all_engine_barrier()


def bcast_mid(ap, n):
    return ap.unsqueeze(1).to_broadcast([ap.shape[0], n, ap.shape[1]])


def bcast_last(ap, n):
    return ap.unsqueeze(2).to_broadcast([ap.shape[0], ap.shape[1], n])


class Split:

    def __init__(self, k, scope, name, width, raw_slots, slots, tiles, sources, used=lambda n: ("w_used", n + 1)):
        def sb(n, shape, dt):
            return scope.enter_context(k.nc.sbuf_tensor(f"{n}_{name}", shape, dt))
        self.raw_slots, self.slots, self.tiles, self.sources, self.used = raw_slots, slots, list(tiles), sources, used
        self.raw = sb("w_raw", [P, raw_slots, width], F32)
        self.hi = sb("w_hi", [P, slots, width], F32R)
        self.lo = sb("w_lo", [P, slots, width], F32R)
        self.names = "w_hi w_lo w_used " + " ".join(f"raw{q}" for q in range(raw_slots))
        self.landed, self.widths = [], []
        count = [0] * raw_slots
        for n, tile in enumerate(self.tiles):
            src = sources(tile)
            count[n % raw_slots] += 16 * len(src)
            self.landed.append(count[n % raw_slots])
            self.widths.append(sum(math.prod(a.shape[1:]) for a, _ in src))

    def load(self, sp, s, n):
        q = n % self.raw_slots
        if n >= self.raw_slots:
            sp.wait_ge(s["w_hi"], n - self.raw_slots + 1)
            sp.wait_ge(s["w_lo"], n - self.raw_slots + 1)
        o = 0
        for src, c in self.sources(self.tiles[n]):
            size = math.prod(src.shape[1:])
            sp.dma_start(self.raw[:, q, o:o + size].rearrange("p (c n) -> p c n", c=c), src).then_inc(s[f"raw{q}"], 16)
            o += size

    def split_hi(self, act, s, n):
        q, w = n % self.raw_slots, self.widths[n]
        act.wait_ge(s[f"raw{q}"], self.landed[n])
        if n >= self.slots:
            sem, value = self.used(n - self.slots)
            act.wait_ge(s[sem], value)
        act.copy(self.hi[:, n % self.slots, 0:w], self.raw[:, q, 0:w]).then_inc(s["w_hi"], 1)

    def split_lo(self, dve, s, n):
        q, w = n % self.raw_slots, self.widths[n]
        dve.wait_ge(s["w_hi"], n + 1)
        dve.tensor_tensor(self.lo[:, n % self.slots, 0:w], self.raw[:, q, 0:w],
                          self.hi[:, n % self.slots, 0:w].bitcast(F32), ALU.subtract).then_inc(s["w_lo"], 1)


class Kernel:
    def __init__(self, nc, i, o, ctx):
        self.nc, self.i, self.o = nc, i, o

        def sb(name, shape, dt=F32):
            return ctx.enter_context(nc.sbuf_tensor(name, shape, dt))

        self.ps = ctx.enter_context(nc.psum_tensor("ps", [P, 8, 512], F32))
        self.xT = sb("xT", [P, KC, T])
        self.cst = sb("cst", [P, NCONST, P])
        self.cols = sb("cols", [P, 112 + 94])
        self.condT = sb("condT", [P, KC, 2])
        self.mod = sb("mod", [P, DEPTH, 6, KC, 2])
        self.amul = sb("amul", [P, DEPTH, 2, KC, 2])
        self.slots_h = nc.dram_tensor("slots_h", [(RMAX + 1) * BLK, D], F32).ap()
        self.slots_y = nc.dram_tensor("slots_y", [RMAX * BLK, D], F32).ap()
        self.ident = self.cst[:, C_ID, :]
        self.ones = self.cst[:, C_ONE, :]

    def c(self, n):
        return self.cst[:, n, :]

    def prologue(self):
        nc, i, ps = self.nc, self.i, self.ps
        NW = 24
        SL = 4
        with ExitStack() as scope:
            def sb(name, shape, dt=F32):
                return scope.enter_context(nc.sbuf_tensor(name, shape, dt))
            xin = sb("xin", [P, NT, D])
            rows = sb("rows", [P, 2, P])
            wr = sb("ada_ring", [P, SL, KC, 512])
            modr = sb("mod_row", [2, 2, 512])
            names = "mod_row mod_col consts_in x_in rows_in row_turned cols_out cond x_turned x_out mod_mm mod_out chain " + \
                " ".join(f"w_in{s}" for s in range(SL))
            with stage(nc, names) as (block, s):
                @block.sync
                def _(sp):
                    sp.dma_start(self.cst[:], i["consts"]).then_inc(s["consts_in"], 16)
                    for r0, n, src, half in (
                            (0, 96, i["ada_b"].rearrange("l (c p) -> (l c) p", p=P), 0),
                            (96, 8, i["c_ctx"].rearrange("(c p) -> c p", p=P), 0),
                            (104, 8, i["c"].rearrange("b (c p) -> (b c) p", p=P), 0),
                            (0, 16, i["norm_mix"].rearrange("l (c p) -> (l c) p", p=P), 1),
                            (16, 16, i["norm_ffn"].rearrange("l (c p) -> (l c) p", p=P), 1),
                            (32, 8, i["final_norm"].rearrange("(c p) -> c p", p=P), 1),
                            (40, 54, i["conv_w"].rearrange("l w (c p) -> (l w c) p", p=P), 1)):
                        sp.dma_start(rows[r0:r0 + n, half, :], src).then_inc(s["rows_in"], 16)
                    sp.dma_start(xin[:, 0, :], i["x_prompt"][0]).then_inc(s["x_in"], 16)
                    sp.dma_start(xin[:, 1:NT, :], i["x_sample"][0].rearrange("(t p) d -> p t d", p=P)
                                 ).then_inc(s["x_in"], 16)
                    for n in range(NW):
                        if n >= SL:
                            sp.wait_ge(s["mod_mm"], n - SL + 1)
                        l, j = divmod(n, 12)
                        sp.dma_start(wr[:, n % SL], i["ada_w"][l].rearrange("(c p) n -> p c n", p=P)
                                     [:, :, j * 512:(j + 1) * 512]).then_inc(s[f"w_in{n % SL}"], 16)

                @block.tensor
                def _(pe):
                    pe.wait_ge(s["consts_in"], 16)
                    pe.wait_ge(s["rows_in"], 7 * 16)
                    for half, n in ((0, 112), (1, 94)):
                        pe.transpose(ps[:, half, 0:n], rows[0:n, half, :], self.ident[0:n, 0:n]
                                     ).then_inc(s["row_turned"], 1)
                    pe.wait_ge(s["x_in"], 32)
                    for t in range(NT):
                        for g in range(2):
                            n = 2 * t + g
                            if n >= 4:
                                pe.wait_ge(s["x_out"], n - 3)
                            for c in range(4):
                                mm = pe.transpose(ps[:, 2 + n % 4, c * P:(c + 1) * P],
                                                  xin[:, t, (4 * g + c) * P:(4 * g + c + 1) * P], self.ident)
                            mm.then_inc(s["x_turned"], 1)
                    pe.wait_ge(s["cond"], 1)
                    for n in range(NW + 1):
                        if n < NW:
                            pe.wait_ge(s[f"w_in{n % SL}"], 16 * (n // SL + 1))
                            if n >= 2:
                                pe.wait_ge(s["mod_row"], n - 1)
                            for k in range(KC):
                                mm = pe.matmul(ps[0:2, n % 2, :], self.condT[:, k, :], wr[:, n % SL, k, :],
                                               start=(k == 0), stop=(k == KC - 1))
                            mm.then_inc(s["mod_mm"], 1)
                        if n:
                            pe.wait_ge(s["mod_row"], n)
                            for m in range(4):
                                o = (4 * (n - 1) + m) * 2
                                mm = pe.transpose(ps[:, 6, o:o + 2], modr[:, (n - 1) % 2, m * P:(m + 1) * P], self.ident[0:2, 0:2])
                            mm.then_inc(s["mod_col"], 1)

                @block.scalar
                def _(act):
                    act.wait_ge(s["cols_out"], 2)
                    act.activation(self.condT[:].rearrange("p k s -> p s k"),
                                   self.cols[:, 96:112].rearrange("p (s k) -> p s k", s=2),
                                   ACT.Silu).then_inc(s["cond"], 1)
                    for n in range(NW):
                        act.wait_ge(s["mod_mm"], n + 1)
                        if n >= 2:
                            act.wait_ge(s["mod_col"], n - 1)
                        act.copy(modr[:, n % 2, :], ps[0:2, n % 2, :]).then_inc(s["mod_row"], 1)

                @block.vector
                def _(dve):
                    chain = Chain(dve, s["chain"])
                    dve.wait_ge(s["row_turned"], 2)
                    dve.tensor_copy(self.cols[:, 0:112], ps[:, 0, 0:112]).then_inc(s["cols_out"], 1)
                    dve.tensor_copy(self.cols[:, 112:206], ps[:, 1, 0:94]).then_inc(s["cols_out"], 1)
                    for t in range(NT):
                        for g in range(2):
                            n = 2 * t + g
                            dve.wait_ge(s["x_turned"], n + 1)
                            dve.tensor_copy(self.xT[:, 4 * g:4 * g + 4, t * P:(t + 1) * P],
                                            ps[:, 2 + n % 4, :].rearrange("p (c t) -> p c t", c=4)
                                            ).then_inc(s["x_out"], 1)
                    dve.wait_ge(s["mod_col"], NW)
                    dve.wait_ge(s["cols_out"], 2)
                    chain(dve.tensor_tensor(self.mod[:].rearrange("p l m k s -> p (l m k) s"),
                                            ps[:, 6, 0:192].rearrange("p (a s) -> p a s", s=2),
                                            bcast_last(self.cols[:, 0:96], 2), ALU.add))
                    for l in range(DEPTH):
                        for w in range(2):
                            g0 = 112 + 16 * w + 8 * l
                            dve.scalar_tensor_tensor(
                                out=self.amul[:, l, w], in0=self.mod[:, l, 3 * w + 1], scalar=1.0,
                                in1=bcast_last(self.cols[:, g0:g0 + 8], 2), op0=ALU.add, op1=ALU.mult
                            ).then_inc(s["mod_out"], 1)

    NORM = "sq_act sq_dve summed ms root rstd scaled moved n_hi n_lo"

    def norm_programs(self, s, sq, rstd, mul, add, h=None, parts=None):
        ps, xT = self.ps, self.xT

        def act_squares(act):
            for k in range(0, KC, 2):
                act.activation(sq[:, k], xT[:, k], ACT.Square).then_inc(s["sq_act"], 1)

        def act_rest(act):
            act.wait_ge(s["ms"], 2)
            act.activation(rstd, rstd, ACT.Sqrt).then_inc(s["root"], 1)
            for k in range(KC):
                act.wait_ge(s["scaled"], k + 1)
                for j, (a, b) in enumerate(STREAMS):
                    act.activation((sq if parts else h)[:, k, a:b], sq[:, k, a:b], ACT.Identity, scale=mul(k, j),
                                   bias=add(k, j) if add else 0.0).then_inc(s["moved"], 1)
                if parts:
                    act.wait_ge(s["moved"], 2 * k + 2)
                    act.copy(parts[0][:, k], sq[:, k]).then_inc(s["n_hi"], 1)

        def dve_squares(dve):
            for k in range(1, KC, 2):
                dve.tensor_tensor(sq[:, k], xT[:, k], xT[:, k], ALU.mult).then_inc(s["sq_dve"], 1)

        def dve_rest(dve):
            dve.wait_ge(s["summed"], 1)
            for j, (a, b) in enumerate(STREAMS):
                dve.tensor_scalar(rstd[:, a:b], ps[:, j, 0:b - a], 1.0 / D, EPS, ALU.mult, ALU.add
                                  ).then_inc(s["ms"], 1)
            dve.wait_ge(s["root"], 1)
            dve.reciprocal(rstd, rstd).then_inc(s["rstd"], 1)
            dve.wait_ge(s["rstd"], 1)
            for k in range(KC + 1):
                if k < KC:
                    dve.tensor_tensor(sq[:, k], xT[:, k], rstd, ALU.mult).then_inc(s["scaled"], 1)
                if parts and k:
                    dve.wait_ge(s["n_hi"], k)
                    dve.tensor_tensor(parts[1][:, k - 1], sq[:, k - 1], parts[0][:, k - 1].bitcast(F32), ALU.subtract
                                      ).then_inc(s["n_lo"], 1)

        def pe_sums(pe):
            for k in range(KC):
                pe.wait_ge(s["sq_dve" if k % 2 else "sq_act"], k // 2 + 1)
                for j, (a, b) in enumerate(STREAMS):
                    mm = pe.matmul(ps[:, j, 0:b - a], self.ones, sq[:, k, a:b], start=(k == 0), stop=(k == KC - 1))
            mm.then_inc(s["summed"], 1)
        return act_squares, act_rest, dve_squares, dve_rest, pe_sums

    def norm(self, mul, add, h):
        nc = self.nc
        with ExitStack() as scope:
            sq = scope.enter_context(nc.sbuf_tensor(f"sq_{nc.next_id()}", [P, KC, T], F32))
            rstd = scope.enter_context(nc.sbuf_tensor(f"rstd_{nc.next_id()}", [P, T], F32))
            with stage(nc, self.NORM) as (block, s):
                act_squares, act_rest, dve_squares, dve_rest, pe_sums = self.norm_programs(s, sq, rstd[:], mul, add, h=h)

                @block.scalar
                def _(act):
                    act_squares(act)
                    act_rest(act)

                @block.vector
                def _(dve):
                    dve_squares(dve)
                    dve_rest(dve)

                @block.tensor
                def _(pe):
                    pe_sums(pe)

    def mixer(self, l):
        nc, i, ps = self.nc, self.i, self.ps
        with ExitStack() as scope:
            def sb(name, shape, dt=F32):
                return scope.enter_context(nc.sbuf_tensor(f"{name}_{l}", shape, dt))
            self.tm = sb("tm", [P, NT, TM])
            self.bg = sb("bg", [P, 2, NT, 2, HA])
            self.oA = sb("oA", [P, NT, AW])
            with ExitStack() as s2:
                def sb2(name, shape, dt=F32):
                    return s2.enter_context(nc.sbuf_tensor(f"{name}_{l}", shape, dt))
                self.qkv = sb2("qkv", [P, NT, 18, HD])
                with ExitStack() as s3:
                    hi, lo = (s3.enter_context(nc.sbuf_tensor(f"h_{n}_{l}", [P, KC, T], F32R)) for n in ("hi", "lo"))
                    self.in_proj(l, hi, lo)
                self.kqT = sb2("kqT", [P, NT, 3, 2, P])
                self.eg = sb2("eg", [P, 3, 2, NT, HA])
                self.glp = sb2("glp", [P, 2, NT, 3])
                self.delta_prep(l)
                self.delta_scan(l)
            self.mixed = sb("mixed", [P, NT, D])
            self.oC = self.oA[:, :, 0:HC * HD].rearrange("p t (h d) -> p t h d", d=HD)
            self.gdiff = sb("gdiff", [P, HD])
            self.attention(l)
            self.mhi, self.mlo = sb("mixed_hi", [P, KC, T], F32R), sb("mixed_lo", [P, KC, T], F32R)
            self.out_proj(l)

    def in_proj(self, l, hhi, hlo):
        nc, i, ps, tm = self.nc, self.i, self.ps, self.tm
        w = i["w_in"][l].rearrange("(c p) n -> p c n", p=P)
        tiles = [(0, KC, c * P, P) for c in range(9)]
        tiles += [(4 * half, 4, FM + n * TMT, TMT) for n in range(4) for half in range(2)]
        PADW = T + 4
        at = (1, 131)
        with ExitStack() as scope:
            def sb(name, shape, dt=F32):
                return scope.enter_context(nc.sbuf_tensor(f"{name}_{l}", shape, dt))
            ws = Split(self, scope, f"in_{l}", 4 * TMT, 2, 2, tiles,
                       lambda tile: [(w[:, tile[0]:tile[0] + tile[1], tile[2]:tile[2] + tile[3]], tile[1])],
                       lambda n: ("tm_mm", NT * ((n - 8) // 2)) if n > 9 and n % 2 == 0 else
                       ("w_used", n + 1 if n < 9 else 10 + (n - 9) // 2))
            pad = sb("conv_in_out", [P, 10, PADW])
            names = "tm_part tm_mm fm_act fm_dve tm_out padded chain conv silu turned qkv_out " + ws.names + " " + self.NORM
            room = pad[:].rearrange("p c n -> p (c n)")
            sq, rstd = room[:, 0:KC * T].rearrange("p (c t) -> p c t", c=KC), room[:, KC * T:(KC + 1) * T]
            with stage(nc, names) as (block, s):
                act_squares, act_rest, dve_squares, dve_rest, pe_sums = self.norm_programs(
                    s, sq, rstd, lambda c, j: self.amul[:, l, 0, c, j:j + 1], lambda c, j: self.mod[:, l, 0, c, j:j + 1],
                    parts=(hhi, hlo))

                @block.sync
                def _(sp):
                    for n in range(len(tiles)):
                        ws.load(sp, s, n)

                @block.gpsimd
                def _(pool):
                    pool.wait_ge(s["n_lo"], KC)
                    pool.memset(pad[:, :, 0:1], 0.0).then_inc(s["padded"], 1)
                    pool.memset(pad[:, :, 129:131], 0.0).then_inc(s["padded"], 1)
                    pool.memset(pad[:, :, PADW - 1:PADW], 0.0).then_inc(s["padded"], 1)

                @block.tensor
                def _(pe):
                    pe_sums(pe)
                    for c in range(9):
                        pe.wait_ge(s["w_lo"], c + 1)
                        if c >= 4:
                            pe.wait_ge(s["fm_act"], c - 3)
                            pe.wait_ge(s["fm_dve"], c - 3)
                        for k in range(KC):
                            if c == 0:
                                pe.wait_ge(s["n_lo"], k + 1)
                            for n, (wt, x) in enumerate(((ws.hi, hhi), (ws.hi, hlo), (ws.lo, hhi))):
                                for j, (a, b) in enumerate(HALVES):
                                    mm = pe.matmul(ps[:, 2 * (c % 4) + j, 0:b - a], wt[:, c % 2, k * P:(k + 1) * P], x[:, k, a:b],
                                                   start=(k == 0 and n == 0), stop=(k == KC - 1 and n == 2))
                        mm.then_inc(s["w_used"], 1)
                    pe.wait_ge(s["fm_act"], 9)
                    pe.wait_ge(s["fm_dve"], 9)
                    for tile in range(9, 17):
                        n, half = divmod(tile - 9, 2)
                        pe.wait_ge(s["w_lo"], tile + 1)
                        for t in range(NT):
                            if half == 0 and n:
                                pe.wait_ge(s["tm_out"], NT * (n - 1) + t + 1)
                            for k in range(4):
                                for m, (x, wt) in enumerate(((hhi, ws.hi), (hhi, ws.lo), (hlo, ws.hi))):
                                    mm = pe.matmul(ps[:, t, 0:TMT], x[:, 4 * half + k, t * P:(t + 1) * P],
                                                   wt[:, tile % 2, k * TMT:(k + 1) * TMT],
                                                   start=(half == 0 and k == 0 and m == 0), stop=(half == 1 and k == 3 and m == 2))
                            mm.then_inc(s["w_used" if t == NT - 1 and not half else "tm_part" if not half else "tm_mm"], 1)
                            if half:
                                c = NT * (n - 1) + t
                                if 0 <= c < 9:
                                    pe.wait_ge(s["silu"], c + 1)
                                    if c:
                                        pe.wait_ge(s["qkv_out"], c)
                                    for u in range(NT):
                                        x0 = 0 if u == 0 else 130 + (u - 1) * P
                                        mm = pe.transpose(ps[:, 5 + u // 4, (u % 4) * P:(u % 4 + 1) * P],
                                                          pad[:, c, x0:x0 + P], self.ident)
                                    mm.then_inc(s["turned"], 1)

                @block.scalar
                def _(act):
                    act_squares(act)
                    ws.split_hi(act, s, 0)
                    act_rest(act)
                    for c in range(9):
                        ws.split_hi(act, s, c + 1)
                        act.wait_ge(s["w_used"], c + 1)
                        act.copy(pad[:, c + 1, at[0]:at[0] + P], ps[:, 2 * (c % 4), 0:P])
                        act.copy(pad[:, c + 1, at[1]:at[1] + T // 2 - P], ps[:, 2 * (c % 4), P:T // 2]).then_inc(s["fm_act"], 1)
                    for q in range(20):
                        n, t = divmod(q, NT)
                        if t == 0 and 10 + 2 * n < 17:
                            ws.split_hi(act, s, 10 + 2 * n)
                        act.wait_ge(s["tm_mm"], q + 1)
                        act.copy(tm[:, t, n * TMT:(n + 1) * TMT], ps[:, t, 0:TMT]).then_inc(s["tm_out"], 1)
                        if t == 0 and 11 + 2 * n < 17:
                            ws.split_hi(act, s, 11 + 2 * n)
                        c = q - NT + 1
                        if 0 <= c < 9:
                            act.wait_ge(s["conv"], c + 1)
                            act.activation(pad[:, c, 0:PADW - 2], pad[:, c, 0:PADW - 2], ACT.Silu).then_inc(s["silu"], 1)

                @block.vector
                def _(dve):
                    chain = Chain(dve, s["chain"])
                    dve_squares(dve)
                    ws.split_lo(dve, s, 0)
                    dve_rest(dve)
                    for c in range(9):
                        ws.split_lo(dve, s, c + 1)
                        dve.wait_ge(s["w_used"], c + 1)
                        dve.tensor_copy(pad[:, c + 1, at[1] + T // 2 - P:at[1] + 4 * P], ps[:, 2 * (c % 4) + 1, 0:T // 2]
                                        ).then_inc(s["fm_dve"], 1)
                    dve.wait_ge(s["padded"], 3)
                    dve.wait_ge(s["fm_act"], 9)
                    dve.wait_ge(s["fm_dve"], 9)

                    def convolve(c):
                        tap = [self.cols[:, 112 + 40 + (l * 3 + u) * 9 + c:][:, 0:1] for u in range(3)]
                        x, y = pad[:, c + 1], pad[:, c, 0:PADW - 2]
                        if c:
                            dve.wait_ge(s["conv"], c)
                        chain(dve.tensor_scalar(y, x[:, 0:PADW - 2], tap[0], None, ALU.mult))
                        chain(dve.scalar_tensor_tensor(out=y, in0=x[:, 1:PADW - 1], scalar=tap[1], in1=y,
                                                       op0=ALU.mult, op1=ALU.add))
                        dve.scalar_tensor_tensor(out=y, in0=x[:, 2:PADW], scalar=tap[2], in1=y,
                                                 op0=ALU.mult, op1=ALU.add).then_inc(s["conv"], 1)
                    ws.split_lo(dve, s, 10)
                    convolve(0)
                    convolve(1)
                    ws.split_lo(dve, s, 11)
                    ws.split_lo(dve, s, 12)
                    for c in range(9):
                        dve.wait_ge(s["turned"], c + 1)
                        b0 = 5
                        dve.tensor_copy(self.qkv[:, 0:NT, 2 * c:2 * c + 2, :].rearrange("p t h d -> p t (h d)"),
                                        ps[:, b0:b0 + 2, :].rearrange("p b (t d) -> p (b t) d", t=4)[:, 0:NT, :]
                                        ).then_inc(s["qkv_out"], 1)
                        if c + 2 < 9:
                            convolve(c + 2)
                        if c in (0, 4):
                            ws.split_lo(dve, s, 13 if c == 0 else 14)
                        if c in (5, 8):
                            ws.split_lo(dve, s, 15 if c == 5 else 16)

    def delta_prep(self, l):
        nc, i, ps, tm, qkv, bg = self.nc, self.i, self.ps, self.tm, self.qkv, self.bg
        with ExitStack() as scope:
            def sb(name, shape, dt=F32):
                return scope.enter_context(nc.sbuf_tensor(f"{name}_{l}", shape, dt))
            sq = sb("qk_sq", [P, NT, 12, HD])
            r = sb("qk_r", [P, NT, 12])
            ab = sb("a_log_dt", [P, 2, 2, HA])
            e1 = sb("e1", [P, NT, 2, HA])
            e2 = sb("e2", [P, NT, 2, HA])
            na = sb("na", [P, 12])
            with stage(nc, "par_in chain expd lnd neg g_done rooted qk_done turned kq_out cum eg_out half") as (block, s):
                @block.sync
                def _(sp):
                    for j, name in enumerate(("dn_a_log", "dn_dt_bias")):
                        sp.dma_start(ab[:, j], i[name][l].partition_broadcast(P)).then_inc(s["par_in"], 16)

                braw = tm[:, :, BE0:BE0 + 12]
                araw = tm[:, :, AR0:AR0 + 12]
                e1f = e1[:].rearrange("p t d h -> p t (d h)")
                e2f = e2[:].rearrange("p t d h -> p t (d h)")
                beta = bg[:, 0].rearrange("p t d h -> p t (d h)")
                g = bg[:, 1].rearrange("p t d h -> p t (d h)")
                abf = ab[:].rearrange("p j d h -> p j (d h)")

                @block.vector
                def _(dve):
                    chain = Chain(dve, s["chain"])
                    dve.wait_ge(s["par_in"], 32)
                    chain(dve.tensor_tensor(g, araw, bcast_mid(abf[:, 1], NT), ALU.add))
                    chain(dve.tensor_scalar(e2f, g, -1.0, None, ALU.mult))
                    dve.tensor_tensor(e2f, e2f, g, ALU.min).then_inc(s["neg"], 1)
                    dve.wait_ge(s["neg"], 1)
                    chain(dve.tensor_scalar(g, g, 0.0, None, ALU.max))
                    dve.wait_ge(s["expd"], 3)
                    chain(dve.tensor_scalar(e1f, e1f, 1.0, None, ALU.add))
                    chain(dve.reciprocal(beta, e1f))
                    dve.tensor_scalar(e2f, e2f, 1.0, None, ALU.add).then_inc(s["neg"], 1)
                    chain(dve.tensor_scalar(na[:], na[:], -1.0, None, ALU.mult))
                    dve.wait_ge(s["lnd"], 1)
                    chain(dve.tensor_tensor(g, g, e2f, ALU.add))
                    dve.tensor_tensor(g, g, bcast_mid(na[:], NT), ALU.mult).then_inc(s["g_done"], 1)
                    chain(dve.tensor_tensor(sq[:], qkv[:, :, 0:12, :], qkv[:, :, 0:12, :], ALU.mult))
                    chain(dve.tensor_reduce(r[:], sq[:], AX.X, ALU.add))
                    dve.tensor_scalar(r[:], r[:], EPS, None, ALU.add).then_inc(s["neg"], 1)
                    dve.wait_ge(s["rooted"], 1)
                    chain(dve.reciprocal(r[:], r[:]))
                    chain(dve.tensor_scalar(r[:, :, 0:HA], r[:, :, 0:HA], HD ** -0.5, None, ALU.mult))
                    for t in range(NT):
                        dve.tensor_tensor(qkv[:, t, 0:12, :], qkv[:, t, 0:12, :], bcast_last(r[:, t, :], HD),
                                          ALU.mult).then_inc(s["qk_done"], 1)
                    for t in range(NT):
                        dve.wait_ge(s["turned"], t + 1)
                        b0 = 2 * (t % 2)
                        dve.tensor_copy(self.kqT[:, t].rearrange("p h j n -> p (h j) n"),
                                        ps[:, b0:b0 + 2, :].rearrange("p b (t d) -> p (b t) d", t=4)[:, 0:6, :]
                                        ).then_inc(s["kq_out"], 1)
                    dve.wait_ge(s["eg_out"], 1)
                    for j in range(2):
                        dve.tensor_copy(self.glp[64 * j:64 * j + 64].rearrange("p d t h -> p (d t) h"),
                                        self.eg[64 * j:64 * j + 64, 2].rearrange("p d t (h j) -> p (d t) h j", j=2)
                                        [:, :, :, j]).then_inc(s["half"], 1)

                @block.scalar
                def _(act):
                    act.wait_ge(s["par_in"], 32)
                    act.activation(e1f, braw, ACT.Exp, scale=-1.0).then_inc(s["expd"], 1)
                    act.activation(na[:], abf[:, 0], ACT.Exp).then_inc(s["expd"], 1)
                    act.wait_ge(s["neg"], 1)
                    act.activation(e2f, e2f, ACT.Exp).then_inc(s["expd"], 1)
                    act.wait_ge(s["neg"], 2)
                    act.activation(e2f, e2f, ACT.Ln).then_inc(s["lnd"], 1)
                    act.wait_ge(s["cum"], 1)
                    act.activation(self.eg[:].rearrange("p k d t h -> p (k d t h)"), ps[:, 4, 0:180], ACT.Exp
                                   ).then_inc(s["eg_out"], 1)
                    act.wait_ge(s["neg"], 3)
                    act.activation(r[:], r[:], ACT.Sqrt).then_inc(s["rooted"], 1)

                @block.tensor
                def _(pe):
                    pe.wait_ge(s["g_done"], 1)
                    for k, table in enumerate((C_U, C_SL, None)):
                        for d in range(2):
                            o = (2 * k + d) * NT * HA
                            lhsT = self.ones if table is None else self.c(table + d)
                            mm = pe.matmul(ps[:, 4, o:o + NT * HA], lhsT, bg[:, 1, :, d, :], start=True, stop=True)
                    mm.then_inc(s["cum"], 1)
                    for t in range(NT):
                        pe.wait_ge(s["qk_done"], t + 1)
                        if t >= 2:
                            pe.wait_ge(s["kq_out"], t - 1)
                        for pr in range(3):
                            for j, h0 in enumerate((HA, 0)):
                                n = 2 * pr + j
                                mm = pe.transpose(ps[:, 2 * (t % 2) + n // 4, (n % 4) * P:(n % 4 + 1) * P],
                                                  qkv[:, t, h0 + 2 * pr:h0 + 2 * pr + 2, :], self.ident)
                        mm.then_inc(s["turned"], 1)

    def delta_scan(self, l):
        nc, i, ps, qkv, bg = self.nc, self.i, self.ps, self.qkv, self.bg
        kqT, eg = self.kqT, self.eg
        W = HA * P
        with ExitStack() as scope:
            def sb(name, shape, dt=F32):
                return scope.enter_context(nc.sbuf_tensor(f"{name}_{l}", shape, dt))
            XT = sb("XT", [P, NT, 2, HA, P])
            AT = sb("AT", [P, NT, 2, HA, P])
            with ExitStack() as inner:
                def sbi(name, shape, dt=F32):
                    return inner.enter_context(nc.sbuf_tensor(f"{name}_{l}", shape, dt))
                MT = sbi("MT", [P, 2, 2, HA, P])
                G, DD = (self.oA[:].rearrange("p t n -> p (t n)")[:, u * W:(u + 1) * W].rearrange("p (h n) -> p h n", h=HA)
                         for u in range(2))
                DT = sbi("M_level", [P, 2, HA, P])
                Y = sbi("Y", [P, 2, HA, P])
                X = sbi("X", [P, 2, HA, P])
                L = NLEV - 1
                with stage(nc, "gu dm dexp kq kq_out mt xt0 ms y y_out p xt xturn x_out chain") as (block, s):
                    def region(n):
                        return ps[:, 2 * n:2 * n + 2, :].rearrange("p b n -> p (b n)")[:, 0:W]
                    in_x, in_y, in_p, forming = (region(0), region(1)), (region(2), region(0)), (region(1), region(2)), region(3)

                    def head(ap, h):
                        return ap[:, h * P:(h + 1) * P]

                    def flat(ap):
                        return ap.rearrange("p h n -> p (h n)")

                    @block.tensor
                    def _(pe):
                        def kk(t, par):
                            if par:
                                pe.wait_ge(s["kq_out"], 4 * t + 2)
                            elif t:
                                pe.wait_ge(s["dexp"], 2 * t)
                            for i_ in range(3):
                                q = 64 * par
                                mm = pe.matmul(forming[:, 256 * i_:256 * i_ + 256], kqT[q:q + 64, t, i_, 0, :],
                                               kqT[q:q + 64, t, i_, :, :], start=True, stop=True)
                            mm.then_inc(s["kq"], 1)

                        def decay(t, d):
                            pe.wait_ge(s["gu"], 2 * t + d + 1)
                            if d:
                                pe.wait_ge(s["dexp"], 2 * t + 1)
                            else:
                                pe.wait_ge(s["kq_out"], 4 * t + 4)
                            for c0, c1 in ((0, 512), (512, W)):
                                mm = pe.matmul(forming[:, c0:c1], self.c(C_SL + d), flat(G)[:, c0:c1], start=True, stop=True)
                            mm.then_inc(s["dm"], 1)
                        for par in range(2):
                            kk(0, par)
                        for d in range(2):
                            decay(0, d)
                        for t in range(NT):
                            for lev in range(NLEV):
                                n = t * L + lev - 1
                                if lev:
                                    for d in range(2):
                                        pe.wait_ge(s["ms"], 2 * n + d + 1)
                                        pe.wait_ge(s["x_out"], 2 * n + d + 1)
                                        for h in range(HA):
                                            mm = pe.matmul(head(in_y[d], h), DT[:, d, h], X[:, d, h], start=True, stop=True)
                                        mm.then_inc(s["y"], 1)
                                    for d in range(2):
                                        pe.wait_ge(s["y_out"], 2 * n + d + 1)
                                        for h in range(HA):
                                            mm = pe.matmul(head(in_p[d], h), Y[:, d, h], XT[:, t, d, h], start=True, stop=True)
                                        mm.then_inc(s["p"], 1)
                                elif t:
                                    pe.wait_ge(s["xt"], 2 * t * L)
                                if t + 1 < NT and lev in (1, 2):
                                    kk(t + 1, lev - 1)
                                if t + 1 < NT and lev in (3, 4):
                                    decay(t + 1, lev - 3)
                                if lev < NLEV - 1:
                                    for d in range(2):
                                        if lev:
                                            pe.wait_ge(s["xt"], 2 * n + d + 1)
                                        else:
                                            pe.wait_ge(s["xt0"], 2 * t + d + 1)
                                        for h in range(HA):
                                            mm = pe.transpose(head(in_x[d], h), XT[:, t, d, h], self.ident)
                                        mm.then_inc(s["xturn"], 1)

                    @block.scalar
                    def _(act):
                        def kq_copy(t, par):
                            act.wait_ge(s["kq"], 2 * t + par + 1)
                            if t >= 2:
                                act.wait_ge(s["ms"], 2 * L * (t - 1))
                            for j, dst in enumerate((MT[:, t % 2, 1], AT[:, t, 1])):
                                act.copy(dst[:, par:HA:2], forming.rearrange("p (i j n) -> p j i n", i=3, j=2)[:, j]
                                         ).then_inc(s["kq_out"], 1)

                        def decay_exp(t, d):
                            act.wait_ge(s["dm"], 2 * t + d + 1)
                            if 2 * t + d:
                                act.wait_ge(s["mt"], 2 * t + d)
                            act.activation(flat(DD), forming, ACT.Exp).then_inc(s["dexp"], 1)
                        for par in range(2):
                            kq_copy(0, par)
                        for d in range(2):
                            decay_exp(0, d)
                        for t in range(NT):
                            for lev in range(NLEV):
                                n = t * L + lev - 1
                                if lev:
                                    for d in range(2):
                                        act.wait_ge(s["y"], 2 * n + d + 1)
                                        act.copy(flat(Y[:, d]), in_y[d]).then_inc(s["y_out"], 1)
                                if lev < NLEV - 1:
                                    for d in range(2):
                                        act.wait_ge(s["xturn"], 2 * (n + 1) + d + 1)
                                        act.copy(flat(X[:, d]), in_x[d]).then_inc(s["x_out"], 1)
                                if t + 1 < NT and lev in (1, 2):
                                    kq_copy(t + 1, lev - 1)
                                if t + 1 < NT and lev in (3, 4):
                                    decay_exp(t + 1, lev - 3)

                    @block.gpsimd
                    def _(pool):
                        for t in range(NT):
                            for lev in range(1, NLEV):
                                n = t * L + lev - 1
                                for d in range(2):
                                    if lev == 1:
                                        pool.wait_ge(s["xt0"], 2 * t + d + 1)
                                    if n:
                                        pool.wait_ge(s["y"], 2 * (n - 1) + d + 1)
                                    pool.tensor_tensor(DT[:, d], MT[:, t % 2, d], bcast_mid(self.c(C_LV + d * NLEV + lev), HA),
                                                       ALU.mult).then_inc(s["ms"], 1)

                    @block.vector
                    def _(dve):
                        chain = Chain(dve, s["chain"])

                        def log_decay(t, d):
                            if 2 * t + d:
                                dve.wait_ge(s["dm"], 2 * t + d)
                            dve.tensor_tensor(G, bcast_mid(self.c(C_U + d), HA), bcast_last(bg[:, 1, t, d, :], P), ALU.mult
                                              ).then_inc(s["gu"], 1)

                        def form(t, d):
                            m = MT[:, t % 2, d]
                            dve.wait_ge(s["dexp"], 2 * t + d + 1)
                            dve.wait_ge(s["kq_out"], 4 * t + 4)
                            if t >= 2:
                                dve.wait_ge(s["ms"], 2 * L * (t - 1))
                            chain(dve.tensor_tensor(DD, DD, bcast_mid(self.c(C_U + d), HA), ALU.mult))
                            chain(dve.tensor_tensor(AT[:, t, d], AT[:, t, 1], DD, ALU.mult))
                            chain(dve.tensor_tensor(m, MT[:, t % 2, 1], DD, ALU.mult))
                            dve.tensor_tensor(m, m, bcast_last(bg[:, 0, t, d, :], P), ALU.mult).then_inc(s["mt"], 1)
                            dve.wait_ge(s["mt"], 2 * t + d + 1)
                            chain(dve.tensor_tensor(XT[:, t, d], m, bcast_mid(self.c(C_LV + d * NLEV), HA), ALU.mult))
                            dve.tensor_tensor(XT[:, t, d], bcast_mid(self.ident, HA), XT[:, t, d], ALU.subtract
                                              ).then_inc(s["xt0"], 1)
                        log_decay(0, 0)
                        log_decay(0, 1)
                        form(0, 0)
                        form(0, 1)
                        for t in range(NT):
                            for lev in range(1, NLEV):
                                n = t * L + lev - 1
                                for d in range(2):
                                    dve.wait_ge(s["p"], 2 * n + d + 1)
                                    if lev == 1:
                                        dve.wait_ge(s["xt0"], 2 * t + d + 1)
                                    else:
                                        dve.wait_ge(s["xt"], 2 * (n - 1) + d + 1)
                                    dve.tensor_tensor(flat(XT[:, t, d]), flat(XT[:, t, d]), in_p[d], ALU.subtract
                                                      ).then_inc(s["xt"], 1)
                                if t + 1 < NT:
                                    if lev in (2, 3):
                                        log_decay(t + 1, lev - 2)
                                    if lev in (4, 5):
                                        form(t + 1, lev - 4)
            S = sb("S", [P, 2, 2, 3, 2 * HD])
            kd_b = sb("kd", [P, NT, HA, HD])
            kd = [qkv[:, :, 0:HA, :], kd_b[:]]
            tk = sb("tk", [P, 2, HA, HD])
            t1 = sb("t1", [P, 2, HA, HD])
            vn = sb("vn", [P, 2, HA, HD])
            tq = sb("tq", [P, 2, HA, HD])
            o = self.oA
            steps = [(0, 0, 0), (0, 0, 1)]
            for n in range(4):
                steps += [(1, 1 + n, 0), (1, 4 - n, 1)]
            names = "s_in s_zero kd o_zero ks t1 xt1 vn av s_new o_sum s_out chain sdec used"
            with stage(nc, names) as (block, s):
                @block.sync
                def _(sp):
                    sp.wait_ge(s["s_zero"], 1)
                    for d in range(2):
                        for j in range(2):
                            sp.dma_start(S[64 * j:64 * j + 64, 1, d, :, HD * j:HD * j + HD], i["state_delta"][0, l, d].rearrange(
                                "(h j) k v -> j k h v", j=2)[j]).then_inc(s["s_in"], 16)
                    for d in range(2):
                        sp.wait_ge(s["s_new"], 2 * d + 2)
                        for j in range(2):
                            sp.dma_start(self.o["state"][0, l, d].rearrange("(h j) k v -> j k h v", j=2)[j],
                                         S[64 * j:64 * j + 64, 0, d, :, HD * j:HD * j + HD]).then_inc(s["s_out"], 16)
                    sp.wait_ge(s["s_out"], 64)

                @block.gpsimd
                def _(pool):
                    pool.memset(S[:], 0.0).then_inc(s["s_zero"], 1)
                    for n, (st, t, d) in enumerate(steps):
                        pool.tensor_tensor(kd[d][:, t], qkv[:, t, HA:2 * HA, :], bcast_last(eg[:, 1, d, t, :], HD),
                                           ALU.mult).then_inc(s["kd"], 1)

                def bank(n, k, w=HA * HD):
                    return ps[:, 4 * (n % 2) + k, 0:w]

                @block.tensor
                def _(pe):
                    def read_state(n):
                        st, t, d = steps[n]
                        if n == 0:
                            pe.wait_ge(s["s_zero"], 1)
                        elif n == 2:
                            pe.wait_ge(s["s_in"], 64)
                        if n >= 4:
                            pe.wait_ge(s["s_new"], 2 * (n - 1))
                        if n >= 2:
                            pe.wait_ge(s["o_sum"], n - 1)
                        for j in range(2):
                            for i_ in range(3):
                                mm = pe.matmul(bank(n, j)[:, i_ * P:(i_ + 1) * P], kqT[:, t, i_, j, :], S[:, st, d, i_],
                                               start=True, stop=True)
                        mm.then_inc(s["ks"], 1)
                    for n0 in range(0, len(steps), 2):
                        for n in (n0, n0 + 1):
                            read_state(n)
                        for n in (n0, n0 + 1):
                            st, t, d = steps[n]
                            pe.wait_ge(s["t1"], n + 1)
                            for h in range(HA):
                                mm = pe.matmul(bank(n, 2)[:, h * HD:(h + 1) * HD], XT[:, t, d, h], t1[:, d, h],
                                               start=True, stop=True)
                            mm.then_inc(s["xt1"], 1)
                        for n in (n0, n0 + 1):
                            st, t, d = steps[n]
                            pe.wait_ge(s["vn"], n + 1)
                            pe.wait_ge(s["kd"], n + 1)
                            for i_ in range(3):
                                pe.matmul(bank(n, 3)[:, i_ * P:(i_ + 1) * P],
                                          kd[d][:, t, 2 * i_:2 * i_ + 2].rearrange("p h d -> p (h d)"),
                                          vn[:, d, 2 * i_:2 * i_ + 2].rearrange("p h d -> p (h d)"), start=True, stop=True)
                            for h in range(HA):
                                mm = pe.matmul(bank(n, 2)[:, h * HD:(h + 1) * HD], AT[:, t, d, h], vn[:, d, h],
                                               start=True, stop=True)
                            mm.then_inc(s["av"], 1)

                @block.vector
                def _(dve):
                    chain = Chain(dve, s["chain"])

                    def v3(ap):
                        return ap.rearrange("p (h d) -> p h d", d=HD)

                    for n0 in range(0, len(steps), 2):
                        for n in (n0, n0 + 1):
                            st, t, d = steps[n]
                            dve.wait_ge(s["ks"], n + 1)
                            chain(dve.tensor_tensor(tk[:, d], v3(bank(n, 0)), bcast_last(eg[:, 0, d, t, :], HD), ALU.mult))
                            dve.tensor_tensor(t1[:, d], qkv[:, t, 2 * HA:3 * HA, :], tk[:, d], ALU.subtract
                                              ).then_inc(s["t1"], 1)
                        for n in (n0, n0 + 1):
                            st, t, d = steps[n]
                            dve.tensor_tensor(tq[:, d], v3(bank(n, 1)), bcast_last(eg[:, 0, d, t, :], HD), ALU.mult
                                              ).then_inc(s["used"], 1)
                            dve.tensor_tensor(S[:, st, d], S[:, st, d], bcast_last(self.glp[:, d, t, :], 2 * HD), ALU.mult
                                              ).then_inc(s["sdec"], 1)
                        for n in (n0, n0 + 1):
                            st, t, d = steps[n]
                            dve.wait_ge(s["xt1"], n + 1)
                            dve.tensor_tensor(vn[:, d], v3(bank(n, 2)), bcast_last(bg[:, 0, t, d, :], HD), ALU.mult
                                              ).then_inc(s["vn"], 1)
                        for n in (n0, n0 + 1):
                            st, t, d = steps[n]
                            dve.wait_ge(s["used"], n + 1)
                            ot = o[:, t, 0:AW]
                            if n < 2:
                                first = d == 0
                            else:
                                first = n0 < 6
                            if not first:
                                chain(dve.tensor_tensor(ot, ot, tq[:, d].rearrange("p h d -> p (h d)"), ALU.add))
                            dve.wait_ge(s["av"], n + 1)
                            dve.wait_ge(s["sdec"], n + 1)
                            for j in range(2):
                                q = slice(HD * j, HD * j + HD)
                                dve.tensor_tensor(S[q, st, d, :, q], S[q, st, d, :, q],
                                                  bank(n, 3)[q].rearrange("p (i v) -> p i v", i=3)[:, :, q], ALU.add
                                                  ).then_inc(s["s_new"], 1)
                            if first:
                                dve.tensor_tensor(ot, bank(n, 2), tq[:, d].rearrange("p h d -> p (h d)"), ALU.add
                                                  ).then_inc(s["o_sum"], 1)
                            else:
                                dve.tensor_tensor(ot, bank(n, 2), ot, ALU.add).then_inc(s["o_sum"], 1)
                            dve.wait_ge(s["o_sum"], n + 1)
                            dve.wait_ge(s["s_new"], 2 * n + 2)

    def attention(self, l):
        nc, i, ps, tm, mixed, oC, gdiff = self.nc, self.i, self.ps, self.tm, self.mixed, self.oC, self.gdiff
        lam_init = 0.8 - 0.6 * math.exp(-0.3 * l)
        NK = KEYS // P
        NC2 = 2 * HC
        V1 = HD + 1
        RB, RC = HD, 3 * DHC
        with ExitStack() as scope:
            def sb(name, shape, dt=F32):
                return scope.enter_context(nc.sbuf_tensor(f"{name}_{l}", shape, dt))
            qB = sb("qB", [P, HB, T], F32R)
            kB = sb("kB", [P, KVB, KEYS], F32R)
            kBlo = sb("kB_lo", [P, KVB, KEYS], F32R)
            qC = sb("qC", [P, NC2, T], F32R)
            kC = sb("kC", [P, NC2, KEYS], F32R)
            vB = sb("vB", [P, NK, KVB, V1])
            vC = sb("vC", [P, NK, HC, V1])
            nlam = sb("nlam", [P, 1])
            with ExitStack() as inner:
                def sbi(name, shape, dt=F32):
                    return inner.enter_context(nc.sbuf_tensor(f"{name}_{l}", shape, dt))
                sq = mixed[:, :, AW:AW + 8 * HD].rearrange("p t (h d) -> p t h d", d=HD)
                r = sbi("n_r", [P, NT, 8])
                ro = sbi("n_ro", [P, NT, HA])
                gqk = sbi("gqk", [P, 8, HD])
                gdn = sbi("gdn", [P, HD])
                ta, tb = mixed[:, 0, AW:AW + 512], mixed[:, 1, AW:AW + 512]
                rope = sbi("rope", [P, 4, 192])
                ckB = sbi("ckB", [P, 2, KVB * HD])
                ckC = sbi("ckC", [P, 2, HC * HD])
                lv = sbi("lv", [P, 4, DHC])
                lp = sbi("lp", [P, 2, DHC])
                ls = sbi("ls", [P, 2])
                sqB = sbi("split_qB", [P, HB, 2, HD], F32R)
                skB = sbi("split_kB", [P, KVB, 2, HD], F32R)
                slB = sbi("split_lB", [P, KVB, HD + 2], F32R)
                sqC = sbi("split_qC", [P, NC2, 3, DHC], F32R)
                skC = sbi("split_kC", [P, NC2, 3 * DHC + 2], F32R)
                items = [("cache", 0), ("cache", 1)] + [("new", t) for t in range(NT)]

                def source(item, kind):
                    what, t = item
                    d = (HD, DHC)[kind]
                    if what == "cache":
                        q, k = None, (ckB, ckC)[kind][:, t]
                    elif kind == 0:
                        q, k = tm[:, t, QB0:KB0], tm[:, t, KB0:VB0]
                    else:
                        q, k = tm[:, t, QC0:KCC0], tm[:, t, KCC0:VC0]
                    return [a if a is None else a.rearrange("p (h d) -> p h d", d=d) for a in (q, k)]

                def key0(item):
                    what, t = item
                    return P * (1 + t) if what == "cache" else 0 if t == 0 else P + PAST + (t - 1) * P
                names = ("par_in cache_in chain ms root gate silu normed roped ctx_out lsum lexp ones v_in inv gated hi lo "
                         "turned t_out")
                with stage(nc, names) as (block, s):
                    @block.sync
                    def _(sp):
                        for h in range(HB):
                            sp.dma_start(gqk[:, h], i["gqa_q_norm"][l].partition_broadcast(P)).then_inc(s["par_in"], 16)
                        for h in range(KVB):
                            sp.dma_start(gqk[:, HB + h], i["gqa_k_norm"][l].partition_broadcast(P)).then_inc(s["par_in"], 16)
                        sp.dma_start(gdn[:], i["dn_norm"][l].partition_broadcast(P)).then_inc(s["par_in"], 16)
                        sp.dma_start(gdiff[:], i["diff_norm"][l].partition_broadcast(P)).then_inc(s["par_in"], 16)
                        sp.dma_start(lv[:], i["diff_lambda"][l].partition_broadcast(P)).then_inc(s["par_in"], 16)
                        sp.dma_start(ckB[:], i["cache_gqa_k"][0, l].rearrange("(t p) h d -> p t (h d)", p=P)).then_inc(s["cache_in"], 16)
                        sp.dma_start(ckC[:], i["cache_diff_k"][0, l].rearrange("(t p) h m d -> p t (h m d)", p=P)).then_inc(s["cache_in"], 16)
                        sp.dma_start(rope[:], i["rope"]).then_inc(s["par_in"], 16)
                        for u in range(2):
                            sp.dma_start(vB[:, 1 + u, :, 0:HD], i["cache_gqa_v"][0, l, u * P:(u + 1) * P]).then_inc(s["cache_in"], 16)
                            sp.dma_start(vC[:, 1 + u, :, 0:HD], i["cache_diff_v"][0, l, u * P:(u + 1) * P]).then_inc(s["cache_in"], 16)
                        for name, c0, n, pat in (("gv", VB0, KVB * HD, "t h d -> t (h d)"), ("dk", KCC0, HC * HD, "t h m d -> t (h m d)"),
                                                 ("dv", VC0, HC * HD, "t h d -> t (h d)")):
                            sp.dma_start(self.o[name][0, l].rearrange(pat), tm[:, 0, c0:c0 + n]).then_inc(s["ctx_out"], 16)
                        sp.wait_ge(s["normed"], 1)
                        sp.dma_start(self.o["gk"][0, l].rearrange("t h d -> t (h d)"), tm[:, 0, KB0:VB0]).then_inc(s["ctx_out"], 16)
                        sp.wait_ge(s["ctx_out"], 64)
                        sp.wait_ge(s["cache_in"], 96)

                    qk = tm[:, :, QB0:VB0].rearrange("p t (h d) -> p t h d", d=HD)
                    oA = self.oA[:].rearrange("p t (h d) -> p t h d", d=HD)

                    @block.gpsimd
                    def _(pool):
                        for a in (slB[:, :, HD:HD + 2], skC[:, :, RC:RC + 2]):
                            pool.memset(a.bitcast(F32), 1.0).then_inc(s["ones"], 1)
                        for v, c0, n in ((vB, VB0, KVB), (vC, VC0, HC)):
                            pool.memset(v[:, :, :, HD:V1], 1.0).then_inc(s["v_in"], 1)
                            for t in range(NT):
                                kt = 0 if t == 0 else t + 2
                                pool.tensor_copy(v[:, kt, :, 0:HD], tm[:, t, c0:c0 + n * HD].rearrange("p (h d) -> p h d", d=HD)
                                                 ).then_inc(s["v_in"], 1)
                        pool.wait_ge(s["par_in"], 12 * 16)
                        pool.wait_ge(s["inv"], 1)
                        pool.wait_ge(s["silu"], 1)
                        gated = Chain(pool, s["gated"])
                        for t in range(NT):
                            gated(pool.tensor_tensor(oA[:, t], oA[:, t], bcast_last(ro[:, t, :], HD), ALU.mult))
                            gated(pool.tensor_tensor(oA[:, t], oA[:, t], bcast_mid(gdn[:], HA), ALU.mult))
                            gated(pool.tensor_tensor(mixed[:, t, 0:AW], self.oA[:, t], tm[:, t, Z0:Z0 + AW], ALU.mult))

                    @block.vector
                    def _(dve):
                        chain = Chain(dve, s["chain"])

                        def split_lo(n):
                            for kind, (sq_, sk_hi, sk_lo) in enumerate((
                                    (sqB[:, :, 1], skB[:, :, 0], slB[:, :, 0:HD]),
                                    (sqC[:, :, 1], skC[:, :, 0:DHC], skC[:, :, 2 * DHC:3 * DHC]))):
                                q, k = source(items[n], kind)
                                dve.wait_ge(s["hi"], 2 * n + kind + 1)
                                last = dve.tensor_tensor(sk_lo, k, sk_hi.bitcast(F32), ALU.subtract)
                                if q is not None:
                                    q_hi = (sqB[:, :, 0], sqC[:, :, 0])[kind]
                                    last = dve.tensor_tensor(sq_, q, q_hi.bitcast(F32), ALU.subtract)
                                last.then_inc(s["lo"], 1)
                        dve.wait_ge(s["par_in"], 12 * 16)
                        chain(dve.tensor_tensor(sq[:], qk, qk, ALU.mult))
                        chain(dve.tensor_reduce(r[:], sq[:], AX.X, ALU.add))
                        dve.tensor_scalar(r[:], r[:], 1.0 / HD, EPS, ALU.mult, ALU.add).then_inc(s["ms"], 1)
                        dve.wait_ge(s["ms"], 1)
                        chain(dve.tensor_tensor(sq[:, :, 0:HA], oA, oA, ALU.mult))
                        chain(dve.tensor_reduce(ro[:], sq[:, :, 0:HA], AX.X, ALU.add))
                        dve.tensor_scalar(ro[:], ro[:], 1.0 / HD, EPS, ALU.mult, ALU.add).then_inc(s["ms"], 1)
                        for j in range(2):
                            chain(dve.tensor_tensor(lp[:, j], lv[:, 2 * j], lv[:, 2 * j + 1], ALU.mult))
                        dve.tensor_reduce(ls[:], lp[:], AX.X, ALU.add).then_inc(s["lsum"], 1)
                        dve.wait_ge(s["cache_in"], 96)
                        dve.wait_ge(s["root"], 2)
                        chain(dve.reciprocal(r[:], r[:]))
                        dve.reciprocal(ro[:], ro[:]).then_inc(s["inv"], 1)
                        split_lo(0)
                        for t in range(NT):
                            chain(dve.tensor_tensor(qk[:, t], qk[:, t], bcast_last(r[:, t, :], HD), ALU.mult))
                            dve.tensor_tensor(qk[:, t], qk[:, t], gqk[:], ALU.mult).then_inc(s["normed"], 1)
                            dve.wait_ge(s["normed"], t + 1)
                            for kind, (x0, hd, tab) in enumerate(((QB0, HD, 0), (QC0, DHC, 128)) if t else ()):
                                nh, nf = 512 // hd, hd // 4
                                x = tm[:, t, x0:x0 + 512]
                                cos = rope[:, t - 1, tab:tab + hd]
                                sin = rope[:, t - 1, tab + hd:tab + 2 * hd]

                                def quarters(ap, h):
                                    return ap.rearrange("p (n a h f) -> p n a h f", a=2, h=2, f=nf)[:, :, :, h, :]
                                dve.tensor_tensor(ta.rearrange("p (n d) -> p n d", d=hd), x.rearrange("p (n d) -> p n d", d=hd),
                                                  bcast_mid(cos, nh), ALU.mult).then_inc(s["gate"], 1)
                                for half in range(2):
                                    sn = sin.rearrange("p (a h f) -> p a h f", a=2, h=2)[:, :, half, :]
                                    dve.tensor_tensor(quarters(tb, half), quarters(x, 1 - half),
                                                      sn.unsqueeze(1).to_broadcast([P, nh, 2, nf]), ALU.mult).then_inc(s["gate"], 1)
                                dve.wait_ge(s["gate"], 6 * (t - 1) + 3 * kind + 3)
                                dve.tensor_tensor(x, ta, tb, ALU.add).then_inc(s["roped"], 1)
                                dve.wait_ge(s["roped"], 2 * (t - 1) + kind + 1)
                            split_lo(t + 1)
                        split_lo(NT + 1)
                        dve.wait_ge(s["lexp"], 1)
                        chain(dve.tensor_tensor(nlam[:], ls[:, 1:2], ls[:, 0:1], ALU.subtract))
                        chain(dve.tensor_scalar(nlam[:], nlam[:], -lam_init, None, ALU.add))
                        chain(dve.tensor_scalar(gdiff[:], gdiff[:], 1.0 - lam_init, None, ALU.mult))

                    @block.scalar
                    def _(act):
                        def split_hi(n):
                            what, t = items[n]
                            if what == "new":
                                act.wait_ge(s["roped" if t else "normed"], 2 * t if t else 1)
                            for kind, (sq_, sk_) in enumerate((
                                    (sqB[:, :, 0].unsqueeze(2), skB[:]),
                                    (sqC[:, :, 0:3:2], skC[:, :, 0:2 * DHC].rearrange("p h (u d) -> p h u d", u=2)))):
                                q, k = source(items[n], kind)
                                if n:
                                    act.wait_ge(s["turned"], 2 * (n - 1) + kind + 1)
                                last = act.copy(sk_, k.unsqueeze(2).to_broadcast(sk_.shape))
                                if q is not None:
                                    last = act.copy(sq_, q.unsqueeze(2).to_broadcast(sq_.shape))
                                last.then_inc(s["hi"], 1)

                        def evac(n):
                            what, t = items[n]
                            k0 = key0(items[n])
                            bank = [ps[:, b, :].rearrange("p (n q) -> p n q", q=P) for b in range(7)]
                            act.wait_ge(s["turned"], 2 * n + 1)
                            if what == "new":
                                act.copy(qB[:, 0:4, t * P:(t + 1) * P], bank[0])
                                act.copy(qB[:, 4:6, t * P:(t + 1) * P], bank[1][:, 0:2])
                            act.copy(kB[:, :, k0:k0 + P], bank[1][:, 2:4])
                            act.copy(kBlo[0:HD + 2, :, k0:k0 + P], bank[2][0:HD + 2, 0:2]).then_inc(s["t_out"], 1)
                            act.wait_ge(s["turned"], 2 * n + 2)
                            for b in range(2):
                                if what == "new":
                                    act.copy(qC[0:RC, 4 * b:4 * b + 4, t * P:(t + 1) * P], bank[3 + b][0:RC])
                                last = act.copy(kC[0:RC + 2, 4 * b:4 * b + 4, k0:k0 + P], bank[5 + b][0:RC + 2])
                            last.then_inc(s["t_out"], 1)
                        act.wait_ge(s["ms"], 1)
                        act.activation(r[:], r[:], ACT.Sqrt).then_inc(s["root"], 1)
                        act.wait_ge(s["ms"], 2)
                        act.activation(ro[:], ro[:], ACT.Sqrt).then_inc(s["root"], 1)
                        act.wait_ge(s["cache_in"], 96)
                        split_hi(0)
                        act.wait_ge(s["lsum"], 1)
                        act.activation(ls[:], ls[:], ACT.Exp).then_inc(s["lexp"], 1)
                        act.activation(tm[:, :, Z0:Z0 + AW], tm[:, :, Z0:Z0 + AW], ACT.Silu).then_inc(s["silu"], 1)
                        for n in range(1, len(items)):
                            split_hi(n)
                            evac(n - 1)
                        evac(len(items) - 1)

                    @block.tensor
                    def _(pe):
                        pe.wait_ge(s["ones"], 2)
                        for n, (what, t) in enumerate(items):
                            new = what == "new"
                            pe.wait_ge(s["lo"], 2 * n + 1)
                            if n:
                                pe.wait_ge(s["t_out"], 2 * n - 1)
                            out = [ps[:, b, :].rearrange("p (n q) -> p n q", q=P) for b in range(7)]
                            for h in range(HB if new else 0):
                                pe.transpose(out[h // 4][:, h % 4], sqB[:, h].rearrange("p u d -> p (u d)").bitcast(F32), self.ident)
                            for g in range(KVB):
                                pe.transpose(out[1][:, 2 + g], skB[:, g].rearrange("p u d -> p (u d)").bitcast(F32), self.ident)
                            for g in range(KVB):
                                mm = pe.transpose(out[2][0:HD + 2, g], slB[:, g].bitcast(F32), self.ident)
                            mm.then_inc(s["turned"], 1)
                            pe.wait_ge(s["lo"], 2 * n + 2)
                            if n:
                                pe.wait_ge(s["t_out"], 2 * n)
                            for h in range(NC2 if new else 0):
                                pe.transpose(out[3 + h // 4][0:RC, h % 4], sqC[:, h].rearrange("p u d -> p (u d)").bitcast(F32), self.ident)
                            for h in range(NC2):
                                mm = pe.transpose(out[5 + h // 4][0:RC + 2, h % 4], skC[:, h].bitcast(F32), self.ident)
                            mm.then_inc(s["turned"], 1)

            units = [("B", h, 0) for h in range(HB)] + [("C", h, m) for h in range(HC) for m in range(2)]
            NU, NKL = len(units), (PAST + 4 * P) // P
            PW = NKL * 4 * P + P
            pT = tm[:].rearrange("p t n -> p (t n)")[:, 0:2 * PW].rearrange("p (u n) -> p u n", u=2)
            qBx = sb("qB_hi_max", [P, 2, T], F32R)
            mx = sb("max", [P, 2, NT])
            mrow = sb("max_split", [P, 2, NT, RC + 2], F32R)
            rs = sb("sum_inverse", [P, 2, NT])
            oc1 = sb("second_map", [P, NT, HD])
            zero = sb("zeros", [P, 2 * D])

            def max_item(u):
                return 9 * u

            def score_item(u, k):
                return 9 * u + 2 + k
            with stage(nc, "scores smax nmax chain ring_in ring_out q_hi pv o_out zeroed filled cleared") as (block, s):
                @block.gpsimd
                def _(pool):
                    pool.memset(mrow[:].bitcast(F32), 0.0).then_inc(s["cleared"], 1)
                    for u in range(HB):
                        if u >= 2:
                            pool.wait_ge(s["ring_in"], score_item(u - 2, NKL) + 1)
                        pool.tensor_copy(qBx[0:HD, u % 2, :], qB[0:HD, u, :]).then_inc(s["q_hi"], 1)
                    if l == 0:
                        pool.memset(zero[:], 0.0).then_inc(s["zeroed"], 1)

                if l == 0:
                    @block.sync
                    def _(sp):
                        sp.wait_ge(s["zeroed"], 1)
                        n = 0
                        for slots in (self.slots_h, self.slots_y):
                            for r in range(slots.shape[0] // BLK):
                                sp.dma_start(slots[r * BLK:(r + 1) * BLK].rearrange("(p a) d -> p (a d)", a=2), zero[:]
                                             ).then_inc(s["filled"], 16)
                                n += 1
                        sp.wait_ge(s["filled"], 16 * n)

                @block.tensor
                def _(pe):
                    def scores(u, t):
                        kind, h, m = units[u]
                        n = NT * u + t
                        if n >= 2:
                            pe.wait_ge(s["smax"], n - 1)
                        k0, k1 = (0, P) if t == 0 else (P, KEYS)
                        qs = slice(t * P, (t + 1) * P)
                        for a in range(k0, k1, 512):
                            b = min(a + 512, k1)
                            out = ps[:, 2 * (n % 2) + (a - k0) // 512, 0:b - a]
                            if kind == "B":
                                pe.matmul(out, qB[:, h, qs], kB[:, h // 3, a:b], start=True, stop=False)
                                mm = pe.matmul(out, qB[0:HD, h, qs], kBlo[0:HD, h // 3, a:b], start=False, stop=True)
                            else:
                                c = 2 * h + m
                                mm = pe.matmul(out, qC[0:RC, c, qs], kC[0:RC, c, a:b], start=True, stop=True)
                        mm.then_inc(s["scores"], 1)

                    def turn_max(u):
                        rows = (RB if units[u][0] == "B" else RC) + 2
                        pe.wait_ge(s["nmax"], 2 * u + 2)
                        for j, tiles in enumerate((range(1, NT), range(1))):
                            item = max_item(u) + j
                            if item >= 2:
                                pe.wait_ge(s["ring_out"], item - 1)
                            for n, t in enumerate(tiles):
                                mm = pe.transpose(ps[0:rows, 4 + item % 2, n * P:(n + 1) * P],
                                                  mrow[:, u % 2, t, 0:rows].bitcast(F32), self.ident)
                            mm.then_inc(s["ring_in"], 1)

                    def key_major(u, k):
                        kind, h, m = units[u]
                        item = score_item(u, k)
                        pe.wait_ge(s["ring_out"], item - 1 if k else max_item(u) + 2)
                        ks = slice(P * (k + 1), P * (k + 2)) if k < NKL else slice(0, P)
                        qs = slice(P, T) if k < NKL else slice(0, P)
                        out = ps[:, 4 + item % 2, 0:(4 * P if k < NKL else P)]
                        if kind == "B":
                            if k == 0:
                                pe.wait_ge(s["q_hi"], u + 1)
                            pe.matmul(out, kB[:, h // 3, ks], qB[:, h, qs], start=True, stop=False)
                            mm = pe.matmul(out, kBlo[0:RB + 2, h // 3, ks], qBx[0:RB + 2, u % 2, qs], start=False, stop=True)
                        else:
                            c = 2 * h + m
                            mm = pe.matmul(out, kC[0:RC + 2, c, ks], qC[0:RC + 2, c, qs], start=True, stop=True)
                        mm.then_inc(s["ring_in"], 1)

                    def weigh(u, part):
                        kind, h, m = units[u]
                        if part == 0:
                            pe.wait_ge(s["ring_out"], score_item(u, NKL) + 1)
                            if u >= 2:
                                pe.wait_ge(s["o_out"], u - 1)
                        v, g = (vB, h // 3) if kind == "B" else (vC, h)
                        todo = [(0, NKL, 0)] + [(t, k, k + 1) for t in range(1, NT) for k in range(NKL)]
                        n0, n1 = 0 if part == 0 else 4 * part + 1, 4 * part + 5
                        for t, k, kt in todo[n0:n1]:
                            p0 = k * 4 * P + (0 if t == 0 else (t - 1) * P)
                            mm = pe.matmul(ps[:, 6 + u % 2, t * V1:(t + 1) * V1], pT[:, u % 2, p0:p0 + P], v[:, kt, g, :],
                                           start=(t == 0 or k == 0), stop=(t == 0 or k == NKL - 1))
                        if part == 5:
                            mm.then_inc(s["pv"], 1)
                    for t in range(NT):
                        scores(0, t)
                    turn_max(0)
                    for u in range(NU + 1):
                        for k in range(NKL):
                            if u + 1 < NU and k < NT:
                                scores(u + 1, k)
                            if u:
                                weigh(u - 1, k)
                            if u < NU:
                                key_major(u, k)
                        if u < NU:
                            key_major(u, NKL)
                        if u + 1 < NU:
                            turn_max(u + 1)

                @block.vector
                def _(dve):
                    chain = Chain(dve, s["chain"])

                    def maxima(u):
                        kind, h, m = units[u]
                        for t in range(NT):
                            n = NT * u + t
                            dve.wait_ge(s["scores"], n + 1)
                            sc = ps[:, 2 * (n % 2):2 * (n % 2) + 2, :].rearrange("p b n -> p (b n)")[:, 0:(NKL * P if t else P)]
                            dve.tensor_reduce(mx[:, u % 2, t:t + 1], sc, AX.X, ALU.max).then_inc(s["smax"], 1)
                        dve.wait_ge(s["smax"], NT * (u + 1))
                        if u >= 2:
                            dve.wait_ge(s["ring_in"], max_item(u - 2) + 2)
                        c = RB if kind == "B" else RC
                        dve.tensor_scalar(mrow[:, u % 2, :, c], mx[:, u % 2], -1.0, None, ALU.mult).then_inc(s["nmax"], 1)
                        dve.wait_ge(s["nmax"], 2 * u + 1)
                        dve.scalar_tensor_tensor(out=mrow[:, u % 2, :, c + 1], in0=mx[:, u % 2], scalar=-1.0,
                                                 in1=mrow[:, u % 2, :, c].bitcast(F32), op0=ALU.mult, op1=ALU.subtract
                                                 ).then_inc(s["nmax"], 1)

                    def out(u):
                        kind, h, m = units[u]
                        dve.wait_ge(s["pv"], u + 1)
                        po = ps[:, 6 + u % 2, 0:NT * V1].rearrange("p (t d) -> p t d", d=V1)
                        inv = rs[:, u % 2]
                        chain(dve.reciprocal(inv, po[:, :, HD]))
                        if m:
                            chain(dve.tensor_scalar(inv, inv, nlam[:, 0:1], None, ALU.mult))
                        dst = mixed[:, :, AW + h * HD:AW + (h + 1) * HD] if kind == "B" else oc1[:] if m else oC[:, :, h]
                        dve.tensor_tensor(dst, po[:, :, 0:HD], bcast_last(inv, HD), ALU.mult).then_inc(s["o_out"], 1)
                        if m:
                            dve.wait_ge(s["o_out"], u + 1)
                            chain(dve.tensor_tensor(oC[:, :, h], oC[:, :, h], oc1[:], ALU.add))
                    dve.wait_ge(s["cleared"], 1)
                    maxima(0)
                    for u in range(NU + 1):
                        if u + 1 < NU:
                            maxima(u + 1)
                        if u:
                            out(u - 1)

                @block.scalar
                def _(act):
                    def max_rows(u):
                        kind, h, m = units[u]
                        r0 = RB if kind == "B" else RC
                        q = qBx[:, u % 2] if kind == "B" else qC[:, 2 * h + m]
                        for j, (a, b) in enumerate(((P, T), (0, P))):
                            item = max_item(u) + j
                            act.wait_ge(s["ring_in"], item + 1)
                            act.copy(q[r0:r0 + 2, a:b], ps[r0:r0 + 2, 4 + item % 2, 0:b - a]).then_inc(s["ring_out"], 1)
                    max_rows(0)
                    for u in range(NU):
                        kind, h, m = units[u]
                        scale = HD ** -0.5 if kind == "B" else DHC ** -0.5
                        if u >= 2:
                            act.wait_ge(s["pv"], u - 1)
                        for k in range(NKL + 1):
                            item = score_item(u, k)
                            n = 4 * P if k < NKL else P
                            act.wait_ge(s["ring_in"], item + 1)
                            act.activation(pT[:, u % 2, k * 4 * P:k * 4 * P + n], ps[:, 4 + item % 2, 0:n], ACT.Exp, scale=scale
                                           ).then_inc(s["ring_out"], 1)
                        if u + 1 < NU:
                            max_rows(u + 1)

    def out_proj(self, l):
        nc, ps, mixed, oC, gdiff = self.nc, self.ps, self.mixed, self.oC, self.gdiff
        with ExitStack() as scope:
            def sb(name, shape, dt=F32):
                return scope.enter_context(nc.sbuf_tensor(f"{name}_{l}", shape, dt))
            dsq = sb("d_sq", [P, NT, HC, HD])
            dr = sb("d_r", [P, NT, HC])
            w = self.i["w_out"][l].rearrange("(c p) n -> p c n", p=P)
            ws = Split(self, scope, f"out_{l}", KC * P, 3, 2, range(KC), lambda m: [(w[:, :, m * P:(m + 1) * P], KC)])
            with stage(nc, "chain ms root o_done turned hi lo added " + ws.names) as (block, s):
                mc = mixed[:, :, 2 * AW:D].rearrange("p t (h d) -> p t h d", d=HD)

                @block.vector
                def _(dve):
                    chain = Chain(dve, s["chain"])
                    chain(dve.tensor_tensor(dsq[:], oC, oC, ALU.mult))
                    chain(dve.tensor_reduce(dr[:], dsq[:], AX.X, ALU.add))
                    dve.tensor_scalar(dr[:], dr[:], 1.0 / HD, EPS, ALU.mult, ALU.add).then_inc(s["ms"], 1)
                    dve.wait_ge(s["root"], 1)
                    chain(dve.reciprocal(dr[:], dr[:]))
                    for t in range(NT):
                        chain(dve.tensor_tensor(oC[:, t], oC[:, t], bcast_last(dr[:, t, :], HD), ALU.mult))
                        dve.tensor_tensor(mc[:, t], oC[:, t], bcast_mid(gdiff[:], HC), ALU.mult).then_inc(s["o_done"], 1)
                    ws.split_lo(dve, s, 0)
                    for n in range(2 * NT):
                        t, g = divmod(n, 2)
                        dve.wait_ge(s["hi"], n + 1)
                        dve.tensor_tensor(self.mlo[:, 4 * g:4 * g + 4, t * P:(t + 1) * P], ps[:, n % 8, :].rearrange("p (c q) -> p c q", c=4),
                                          self.mhi[:, 4 * g:4 * g + 4, t * P:(t + 1) * P].bitcast(F32), ALU.subtract).then_inc(s["lo"], 1)
                    for m in range(KC):
                        if m + 1 < KC:
                            ws.split_lo(dve, s, m + 1)
                        self.add_chunk(dve, s, l, 2, m, m + 1)

                @block.scalar
                def _(act):
                    act.wait_ge(s["ms"], 1)
                    act.activation(dr[:], dr[:], ACT.Sqrt).then_inc(s["root"], 1)
                    for m in range(2):
                        ws.split_hi(act, s, m)
                    for n in range(2 * NT):
                        t, g = divmod(n, 2)
                        act.wait_ge(s["turned"], n + 1)
                        act.copy(self.mhi[:, 4 * g:4 * g + 4, t * P:(t + 1) * P], ps[:, n % 8, :].rearrange("p (c q) -> p c q", c=4)
                                 ).then_inc(s["hi"], 1)
                    for m in range(2, KC):
                        ws.split_hi(act, s, m)

                @block.sync
                def _(sp):
                    for m in range(KC):
                        ws.load(sp, s, m)

                @block.tensor
                def _(pe):
                    for n in range(2 * NT):
                        t, g = divmod(n, 2)
                        if n >= 8:
                            pe.wait_ge(s["lo"], n - 7)
                        if g:
                            pe.wait_ge(s["o_done"], t + 1)
                        for c in range(4):
                            mm = pe.transpose(ps[:, n % 8, c * P:(c + 1) * P], mixed[:, t, (4 * g + c) * P:(4 * g + c + 1) * P], self.ident)
                        mm.then_inc(s["turned"], 1)
                    pe.wait_ge(s["lo"], 2 * NT)
                    for m in range(KC):
                        pe.wait_ge(s["w_lo"], m + 1)
                        if m >= 4:
                            pe.wait_ge(s["added"], len(PIECES) * (m - 3))
                        for k in range(KC):
                            for n, (wt, x) in enumerate(((ws.hi, self.mhi), (ws.hi, self.mlo), (ws.lo, self.mhi))):
                                for j, (a, b) in enumerate(HALVES):
                                    mm = pe.matmul(ps[:, 2 * (m % 4) + j, 0:b - a], wt[:, m % 2, k * P:(k + 1) * P], x[:, k, a:b],
                                                   start=(k == 0 and n == 0), stop=(k == KC - 1 and n == 2))
                        mm.then_inc(s["w_used"], 1)


    def add_chunk(self, dve, s, l, gate, m, used):
        dve.wait_ge(s["w_used"], used)
        for a, b, half, j in PIECES:
            x = self.xT[:, m, a:b]
            a0 = HALVES[half][0]
            dve.scalar_tensor_tensor(out=x, in0=self.ps[:, 2 * (m % 4) + half, a - a0:b - a0], scalar=self.mod[:, l, gate, m, j:j + 1],
                                     in1=x, op0=ALU.mult, op1=ALU.add).then_inc(s["added"], 1)

    def moe(self, l):
        nc, i, ps = self.nc, self.i, self.ps
        slots_h, slots_y = self.slots_h, self.slots_y
        with ExitStack() as outer:
            def sbo(name, shape, dt=F32):
                return outer.enter_context(nc.sbuf_tensor(name, shape, dt))
            pos = sbo("slot_of_choice", [P, 2, NT], U32)
            w = sbo("choice_weight", [P, NT, 2])
            self.hT = sbo("h_moe", [P, KC, T])
            self.norm(lambda c, j: self.amul[:, l, 1, c, j:j + 1], lambda c, j: self.mod[:, l, 3, c, j:j + 1], h=self.hT)
            meta = sbo("round_table", [P, RMAX + 2], I32)
            self.route(pos, w, meta)
            self.rounds(meta)
            self.combine(l, pos, w)

    def route(self, pos, w, meta):
        nc, i, ps = self.nc, self.i, self.ps
        with ExitStack() as scope:
            def sb(name, shape, dt=F32):
                return scope.enter_context(nc.sbuf_tensor(name, shape, dt))
            rw = sb("router_w", [P, KC, NE])
            htok = sb("h_tokens", [P, NT, D])
            lg = sb("logits", [P, NT, NE])
            top = sb("top", [P, NT, 8])
            idx = sb("top_idx", [P, NT, 8], U32)
            idf = sb("top_idx_f", [P, NT, 2])
            e = sb("top_e", [P, NT, 1])
            io = sb("iota", [P, 16])
            oh = sb("chosen", [P, 2, NT, NE])
            both = sb("chosen_both", [P, NT, NE])
            blocks = sb("blocks", [P, NE])
            ends = sb("block_ends", [P, 2, NE])
            tmp = sb("route_tmp", [P, 16, NE])
            posf = sb("slot_f", [P, 2, NT])
            metaf = sb("round_table_f", [P, RMAX + 2])
            with stage(nc, "w_in io mm chain diff expd both count turned h_act h_dve slots scattered") as (block, s):
                @block.sync
                def _(sp):
                    sp.dma_start(rw[:], i["moe_router"][0].rearrange("(c p) e -> p c e", p=P)).then_inc(s["w_in"], 16)
                    sp.dma_start(io[:], i["iota"].partition_broadcast(P)).then_inc(s["io"], 16)

                @block.tensor
                def _(pe):
                    pe.wait_ge(s["w_in"], 16)
                    for t in range(NT):
                        for k in range(KC):
                            mm = pe.matmul(ps[:, 0, t * NE:(t + 1) * NE], self.hT[:, k, t * P:(t + 1) * P], rw[:, k, :],
                                           start=(k == 0), stop=(k == KC - 1))
                    mm.then_inc(s["mm"], 1)
                    for n in range(2 * NT):
                        t, g = divmod(n, 2)
                        if n >= 6:
                            pe.wait_ge(s["h_dve" if g else "h_act"], t - 2)
                        for c in range(4):
                            mm = pe.transpose(ps[:, 2 + n % 6, c * P:(c + 1) * P], self.hT[:, 4 * g + c, t * P:(t + 1) * P], self.ident)
                        mm.then_inc(s["turned"], 1)
                    pe.wait_ge(s["both"], 1)
                    for t in range(NT + 1):
                        for u in range(min(t + 1, NT)):
                            mm = pe.matmul(ps[:, 1, t * NE:(t + 1) * NE], self.c(C_SL + 1) if u == t else self.ones, both[:, u, :],
                                           start=(u == 0), stop=(u == min(t, NT - 1)))
                    mm.then_inc(s["count"], 1)

                @block.scalar
                def _(act):
                    act.wait_ge(s["diff"], 1)
                    act.activation(e[:], e[:], ACT.Exp).then_inc(s["expd"], 1)
                    for t in range(NT):
                        act.wait_ge(s["turned"], 2 * t + 1)
                        act.copy(htok[:, t, 0:512], ps[:, 2 + (2 * t) % 6, :]).then_inc(s["h_act"], 1)

                @block.vector
                def _(dve):
                    chain = Chain(dve, s["chain"])
                    dve.wait_ge(s["mm"], 1)
                    dve.wait_ge(s["io"], 16)
                    chain(dve.tensor_copy(lg[:].rearrange("p t e -> p (t e)"), ps[:, 0, 0:NT * NE]))
                    for t in range(NT):
                        chain(dve.max(top[:, t], lg[:, t]), wait=t == NT - 1)
                    for t in range(NT):
                        chain(dve.max_index(idx[:, t], top[:, t], lg[:, t]), wait=t == NT - 1)
                    dve.tensor_tensor(e[:], top[:, :, 1:2], top[:, :, 0:1], ALU.subtract).then_inc(s["diff"], 1)
                    dve.wait_ge(s["diff"], 1)
                    chain(dve.tensor_copy(idf[:], idx[:, :, 0:2]))
                    for t in range(NT):
                        for q in range(2):
                            chain(dve.tensor_scalar(oh[:, q, t], io[:, 0:NE], idf[:, t, q:q + 1], None, ALU.is_equal),
                                  wait=t == NT - 1 and q)
                    dve.tensor_tensor(both[:], oh[:, 0], oh[:, 1], ALU.add).then_inc(s["both"], 1)
                    dve.wait_ge(s["expd"], 1)
                    chain(dve.tensor_scalar(w[:, :, 1:2], e[:], 1.0, None, ALU.add))
                    chain(dve.reciprocal(w[:, :, 0:1], w[:, :, 1:2]))
                    chain(dve.tensor_tensor(w[:, :, 1:2], w[:, :, 0:1], e[:], ALU.mult))
                    for t in range(NT):
                        dve.wait_ge(s["turned"], 2 * t + 2)
                        dve.tensor_copy(htok[:, t, 512:D], ps[:, 2 + (2 * t + 1) % 6, :]).then_inc(s["h_dve"], 1)
                    dve.wait_ge(s["count"], 1)
                    cnt = ps[:, 1, NT * NE:(NT + 1) * NE]
                    chain(dve.tensor_scalar(blocks[:], cnt, 0.0, None, ALU.is_gt))
                    for q in range(1, -(-T // BLK)):
                        chain(dve.tensor_scalar(ends[:, 0], cnt, float(q * BLK), None, ALU.is_gt))
                        chain(dve.tensor_tensor(blocks[:], blocks[:], ends[:, 0], ALU.add))
                    chain(dve.tensor_copy(ends[:, 0], blocks[:]))
                    for n, step in enumerate((1, 2, 4)):
                        a, b = n % 2, 1 - n % 2
                        chain(dve.tensor_copy(ends[:, b, 0:step], ends[:, a, 0:step]))
                        chain(dve.tensor_tensor(ends[:, b, step:], ends[:, a, step:], ends[:, a, 0:NE - step], ALU.add))
                    chain(dve.tensor_tensor(tmp[:, 0:16], bcast_mid(ends[:, 1], 16), bcast_last(io[:], NE), ALU.is_le))
                    chain(dve.tensor_reduce(metaf[:, 0:RMAX + 1], tmp[:, 0:RMAX + 1], AX.X, ALU.add))
                    chain(dve.tensor_scalar(metaf[:, 0:RMAX + 1], metaf[:, 0:RMAX + 1], float(NE - 1), None, ALU.min))
                    chain(dve.tensor_copy(metaf[:, RMAX + 1:RMAX + 2], ends[:, 1, NE - 1:NE]))
                    chain(dve.tensor_copy(meta[:], metaf[:]))
                    chain(dve.tensor_tensor(blocks[:], ends[:, 1], blocks[:], ALU.subtract))
                    chain(dve.tensor_scalar(blocks[:], blocks[:], float(BLK), None, ALU.mult))
                    chain(dve.tensor_tensor(tmp[:, 0:NT], ps[:, 1, 0:NT * NE].rearrange("p (t e) -> p t e", e=NE),
                                            bcast_mid(blocks[:], NT), ALU.add))
                    for q in range(2):
                        chain(dve.tensor_tensor(oh[:, q], oh[:, q], tmp[:, 0:NT], ALU.mult))
                        chain(dve.tensor_reduce(posf[:, q], oh[:, q], AX.X, ALU.add))
                    dve.tensor_copy(pos[:], posf[:]).then_inc(s["slots"], 1)

                @block.gpsimd
                def _(pool):
                    pool.wait_ge(s["slots"], 1)
                    for t in range(NT):
                        pool.wait_ge(s["h_act"], t + 1)
                        pool.wait_ge(s["h_dve"], t + 1)
                        for q in range(2):
                            pool.indirect_dma_start(self.slots_h, bass.IndirectOffsetOnAxis(pos[:, q, t:t + 1], 0),
                                                    htok[:, t, :], None).then_inc(s["scattered"], 16)
                    pool.wait_ge(s["scattered"], 16 * 2 * NT)

    def rounds(self, meta):
        nc, i, ps = self.nc, self.i, self.ps
        SL = 3
        GU, W3 = 2 * KC * P, 2 * KC * P + D
        last = [9, 10, 8]
        loads = [4, 4, 3]
        wgu = i["moe_w_gu"][0].rearrange("e (c p) (h j n) -> e p h j c n", p=P, h=2, n=P)
        wdn = i["moe_w_down"][0].rearrange("e (j p) n -> e j p n", p=P)
        yv = self.slots_y.rearrange("(r a p) d -> r p a d", a=2, p=P)
        hv = self.slots_h.rearrange("(r a p) d -> r p a d", a=2, p=P)
        with ExitStack() as scope:
            def sb(name, shape, dt=F32):
                return scope.enter_context(nc.sbuf_tensor(name, shape, dt))
            raw = sb("w_raw", [P, SL, W3])
            whi = sb("w_hi", [P, SL, W3], F32R)
            wlo = sb("w_lo", [P, SL, W3], F32R)
            hblk = sb("h_block", [P, 2, D])
            hhi = sb("h_hi", [P, KC, BLK], F32R)
            hlo = sb("h_lo", [P, KC, BLK], F32R)
            sg = sb("silu_g", [P, 2, BLK])
            ahi = sb("act_hi", [P, 2, BLK], F32R)
            alo = sb("act_lo", [P, 2, BLK], F32R)
            y = sb("y_block", [P, 2, D])
            TB = (2, 3, 1, 0)
            names = ("blk_in turned h_hi h_lo hi_u lo_u hi_d lo_d gu silu prod a_hi a_lo dn y_act y_dve y_store y_free "
                     + " ".join(f"raw{q}" for q in range(SL)))

            def gu(t, j, half, k):
                o = (half * KC + k) * P
                return t[:, j % SL, o:o + P]

            def dn(t, j, half):
                return t[:, j % SL, GU + 512 * half:GU + 512 * half + 512]

            def quarter(n):
                return n // 2, 4 * (n % 2)
            with stage(nc, names) as (block, s):
                @block.sync
                def _(sp):
                    def load_w(e, j):
                        q = j % SL
                        for half in range(2):
                            o = half * KC * P
                            sp.dma_start(raw[:, q, o:o + KC * P].rearrange("p (c n) -> p c n", c=KC),
                                         wgu[e, :, half, j]).then_inc(s[f"raw{q}"], 16)
                        sp.dma_start(raw[:, q, GU:W3], wdn[e, j]).then_inc(s[f"raw{q}"], 16)
                    rounds = sp.value_load(meta[0:1, RMAX + 1:RMAX + 2], min_val=1, max_val=RMAX)
                    e0 = sp.value_load(meta[0:1, 0:1], min_val=0, max_val=NE - 1)
                    sp.dma_start(hblk[:], hv[0]).then_inc(s["blk_in"], 16)
                    for j in range(SL):
                        load_w(e0, j)
                    with sp.Fori(0, rounds) as r:
                        sp.wait_ge(s["turned"], 4 * r + 4)
                        sp.dma_start(hblk[:], hv[r + 1]).then_inc(s["blk_in"], 16)
                        e = sp.value_load(meta[0:1, bass.ds(r, 1)], min_val=0, max_val=NE - 1)
                        for j in range(SL, FC):
                            sp.wait_ge(s["hi_d"], 11 * r + (j - SL) + 1)
                            sp.wait_ge(s["lo_d"], 11 * r + (j - SL) + 1)
                            load_w(e, j)
                        en = sp.value_load(meta[0:1, bass.ds(r + 1, 1)], min_val=0, max_val=NE - 1)
                        for j in range(SL):
                            sp.wait_ge(s["hi_d"], 11 * r + last[j] + 1)
                            sp.wait_ge(s["lo_d"], 11 * r + last[j] + 1)
                            load_w(en, j)

                @block.tensor
                def _(pe):
                    rounds = pe.value_load(meta[0:1, RMAX + 1:RMAX + 2], min_val=1, max_val=RMAX)
                    pe.nop().then_inc(s["dn"], 11)
                    pe.nop().then_inc(s["gu"], 11)

                    def turn(r, quarters):
                        pe.wait_ge(s["blk_in"], 16 * r + 16)
                        for n in quarters:
                            if n >= 2:
                                pe.wait_ge(s["prod"], 11 * r + 8 + n)
                            a, c0 = quarter(n)
                            for c in range(4):
                                mm = pe.transpose(ps[:, TB[n], c * P:(c + 1) * P], hblk[:, a, (c0 + c) * P:(c0 + c + 1) * P], self.ident)
                            mm.then_inc(s["turned"], 1)

                    def down(r, j):
                        pe.wait_ge(s["a_lo"], 11 * r + j + 1)
                        pe.wait_ge(s["lo_d"], 11 * r + j + 1)
                        if j == 0:
                            pe.wait_ge(s["y_act"], 2 * r + 2)
                            pe.wait_ge(s["y_dve"], 2 * r + 2)
                        for a in range(2):
                            for n, (x, wt) in enumerate(((ahi, whi), (ahi, wlo), (alo, whi))):
                                for half in range(2):
                                    mm = pe.matmul(ps[:, 4 + 2 * a + half, :], x[:, j % 2, a * P:(a + 1) * P], dn(wt, j, half),
                                                   start=(j == 0 and n == 0), stop=(j == FC - 1 and n == 2))
                        mm.then_inc(s["dn"], 1)
                    turn(0, range(4))
                    with pe.Fori(0, rounds) as r:
                        pe.wait_ge(s["h_lo"], 4 * r + 4)
                        for j in range(FC):
                            pe.wait_ge(s["lo_u"], 11 * r + j + 1)
                            pe.wait_ge(s["prod"], 11 * r + (11, 10)[j] if j < 2 else 11 * r + 11 + j - 1)
                            for half in range(2):
                                for k in range(KC):
                                    for n, (wt, x) in enumerate(((whi, hhi), (whi, hlo), (wlo, hhi))):
                                        mm = pe.matmul(ps[:, j % 2, half * BLK:(half + 1) * BLK], gu(wt, j, half, k), x[:, k, :],
                                                       start=(k == 0 and n == 0), stop=(k == KC - 1 and n == 2))
                            mm.then_inc(s["gu"], 1)
                            if j == FC - 1:
                                turn(r + 1, [2])
                            if j:
                                down(r, j - 1)
                            if j == FC - 2:
                                turn(r + 1, [0, 1])
                        turn(r + 1, [3])
                        down(r, FC - 1)

                @block.scalar
                def _(act):
                    rounds = act.value_load(meta[0:1, RMAX + 1:RMAX + 2], min_val=1, max_val=RMAX)
                    act.nop().then_inc(s["y_act"], 2)

                    def take_block(r):
                        for n in range(4):
                            a, c0 = quarter(n)
                            act.wait_ge(s["turned"], 4 * r + n + 1)
                            if n == 0:
                                act.wait_ge(s["gu"], 11 * r + 11)
                            act.copy(hhi[:, c0:c0 + 4, a * P:(a + 1) * P], ps[:, TB[n], :].rearrange("p (c q) -> p c q", c=4)
                                     ).then_inc(s["h_hi"], 1)

                    def split(r, j, down):
                        q = j % SL
                        part = slice(GU, W3) if down else slice(0, GU)
                        act.wait_ge(s[f"raw{q}"], 48 * (loads[q] * r + j // SL + 1))
                        act.wait_ge(s["dn" if down else "gu"], 11 * r + last[q] + 1 if j < SL else 11 * r + 11 + j - SL + 1)
                        act.copy(whi[:, q, part], raw[:, q, part]).then_inc(s["hi_d" if down else "hi_u"], 1)
                    take_block(0)
                    for j in range(2):
                        for down in (False, True):
                            split(0, j, down)
                    with act.Fori(0, rounds) as r:
                        for j in range(FC):
                            act.wait_ge(s["gu"], 11 * r + 11 + j + 1)
                            if j == 0:
                                act.wait_ge(s["prod"], 11 * r + 11)
                            else:
                                act.wait_ge(s["prod"], 11 * r + 11 + max(j - 1, 0))
                            act.activation(sg[:, j % 2, :], ps[:, j % 2, 0:BLK], ACT.Silu).then_inc(s["silu"], 1)
                            act.wait_ge(s["prod"], 11 * r + 11 + j + 1)
                            act.wait_ge(s["dn"], 11 * r + 11 + max(j - 1, 0))
                            act.copy(ahi[:, j % 2, :], sg[:, j % 2, :]).then_inc(s["a_hi"], 1)
                            if j + 2 < FC:
                                for down in (False, True):
                                    split(r, j + 2, down)
                            if j == FC - 2:
                                split(r + 1, 0, False)
                        take_block(r + 1)
                        split(r + 1, 0, True)
                        for down in (False, True):
                            split(r + 1, 1, down)
                        act.wait_ge(s["dn"], 11 * r + 22)
                        act.wait_ge(s["y_free"], r + 1)
                        for half in range(2):
                            act.copy(y[:, 0, 512 * half:512 * half + 512], ps[:, 4 + half, :]).then_inc(s["y_act"], 1)

                @block.vector
                def _(dve):
                    rounds = dve.value_load(meta[0:1, RMAX + 1:RMAX + 2], min_val=1, max_val=RMAX)
                    dve.nop().then_inc(s["prod"], 11)
                    dve.nop().then_inc(s["y_dve"], 2)

                    def take_block(r):
                        for n in range(4):
                            a, c0 = quarter(n)
                            dve.wait_ge(s["h_hi"], 4 * r + n + 1)
                            dve.tensor_tensor(hlo[:, c0:c0 + 4, a * P:(a + 1) * P], ps[:, TB[n], :].rearrange("p (c q) -> p c q", c=4),
                                              hhi[:, c0:c0 + 4, a * P:(a + 1) * P].bitcast(F32), ALU.subtract).then_inc(s["h_lo"], 1)

                    def split(r, j, down):
                        q = j % SL
                        part = slice(GU, W3) if down else slice(0, GU)
                        dve.wait_ge(s["hi_d" if down else "hi_u"], 11 * r + j + 1)
                        dve.tensor_tensor(wlo[:, q, part], raw[:, q, part], whi[:, q, part].bitcast(F32), ALU.subtract
                                          ).then_inc(s["lo_d" if down else "lo_u"], 1)
                    take_block(0)
                    for j in range(2):
                        for down in (False, True):
                            split(0, j, down)
                    with dve.Fori(0, rounds) as r:
                        for j in range(FC):
                            dve.wait_ge(s["silu"], 11 * r + j + 1)
                            g = sg[:, j % 2, :]
                            dve.tensor_tensor(g, g, ps[:, j % 2, BLK:2 * BLK], ALU.mult).then_inc(s["prod"], 1)
                            dve.wait_ge(s["a_hi"], 11 * r + j + 1)
                            dve.tensor_tensor(alo[:, j % 2, :], g, ahi[:, j % 2, :].bitcast(F32), ALU.subtract).then_inc(s["a_lo"], 1)
                            if j + 2 < FC:
                                for down in (False, True):
                                    split(r, j + 2, down)
                            if j == FC - 2:
                                split(r + 1, 0, False)
                        take_block(r + 1)
                        split(r + 1, 0, True)
                        for down in (False, True):
                            split(r + 1, 1, down)
                        dve.wait_ge(s["dn"], 11 * r + 22)
                        dve.wait_ge(s["y_free"], r + 1)
                        for half in range(2):
                            dve.tensor_copy(y[:, 1, 512 * half:512 * half + 512], ps[:, 6 + half, :]).then_inc(s["y_dve"], 1)

                @block.gpsimd
                def _(pool):
                    rounds = pool.value_load(meta[0:1, RMAX + 1:RMAX + 2], min_val=1, max_val=RMAX)
                    pool.nop().then_inc(s["y_free"], 1)
                    with pool.Fori(0, rounds) as r:
                        pool.wait_ge(s["y_act"], 2 * r + 4)
                        pool.wait_ge(s["y_dve"], 2 * r + 4)
                        pool.dma_start(yv[r], y[:]).then_inc(s["y_store"], 16)
                        pool.wait_ge(s["y_store"], 16 * r + 16)
                        pool.nop().then_inc(s["y_free"], 1)
                    pool.wait_ge(s["blk_in"], 16 * rounds + 16)
                    for q in range(SL):
                        pool.wait_ge(s[f"raw{q}"], 48 * (loads[q] * rounds + 1))

    def combine(self, l, pos, w):
        nc, i, ps = self.nc, self.i, self.ps
        with ExitStack() as scope:
            y1 = scope.enter_context(nc.sbuf_tensor("y_first", [P, NT, D], F32))
            y2 = scope.enter_context(nc.sbuf_tensor("y_second", [P, NT, D], F32))
            with stage(nc, "first scaled summed turned added " + " ".join(f"g{t}" for t in range(NT))) as (block, s):
                @block.gpsimd
                def _(pool):
                    for t in range(NT):
                        for q, y in ((0, y1), (1, y2)):
                            pool.indirect_dma_start(y[:, t, :], None, self.slots_y, bass.IndirectOffsetOnAxis(pos[:, q, t:t + 1], 0)
                                                    ).then_inc(s[f"g{t}"], 16)
                    for t in range(NT):
                        pool.wait_ge(s[f"g{t}"], 32)

                @block.scalar
                def _(act):
                    for t in range(NT):
                        act.wait_ge(s[f"g{t}"], 32)
                        act.activation(y1[:, t, :], y1[:, t, :], ACT.Copy, scale=w[:, t, 0:1]).then_inc(s["scaled"], 1)

                @block.vector
                def _(dve):
                    def add(n):
                        t, g = divmod(n, 2)
                        dve.wait_ge(s["turned"], n + 1)
                        for c in range(4):
                            x = self.xT[:, 4 * g + c, t * P:(t + 1) * P]
                            ins = dve.scalar_tensor_tensor(out=x, in0=ps[:, n % 8, c * P:(c + 1) * P],
                                                           scalar=self.mod[:, l, 5, 4 * g + c, min(t, 1):min(t, 1) + 1],
                                                           in1=x, op0=ALU.mult, op1=ALU.add)
                        ins.then_inc(s["added"], 1)
                    for t in range(NT):
                        dve.wait_ge(s["scaled"], t + 1)
                        dve.scalar_tensor_tensor(out=y1[:, t, :], in0=y2[:, t, :], scalar=w[:, t, 1:2], in1=y1[:, t, :],
                                                 op0=ALU.mult, op1=ALU.add).then_inc(s["summed"], 1)
                        if t:
                            add(2 * t - 2)
                            add(2 * t - 1)
                    add(2 * NT - 2)
                    add(2 * NT - 1)

                @block.tensor
                def _(pe):
                    for n in range(2 * NT):
                        t, g = divmod(n, 2)
                        pe.wait_ge(s["summed"], t + 1)
                        if n >= 8:
                            pe.wait_ge(s["added"], n - 7)
                        for c in range(4):
                            mm = pe.transpose(ps[:, n % 8, c * P:(c + 1) * P], y1[:, t, (4 * g + c) * P:(4 * g + c + 1) * P], self.ident)
                        mm.then_inc(s["turned"], 1)

    def ffn(self, l):
        nc, i, ps = self.nc, self.i, self.ps
        w1 = i["ffn_w_gu"][0].rearrange("(c p) (h e j n) -> p h e j c n", p=P, h=2, e=2, n=P)
        w2 = i["ffn_w_down"][0].rearrange("(e j p) (m n) -> e m p j n", e=2, p=P, n=P)
        NTL = FC + KC
        tiles = [(e, n) for e in range(2) for n in range(NTL)]

        def sources(tile):
            e, n = tile
            if n < FC:
                return [(w1[:, half, e, n], KC) for half in range(2)]
            return [(w2[e, n - FC], FC)]
        with ExitStack() as scope:
            def sb(name, shape, dt=F32):
                return scope.enter_context(nc.sbuf_tensor(f"{name}_{l}", shape, dt))
            hhi, hlo = sb("ffn_h_hi", [P, KC, T], F32R), sb("ffn_h_lo", [P, KC, T], F32R)
            sq, rstd = sb("sq", [P, KC, T]), sb("rstd", [P, T])
            ahi, alo = sb("act_hi", [P, FC, T], F32R), sb("act_lo", [P, FC, T], F32R)
            sg = sb("silu_g", [P, 2, T])
            ws = Split(self, scope, f"ffn_{l}", 2 * KC * P, 2, 2, tiles, sources)
            with stage(nc, "silu prod a_hi a_lo added " + ws.names + " " + self.NORM) as (block, s):
                act_squares, act_rest, dve_squares, dve_rest, pe_sums = self.norm_programs(
                    s, sq, rstd[:], lambda c, j: self.amul[:, l, 1, c, j:j + 1], lambda c, j: self.mod[:, l, 3, c, j:j + 1],
                    parts=(hhi, hlo))

                @block.sync
                def _(sp):
                    for n in range(len(tiles)):
                        ws.load(sp, s, n)

                @block.tensor
                def _(pe):
                    pe_sums(pe)
                    for q, (e, n) in enumerate(tiles):
                        pe.wait_ge(s["w_lo"], q + 1)
                        u = q % 2
                        if n < FC:
                            j = n
                            if j >= 2:
                                pe.wait_ge(s["prod"], 2 * (e * FC + j - 1))
                            elif e:
                                pe.wait_ge(s["added"], len(PIECES) * KC)
                            for half in range(2):
                                for k in range(KC):
                                    if q == 0 and half == 0:
                                        pe.wait_ge(s["n_lo"], k + 1)
                                    o = (half * KC + k) * P
                                    for m, (wt, x) in enumerate(((ws.hi, hhi), (ws.hi, hlo), (ws.lo, hhi))):
                                        for st, (a, b) in enumerate(HALVES):
                                            mm = pe.matmul(ps[:, 4 * (j % 2) + 2 * half + st, 0:b - a], wt[:, u, o:o + P], x[:, k, a:b],
                                                           start=(k == 0 and m == 0), stop=(k == KC - 1 and m == 2))
                        else:
                            m_ = n - FC
                            if m_ == 0:
                                pe.wait_ge(s["a_lo"], FC * (e + 1))
                            if m_ >= 4:
                                pe.wait_ge(s["added"], len(PIECES) * (e * KC + m_ - 3))
                            for j in range(FC):
                                for m, (wt, x) in enumerate(((ws.hi, ahi), (ws.hi, alo), (ws.lo, ahi))):
                                    for st, (a, b) in enumerate(HALVES):
                                        mm = pe.matmul(ps[:, 2 * (m_ % 4) + st, 0:b - a], wt[:, u, j * P:(j + 1) * P], x[:, j, a:b],
                                                       start=(j == 0 and m == 0), stop=(j == FC - 1 and m == 2))
                        mm.then_inc(s["w_used"], 1)

                @block.scalar
                def _(act):
                    act_squares(act)
                    ws.split_hi(act, s, 0)
                    act_rest(act)
                    for q, (e, n) in enumerate(tiles):
                        if q + 1 < len(tiles):
                            ws.split_hi(act, s, q + 1)
                        if n < FC:
                            c = e * FC + n
                            act.wait_ge(s["w_used"], q + 1)
                            if c >= 2:
                                act.wait_ge(s["a_lo"], c - 1)
                            for st, (a, b) in enumerate(HALVES):
                                act.activation(sg[:, n % 2, a:b], ps[:, 4 * (n % 2) + st, 0:b - a], ACT.Silu).then_inc(s["silu"], 1)
                            act.wait_ge(s["prod"], 2 * c + 2)
                            act.copy(ahi[:, n, :], sg[:, n % 2, :]).then_inc(s["a_hi"], 1)

                @block.vector
                def _(dve):
                    dve_squares(dve)
                    ws.split_lo(dve, s, 0)
                    dve_rest(dve)
                    for q, (e, n) in enumerate(tiles):
                        if q + 1 < len(tiles):
                            ws.split_lo(dve, s, q + 1)
                        if n < FC:
                            c = e * FC + n
                            for st, (a, b) in enumerate(HALVES):
                                dve.wait_ge(s["silu"], 2 * c + st + 1)
                                g = sg[:, n % 2, a:b]
                                dve.tensor_tensor(g, g, ps[:, 4 * (n % 2) + 2 + st, 0:b - a], ALU.mult).then_inc(s["prod"], 1)
                            dve.wait_ge(s["a_hi"], c + 1)
                            dve.tensor_tensor(alo[:, n, :], sg[:, n % 2, :], ahi[:, n, :].bitcast(F32), ALU.subtract
                                              ).then_inc(s["a_lo"], 1)
                        else:
                            if e:
                                dve.wait_ge(s["added"], len(PIECES) * KC)
                            self.add_chunk(dve, s, l, 5, n - FC, q + 1)

    def store(self):
        nc, ps = self.nc, self.ps
        with ExitStack() as scope:
            y = scope.enter_context(nc.sbuf_tensor("y_out", [P, NT, D], F32))
            with stage(nc, "turned out_act out_dve stored") as (block, s):
                @block.tensor
                def _(pe):
                    for n in range(2 * NT):
                        t, g = divmod(n, 2)
                        if n >= 8:
                            pe.wait_ge(s["out_dve" if g else "out_act"], t - 3)
                        for c in range(4):
                            mm = pe.transpose(ps[:, n % 8, c * P:(c + 1) * P], self.hT[:, 4 * g + c, t * P:(t + 1) * P], self.ident)
                        mm.then_inc(s["turned"], 1)

                @block.scalar
                def _(act):
                    for t in range(NT):
                        act.wait_ge(s["turned"], 2 * t + 1)
                        act.copy(y[:, t, 0:512], ps[:, (2 * t) % 8, :]).then_inc(s["out_act"], 1)

                @block.vector
                def _(dve):
                    for t in range(NT):
                        dve.wait_ge(s["turned"], 2 * t + 2)
                        dve.tensor_copy(y[:, t, 512:D], ps[:, (2 * t + 1) % 8, :]).then_inc(s["out_dve"], 1)

                @block.sync
                def _(sp):
                    for t in range(NT):
                        sp.wait_ge(s["out_act"], t + 1)
                        sp.wait_ge(s["out_dve"], t + 1)
                        dst = self.o["yp"][0] if t == 0 else self.o["ys"][0, (t - 1) * P:t * P, :]
                        sp.dma_start(dst, y[:, t]).then_inc(s["stored"], 16)
                    sp.wait_ge(s["stored"], 16 * NT)


def build_program(nc, i, o, stop=None):
    with ExitStack() as ctx:
        k = Kernel(nc, i, o, ctx)
        k.prologue()
        for l in range(DEPTH):
            k.mixer(l)
            if l % 2 == 0:
                k.ffn(l)
            else:
                k.moe(l)
        with nc.sbuf_tensor("h_final", [P, KC, T], F32) as k.hT:
            k.norm(lambda c, j: k.cols[:, 112 + 32 + c:][:, 0:1], None, h=k.hT)
            k.store()


def shape_constants():
    a = np.arange(P)
    r, c = a[:, None], a[None, :]
    t = [r == c, np.ones((P, P)), r <= c, r >= c, r > c, r < c]
    for d in range(2):
        j, i_ = r, c
        for lev in range(NLEV):
            b = 1 << lev
            same = j // (2 * b) == i_ // (2 * b)
            lo, hi = (j, i_) if d == 0 else (i_, j)
            t.append(same & (lo % (2 * b) < b) & (hi % (2 * b) >= b))
    consts = np.stack([np.asarray(x, np.float32) for x in t], axis=1)
    pos = np.arange(4 * P)
    row, col = (pos // 64).astype(np.float32), (pos % 64).astype(np.float32)
    parts = []
    for hd in (HD, DHC):
        nf = hd // 4
        inv = np.float32(10000.0) ** (-np.arange(nf, dtype=np.float32) / np.float32(nf))
        ang = np.stack([row[:, None] * inv, col[:, None] * inv], axis=1)
        cs, sn = np.cos(ang), np.sin(ang)
        parts.append(np.stack([cs, cs], axis=2).reshape(4 * P, hd))
        parts.append(np.stack([-sn, sn], axis=2).reshape(4 * P, hd))
    rope = np.concatenate(parts, axis=1).astype(np.float32).reshape(4, P, 192).transpose(1, 0, 2)
    sel = np.zeros((NE, NE, P), np.float32)
    for e in range(NE):
        sel[e, e] = 1.0
    return {"consts": np.ascontiguousarray(consts), "rope": np.ascontiguousarray(rope),
            "iota": np.arange(16, dtype=np.float32), "sel": sel}


_INS = ["x_prompt", "x_sample", "state_delta", "cache_gqa_k", "cache_gqa_v", "cache_diff_k", "cache_diff_v", "c",
        "c_ctx", "ada_w", "ada_b", "norm_mix", "norm_ffn", "w_in", "conv_w", "dn_a_log", "dn_dt_bias", "dn_norm",
        "gqa_q_norm", "gqa_k_norm", "diff_lambda", "diff_norm", "w_out", "ffn_w_gu", "ffn_w_down", "moe_router",
        "moe_w_gu", "moe_w_down", "final_norm"]
_OUTS = {"yp": (1, P, D), "ys": (1, 4 * P, D), "state": (1, DEPTH, 2, HA, HD, HD), "gk": (1, DEPTH, P, KVB, HD),
         "gv": (1, DEPTH, P, KVB, HD), "dk": (1, DEPTH, P, HC, 2, DHC), "dv": (1, DEPTH, P, HC, HD)}


def kernel(**inputs):
    import concourse.bacc as bacc
    from concourse.bass_utils import run_bass_kernel_spmd

    nc = bacc.Bacc("TRN2", target_bir_lowering=False, num_devices=1)
    arrays, ins, outs = {}, {}, {}
    given = {n: np.ascontiguousarray(inputs[n]) for n in _INS}
    given.update(shape_constants())
    for name, a in given.items():
        arrays[f"in_{name}"] = a
        ins[name] = nc.dram_tensor(f"in_{name}", a.shape, mybir.dt.from_np(a.dtype), kind="ExternalInput").ap()
    for name, shape in _OUTS.items():
        outs[name] = nc.dram_tensor(f"out_{name}", shape, F32, kind="ExternalOutput").ap()
    build_program(nc, ins, outs)
    r = run_bass_kernel_spmd(nc, [arrays], core_ids=[0])
    return tuple(r.results[0][f"out_{name}"] for name in _OUTS)
```
